# Optimizing a Trainium2 kernel written in Bass

```python
import math
import jax, jax.numpy as jnp
from jax import lax
import numpy as np

D_MODEL = 1024
BATCH = 1
SEQ = 512
DEPTH = 1
DEC_BATCH = 8
DEC_SEQ = 8
PAST_LEN = 4096
PAGE_SIZE = 128

N_META = 16
D_LRU = 1024
LRU_BLOCKS = 16
LRU_BW = D_LRU // LRU_BLOCKS
LRU_CONV = 4
LRU_C = 8.0
ML_HEADS = 4
D_ML = 1024
ML_DH = D_ML // ML_HEADS
MLSTM_CHUNK = 64
D_FF = 2816
FFN_CONV = 3
N_IN = D_LRU + 4 * D_ML + 2 * ML_HEADS + 2 * D_MODEL
EPS = 1e-6

kernel_name = "hawk_mlstm_parallel_gated_convffn_step"

def rms_norm(x, g):
    xf = x.astype(jnp.float32)
    out = xf * lax.rsqrt(jnp.mean(xf * xf, axis=-1, keepdims=True) + EPS)
    return (out * g.astype(jnp.float32)).astype(x.dtype)

def causal_dwconv(u, buf, w, b):
    L = u.shape[1]
    W = w.shape[0]
    full = jnp.concatenate([buf.astype(u.dtype), u], axis=1)
    out = b + sum(full[:, j:j + L] * w[j] for j in range(W))
    return out, full[:, L:]

def rg_lru(x, h0, w_r, b_r, w_i, b_i, lam):
    B, L, C = x.shape
    xb = x.reshape(B, L, LRU_BLOCKS, LRU_BW)
    r = jax.nn.sigmoid(jnp.einsum('blnc,ncd->blnd', xb, w_r).reshape(B, L, C) + b_r)
    i = jax.nn.sigmoid(jnp.einsum('blnc,ncd->blnd', xb, w_i).reshape(B, L, C) + b_i)
    log_a = -LRU_C * r.astype(jnp.float32) * jax.nn.softplus(-lam.astype(jnp.float32))
    a = jnp.exp(log_a)
    inp = jnp.sqrt(-jnp.expm1(2.0 * log_a)) * (i * x).astype(jnp.float32)

    def step(h, t):
        a_t, u_t = t
        h = a_t * h + u_t
        return h, h

    h_last, hs = lax.scan(step, h0.astype(jnp.float32),
                          (jnp.swapaxes(a, 0, 1), jnp.swapaxes(inp, 0, 1)))
    return jnp.swapaxes(hs, 0, 1).astype(x.dtype), h_last

def mlstm_chunk(carry, inp):
    C, n, m = carry
    q, k, v, ig, lf = inp
    L = q.shape[2]
    b = jnp.cumsum(lf, axis=-1)
    causal = jnp.tril(jnp.ones((L, L), dtype=bool))
    dmat = jnp.where(causal, b[..., :, None] - b[..., None, :] + ig[..., None, :], -jnp.inf)
    inter = b + m[..., None]
    m_t = jnp.maximum(jnp.max(dmat, axis=-1), inter)
    w = jnp.exp(dmat - m_t[..., None])
    s = jnp.einsum('bhtd,bhsd->bhts', q, k) * w
    e_int = jnp.exp(inter - m_t)
    num = jnp.einsum('bhts,bhsv->bhtv', s, v) + e_int[..., None] * jnp.einsum('bhtd,bhdv->bhtv', q, C)
    den = jnp.sum(s, axis=-1) + e_int * jnp.einsum('bhtd,bhd->bht', q, n)
    h = num / jnp.maximum(jnp.abs(den), jnp.exp(-m_t))[..., None]
    bL = b[..., -1]
    g = bL[..., None] - b + ig
    m_new = jnp.maximum(bL + m, jnp.max(g, axis=-1))
    decay = jnp.exp(bL + m - m_new)
    wk = jnp.exp(g - m_new[..., None])
    C_new = decay[..., None, None] * C + jnp.einsum('bhs,bhsd,bhsv->bhdv', wk, k, v)
    n_new = decay[..., None] * n + jnp.einsum('bhs,bhsd->bhd', wk, k)
    return (C_new, n_new, m_new), h

def mlstm_seq(q, k, v, ig, lf, C, n, m, lead):
    B, H, Ltot, _ = q.shape
    carry = (C, n, m)
    outs = []
    if lead > 0:
        carry, h0 = mlstm_chunk(carry, (q[:, :, :lead], k[:, :, :lead], v[:, :, :lead],
                                        ig[:, :, :lead], lf[:, :, :lead]))
        outs.append(h0)
    T = Ltot - lead
    cs = math.gcd(T, MLSTM_CHUNK)
    nc = T // cs

    def to_chunks(a):
        a = a[:, :, lead:]
        a = a.reshape(a.shape[:2] + (nc, cs) + a.shape[3:])
        return jnp.moveaxis(a, 2, 0)

    carry, hs = lax.scan(mlstm_chunk, carry,
                         (to_chunks(q), to_chunks(k), to_chunks(v), to_chunks(ig), to_chunks(lf)))
    hs = jnp.moveaxis(hs, 0, 2).reshape(B, H, T, v.shape[-1])
    outs.append(hs)
    return jnp.concatenate(outs, axis=2), carry

def conv_ffn(xn, buf, w_up, cw, cb, w_down):
    up = xn @ w_up
    upc, new_buf = causal_dwconv(up, buf, cw, cb)
    val, gate = jnp.split(upc, 2, axis=-1)
    return (jax.nn.gelu(gate) * val) @ w_down, new_buf

def block(x, lead, st, lp):
    lru_conv_buf, lru_h, C, n, m, ffn_buf = st
    sdt = lru_h.dtype
    B, L, _ = x.shape
    xn = rms_norm(x, lp['norm1_g'])
    z = xn @ lp['w_in'] + lp['b_in']
    sizes = [D_LRU, D_ML, D_ML, D_ML, D_ML, ML_HEADS, ML_HEADS, D_MODEL]
    u, q, k, v, o, ipre, fpre, ga, gb = jnp.split(z, np.cumsum(sizes).tolist(), axis=-1)
    uc, new_lru_conv = causal_dwconv(u, lru_conv_buf, lp['lru_conv_w'], lp['lru_conv_b'])
    ha, new_lru_h = rg_lru(uc, lru_h, lp['lru_w_r'], lp['lru_b_r'], lp['lru_w_i'], lp['lru_b_i'], lp['lru_lambda'])

    def heads(a):
        return a.reshape(B, L, ML_HEADS, ML_DH).transpose(0, 2, 1, 3).astype(jnp.float32)

    qh = heads(q) * (ML_DH ** -0.5)
    kh = heads(k)
    vh = heads(v)
    ig = ipre.astype(jnp.float32).transpose(0, 2, 1)
    lf = jax.nn.log_sigmoid(fpre.astype(jnp.float32)).transpose(0, 2, 1)
    hb, (Cn, nn_, mn) = mlstm_seq(qh, kh, vh, ig, lf, C.astype(jnp.float32), n.astype(jnp.float32),
                                  m.astype(jnp.float32), lead)
    hb = hb.transpose(0, 2, 1, 3)
    hb = hb * lax.rsqrt(jnp.mean(hb * hb, axis=-1, keepdims=True) + EPS)
    hb = (hb.reshape(B, L, D_ML) * lp['mlstm_head_g'].astype(jnp.float32)).astype(x.dtype) * jax.nn.sigmoid(o)
    merged = jax.nn.sigmoid(ga) * (ha @ lp['w_branch_a']) + jax.nn.sigmoid(gb) * (hb @ lp['w_branch_b'])
    x = x + merged @ lp['w_out']
    f, new_ffn = conv_ffn(rms_norm(x, lp['norm2_g']), ffn_buf, lp['w_up'], lp['ffn_conv_w'],
                          lp['ffn_conv_b'], lp['w_down'])
    x = x + f
    return x, (new_lru_conv.astype(sdt), new_lru_h.astype(sdt), Cn.astype(sdt), nn_.astype(sdt),
               mn.astype(sdt), new_ffn.astype(sdt))

def setup_inputs(seed: int = 0) -> dict:
    key = jax.random.key(seed)
    ks = jax.random.split(key, 32)

    def nrm(k, shape, s):
        return jax.random.normal(k, shape, jnp.float32) * s

    f_off = D_LRU + 4 * D_ML + ML_HEADS
    b_in = nrm(ks[11], (DEPTH, N_IN), 0.01)
    b_in = b_in.at[:, f_off:f_off + ML_HEADS].add(jnp.linspace(3.0, 6.0, ML_HEADS))
    a0 = jax.random.uniform(ks[18], (DEPTH, D_LRU), jnp.float32, minval=0.9, maxval=0.999)
    s0 = a0 ** (1.0 / LRU_C)
    lru_lambda = jnp.log(s0) - jnp.log1p(-s0)
    return {
        "x_prompt": nrm(ks[0], (BATCH, SEQ, D_MODEL), 1.0),
        "x_sample": nrm(ks[1], (DEC_BATCH, DEC_SEQ, D_MODEL), 1.0),
        "state_lru_conv": nrm(ks[2], (DEPTH, DEC_BATCH, LRU_CONV - 1, D_LRU), 1.0),
        "state_lru_h": nrm(ks[3], (DEPTH, DEC_BATCH, D_LRU), 0.5),
        "state_mlstm_C": nrm(ks[4], (DEPTH, DEC_BATCH, ML_HEADS, ML_DH, ML_DH), 0.05),
        "state_mlstm_n": nrm(ks[5], (DEPTH, DEC_BATCH, ML_HEADS, ML_DH), 0.05),
        "state_mlstm_m": nrm(ks[6], (DEPTH, DEC_BATCH, ML_HEADS), 1.0),
        "state_ffn_conv": nrm(ks[7], (DEPTH, DEC_BATCH, FFN_CONV - 1, 2 * D_FF), 1.0),
        "meta_tokens": nrm(ks[8], (N_META, D_MODEL), 1.0),
        "norm1_g": 1.0 + nrm(ks[9], (DEPTH, D_MODEL), 0.02),
        "w_in": nrm(ks[10], (DEPTH, D_MODEL, N_IN), D_MODEL ** -0.5),
        "b_in": b_in,
        "lru_conv_w": nrm(ks[12], (DEPTH, LRU_CONV, D_LRU), LRU_CONV ** -0.5),
        "lru_conv_b": nrm(ks[13], (DEPTH, D_LRU), 0.01),
        "lru_w_r": nrm(ks[14], (DEPTH, LRU_BLOCKS, LRU_BW, LRU_BW), LRU_BW ** -0.5),
        "lru_b_r": nrm(ks[15], (DEPTH, D_LRU), 0.01),
        "lru_w_i": nrm(ks[16], (DEPTH, LRU_BLOCKS, LRU_BW, LRU_BW), LRU_BW ** -0.5),
        "lru_b_i": nrm(ks[17], (DEPTH, D_LRU), 0.01),
        "lru_lambda": lru_lambda,
        "mlstm_head_g": 1.0 + nrm(ks[19], (DEPTH, D_ML), 0.02),
        "w_branch_a": nrm(ks[20], (DEPTH, D_LRU, D_MODEL), D_LRU ** -0.5),
        "w_branch_b": nrm(ks[21], (DEPTH, D_ML, D_MODEL), D_ML ** -0.5),
        "w_out": nrm(ks[22], (DEPTH, D_MODEL, D_MODEL), D_MODEL ** -0.5),
        "norm2_g": 1.0 + nrm(ks[23], (DEPTH, D_MODEL), 0.02),
        "w_up": nrm(ks[24], (DEPTH, D_MODEL, 2 * D_FF), D_MODEL ** -0.5),
        "ffn_conv_w": nrm(ks[25], (DEPTH, FFN_CONV, 2 * D_FF), FFN_CONV ** -0.5),
        "ffn_conv_b": nrm(ks[26], (DEPTH, 2 * D_FF), 0.01),
        "w_down": nrm(ks[27], (DEPTH, D_FF, D_MODEL), D_FF ** -0.5),
        "final_g": 1.0 + nrm(ks[28], (D_MODEL,), 0.02),
    }

def reference(x_prompt, x_sample, state_lru_conv, state_lru_h, state_mlstm_C, state_mlstm_n,
              state_mlstm_m, state_ffn_conv, meta_tokens, norm1_g, w_in, b_in, lru_conv_w, lru_conv_b,
              lru_w_r, lru_b_r, lru_w_i, lru_b_i, lru_lambda, mlstm_head_g, w_branch_a, w_branch_b,
              w_out, norm2_g, w_up, ffn_conv_w, ffn_conv_b, w_down, final_g):
    dt = x_prompt.dtype
    bp = x_prompt.shape[0]
    meta = jnp.broadcast_to(meta_tokens[None].astype(dt), (bp, N_META, D_MODEL))
    xp = jnp.concatenate([meta, x_prompt], axis=1)
    xs = x_sample
    new_p = []
    new_s = []
    for l in range(DEPTH):
        lp = {
            'norm1_g': norm1_g[l], 'w_in': w_in[l], 'b_in': b_in[l],
            'lru_conv_w': lru_conv_w[l], 'lru_conv_b': lru_conv_b[l],
            'lru_w_r': lru_w_r[l], 'lru_b_r': lru_b_r[l], 'lru_w_i': lru_w_i[l], 'lru_b_i': lru_b_i[l],
            'lru_lambda': lru_lambda[l], 'mlstm_head_g': mlstm_head_g[l],
            'w_branch_a': w_branch_a[l], 'w_branch_b': w_branch_b[l], 'w_out': w_out[l],
            'norm2_g': norm2_g[l], 'w_up': w_up[l], 'ffn_conv_w': ffn_conv_w[l],
            'ffn_conv_b': ffn_conv_b[l], 'w_down': w_down[l],
        }
        zero = (jnp.zeros((bp, LRU_CONV - 1, D_LRU), dt), jnp.zeros((bp, D_LRU), dt),
                jnp.zeros((bp, ML_HEADS, ML_DH, ML_DH), dt), jnp.zeros((bp, ML_HEADS, ML_DH), dt),
                jnp.zeros((bp, ML_HEADS), dt), jnp.zeros((bp, FFN_CONV - 1, 2 * D_FF), dt))
        xp, sp = block(xp, N_META, zero, lp)
        xs, ss = block(xs, 0, (state_lru_conv[l], state_lru_h[l], state_mlstm_C[l], state_mlstm_n[l],
                               state_mlstm_m[l], state_ffn_conv[l]), lp)
        new_p.append(sp)
        new_s.append(ss)

    def stk(lst, i):
        return jnp.stack([t[i] for t in lst], axis=0)

    y_prompt = rms_norm(xp[:, N_META:], final_g)
    y_sample = rms_norm(xs, final_g)
    return (y_prompt, y_sample,
            stk(new_p, 0), stk(new_p, 1), stk(new_p, 2), stk(new_p, 3), stk(new_p, 4), stk(new_p, 5),
            stk(new_s, 0), stk(new_s, 1), stk(new_s, 2), stk(new_s, 3), stk(new_s, 4), stk(new_s, 5))


_drawn_inputs = setup_inputs


def setup_inputs(seed=0):
    import zlib

    import numpy as np

    out = dict(_drawn_inputs(seed))
    spreads = {}
    factors = {'state_mlstm_n': 3.005,
     'lru_b_r': 23.396,
     'lru_b_i': 8.0,
     'mlstm_head_g': 8.0,
     'norm2_g': 2.866,
     'ffn_conv_b': 7.805,
     'final_g': 7.474}
    for name, (base, spread) in spreads.items():
        noise = np.random.default_rng([zlib.crc32(name.encode()), seed]).standard_normal(out[name].shape)
        drawn = base * np.exp(spread * noise) if base else spread * noise
        out[name] = __import__('jax').numpy.asarray(drawn.astype(out[name].dtype))
    for name, factor in factors.items():
        out[name] = (out[name] * factor).astype(out[name].dtype)
    return out
```

```python
import numpy as np
import concourse.bass as bass
from concourse import mybir
from contextlib import ExitStack

F32 = mybir.dt.float32
F32R = mybir.dt.float32r
ALU = mybir.AluOpType
ACT = mybir.ActivationFunctionType
ds = bass.ds

D = 1024
P = 128
KT = D // P
SEQ, META = 512, 16
TP = SEQ + META
NB, LS = 8, 8
T = TP + NB * LS
HALF = T // 2
TT = -(-T // P)
LAST = T - (TT - 1) * P
TAIL = LAST - NB * LS
NS = NB + 1
HEADS, DH = 4, 256
LW, FW = 4, 3
FF = 2816
UPT = 2 * FF // P
HK = FF // P // 2
BW = 64
EPS = 1e-6
LRU_C = 8.0
LSE_TERMS = 8
NEG = -1.0e30
COL_I = D + 4 * D
COL_F = COL_I + HEADS
COL_GA = COL_F + HEADS
COL_GB = COL_GA + D

C_N1, C_N2, C_BIN, C_BGA, C_BGB, C_CW, C_CB, C_BR, C_BI = 0, 8, 16, 56, 64, 72, 104, 112, 120
C_LAM, C_HG, C_H0 = 128, 136, 144
C_NS, C_FCB = 256, 320
C_FCW = (384, 384 + UPT, 512)
C_LC = (640, 768)
C_FC = 896
NROW = 15
ROWS = [128, 80, 108, 88, 44, 96, 96] + [88] * 8

B_GATE, B_U, B_GA, B_WA, B_HEAD = 0, 1, 9, 17, 25
B_GB = B_HEAD + 8 * HEADS
B_WB = B_GB + 8
B_OUT = B_WB + 8
B_FFN = B_OUT + 8
B_HALF = 2 * HK + 8
B_END = B_FFN + 2 * B_HALF
T_COLS = 0
T_XN = 4
T_GATE = T_XN + 8
T_U = T_GATE + 1
T_GA = T_U + 8
T_LC = T_GA + 8
T_WA = T_LC + 2
T_HEAD0 = T_WA + 8
T_HEAD = T_HEAD0 + 8
HT = 14
T_NOUT = T_HEAD + HT * HEADS
T_WB = T_NOUT + 1
T_OUT = T_WB + 16
T_FFN = T_OUT + 8
T_FC = T_FFN + 2 * B_HALF
T_FIN = T_FC + 6

TB = 4 * T
SLOT = 4 * HK * P


class Chain:

    def __init__(self, eng, sem):
        self.eng, self.sem, self.base, self.n = eng, sem, 0, 0

    def __call__(self, ins):
        ins.then_inc(self.sem, 1)
        self.n += 1
        return ins

    def wait(self):
        self.eng.wait_ge(self.sem, self.base + self.n)

    def link(self, ins):
        self(ins)
        self.wait()

    def loop(self, first, last, per, body):
        start = self.n
        with self.eng.Fori(first, last) as i:
            self.base = start + per * (i - first)
            self.n = 0
            body(i)
            assert self.n == per, (self.n, per)
        self.base, self.n = 0, start + per * (last - first)


def flat(ap):
    return ap.rearrange("p o t -> p (o t)")


def hybrid_layer(nc, a, o):
    w_in, b_in = a["w_in"][0], a["b_in"][0]
    ctx = ExitStack()
    with ctx:
        base = 16512

        def sb(name, shape, off, dt=F32):
            return nc.alloc_sbuf_tensor_at(name, shape, dt, offset=base + off)

        def sem(name):
            return ctx.enter_context(nc.semaphore(name))

        o_a = 6 * SLOT
        o_c = o_a + 16 * TB
        o_b = o_c + 8 * TB
        o_h = o_b + 8 * TB
        o_p = o_h + 85568
        stage = sb("stage", [P, 2, HK * P], 0)
        whi = sb("whi", [P, 2, HK * P], 2 * SLOT, F32R)
        wlo = sb("wlo", [P, 2, HK * P], 4 * SLOT, F32R)
        ulast = stage[:, 0, D:D + 8 * 27].rearrange("p (f n) -> p f n", n=27)
        hlast = stage[:, 0, D + 224:D + 224 + 72].rearrange("p (b f) -> p b f", f=8)
        usamp = stage[:, 1, D:D + 176].rearrange("p (s b l) -> p s b l", s=2, l=LW - 1 + LS)
        xh = sb("xh", [P, 8, T], o_a, F32R)
        xl = sb("xl", [P, 8, T], o_a + 8 * TB, F32R)
        merged = sb("merged", [P, 8, T], o_c)
        hb = sb("hb", [P, 8, T], o_b)
        gs = sb("gate_scratch", [HEADS, 6, T], o_b)
        th = sb("lru_tanh", [P, 2, T], o_b + 6 * TB)
        sq_tok = sb("sq_tok", [P, D], o_b)
        conv_out = sb("conv_out", [27, D], o_b)
        h_out = sb("h_out", [72, P], o_b + 4096)
        resid = sb("resid", [P, 8, T], o_b)
        x_tok = sb("x_tok", [P, TT, D], o_h)
        rows = sb("rows", [P, NROW, P], o_h + 20480)
        UW = LW - 1 + T
        u = sb("u", [P, 8, UW], o_h)
        uc = sb("uc", [P, 8, T], o_h + 32 * UW)
        hh = sb("hh", [P, 8, T], o_h + 32 * UW + 8 * TB, F32R)
        hl = sb("hl", [P, 8, T], o_h + 32 * UW + 16 * TB, F32R)
        ri = sb("ri", [P, 2, 2, T], o_h + 32 * UW + 24 * TB)
        SB = 6 * TB + 10240

        def head_slot(name, shape, off):
            return [sb(f"{name}{s}", shape, o_h + SB * s + off) for s in range(2)]

        q = head_slot("q", [P, 2, T], 0)
        k = head_slot("k", [P, 2, T], 2 * TB)
        so = head_slot("sig_o", [P, 2, T], 4 * TB)
        kt = head_slot("k_tok", [P, TT, DH], 6 * TB)
        vt = head_slot("v_tok", [P, TT, DH], 6 * TB + 5120)
        r = o_h + 2 * SB
        vf = sb("v_feat", [P, 2, T], r)
        qe = sb("q_e", [P, 2, T], r + 2 * TB)
        cs = sb("c_sample", [P, 4, 2, DH], r + 4 * TB)
        r += 4 * TB + 8192
        cp0 = sb("c_prompt0", [P, 2, DH], r)
        ebc = sb("e_int", [P, T], r + 2048)
        gbc = sb("guard", [P, T], r + 2048 + TB)
        den = sb("den", [P, T], r + 2048 + 2 * TB)
        hsq = sb("h_sq", [P, 2, T], r + 2048 + 3 * TB)
        r += 2048 + 5 * TB
        argm = sb("arg", [P, P], r)
        wt = sb("w_t", [P, 2, P], r + 512)
        pt = sb("p_t", [P, P], r + 1536)
        kw = sb("k_w", [P, 2, DH], r + 2048)
        ntmp = sb("n_tmp", [P, NS, 2], r + 4096)
        n_rows = sb("n_rows", [72, P], r + 4096 + 96)
        gbs = sb("sig_gb", [P, 8, T], o_h)
        mh = sb("mh", [P, 8, T], o_h + SB, F32R)
        ml = sb("ml", [P, 8, T], o_h + SB + 8 * TB, F32R)
        x_tok2 = sb("x_tok2", [P, TT, D], o_h + SB + 16 * TB)
        xsq = sb("x_sq", [P, 2, T], o_c)
        rbc = sb("rstd", [P, T], o_c + 2 * TB)
        fout = sb("f_out", [18, 2, D], o_c + 3 * TB)
        gh = sb("gh", [P, HK, T], o_h, F32R)
        gl = sb("gl", [P, HK, T], o_h + HK * TB, F32R)
        r = o_h + 2 * HK * TB
        FP = FW - 1 + T
        up = sb("up", [P, 2, FP], r)
        cv = sb("conv", [P, 2, T], r + 4768)
        r += 4768 + 2 * TB
        fsamp = sb("f_samp", [P, 2, NB, FW - 1 + LS], r)
        flast = sb("f_last", [P, UPT, 18], r + 640)
        fgb = sb("final_g_b", [P, D], r + 640 + 72 * UPT)
        y = sb("y", [P, 2, D], o_h)
        fsq = sb("fin_sq", [P, D], o_h + 8192)
        cols = sb("cols", [P, NROW * P], o_p)
        r = o_p + 512 * NROW
        ident = sb("ident", [P, P], r)
        ones = sb("ones", [P, P], r + 512)
        mask = sb("mask", [P, 2, P], r + 1024)
        sel = sb("sel", [P, HEADS, P], r + 2048)
        gq = sb("gate_rows", [P, T], r + 4096)
        r += 4096 + TB
        nst = sb("n_state", [P, NS, 8], r)
        misc = sb("misc", [P, 256], r + 288)
        bd = sb("lru_gate_w", [P, 2, 2, P], r + 1312)
        cp = [cp0, sb("c_prompt1", [P, 2, DH], r + 1312)]
        ss, rms, eps, one = misc[:, 0:5], misc[:, 8:13], misc[:, 16:17], misc[:, 17:18]
        qb, negc = misc[:, 24:32], misc[:, 32:40]
        lam = [misc[:, 40 + 8 * n:48 + 8 * n] for n in range(6)]
        ssf, rmsf = misc[:, 96:101], misc[:, 104:109]
        gbias = misc[0:HEADS, 112:114]
        mst = misc[0:HEADS, 120:128]
        mout = misc[0:HEADS, 128:137]

        ring = ctx.enter_context(nc.psum_tensor("ring", [P, 2, 2, 512], F32))
        bank = ctx.enter_context(nc.psum_tensor("bank", [P, 4, 512], F32))
        wide = [ring[:, s].rearrange("p h t -> p (h t)") for s in range(2)]
        bx = [bank[:, 0], bank[:, 1]]
        by = bank[:, 2]
        bz = bank[:, 3]

        def rt(s, rows_=slice(0, P)):
            return ring[rows_, s, :, 0:HALF]

        def h2(ap):
            return ap.rearrange("p (h t) -> p h t", h=2)

        def h2o(ap):
            return ap.rearrange("p o (h t) -> p (o h) t", h=2)

        w_loaded = [sem("w_loaded0"), sem("w_loaded1")]
        w_hi, w_lo = sem("w_hi"), sem("w_lo")
        tile_done, tile_evicted = sem("tile_done"), sem("tile_evicted")
        x_in = [sem(f"x_in{i}") for i in range(3)]
        rows_in, gate_rows_in, x2_in = sem("rows_in"), sem("gate_in"), sem("x2_in")
        const_done, gate_zero, sq_done, x_scaled, xn_hi = (
            sem("const_done"), sem("gate_zero"), sem("sq_done"), sem("x_scaled"), sem("xn_hi"))
        rms_done = sem("rms_done")
        gate_raw, gate_abs, gate_exp, gates_ready = (
            sem("gate_raw"), sem("gate_abs"), sem("gate_exp"), sem("gates_ready"))
        bd_in = [sem("bd_in0"), sem("bd_in1")]
        bd_zero, conv_done, lru_ps, lru_act, lru_q, lru_sq, lru_h, lru_hi, lru_lo = (
            sem("bd_zero"), sem("conv_done"), sem("lru_ps"), sem("lru_act"), sem("lru_q"),
            sem("lru_sq"), sem("lru_h"), sem("lru_hi"), sem("lru_lo"))
        c_in = [sem(f"c_in{n}") for n in range(4)]
        c_out = [sem(f"c_out{n}") for n in range(4)]
        cp_out = sem("cp_out")
        arg_part = sem("arg_part")
        scores, arg_done, w_done, p_done = sem("scores"), sem("arg_done"), sem("w_done"), sem("p_done")
        qe_done, kw_done, y_done, y_evicted, z_done, z_evicted = (
            sem("qe_done"), sem("kw_done"), sem("y_done"), sem("y_evicted"), sem("z_done"),
            sem("z_evicted"))
        hn_done, hsq_done, hrms_done, head_done = (
            sem("hn_done"), sem("hsq_done"), sem("hrms_done"), sem("head_done"))
        hb_hi, hb_lo, m_done, m_hi, m_lo = (
            sem("hb_hi"), sem("hb_lo"), sem("m_done"), sem("m_hi"), sem("m_lo"))
        xsq_done, ssum_part, x2_hi, x2_lo, frms, rbc_done = (
            sem("xsq_done"), sem("ssum_part"), sem("x2_hi"), sem("x2_lo"),
            sem("frms"), sem("rbc_done"))
        gate_conv, gelu_done, prod_done, g_hi, g_lo = (
            sem("gate_conv"), sem("gelu_done"), sem("prod_done"), sem("g_hi"), sem("g_lo"))
        fin_rms = sem("fin_rms")
        fg_in = sem("fg_in")
        y_out = [sem("y_out0"), sem("y_out1")]
        lru_out, n_out, m_out, f_out = sem("lru_out"), sem("n_out"), sem("m_out"), [sem("f_out0"), sem("f_out1")]
        act_step, dve_step, pool_step = sem("act_step"), sem("dve_step"), sem("pool_step")

        def half_lo(h):
            return HK * h

        block = ctx.enter_context(nc.Block())

        @block.sync
        def _(sp):
            def kview(w, kt_):
                return w.rearrange("(k p) m -> p k m", p=P)

            def load(b, slot, src, c0, k0=0, kn=KT):
                sp.dma_start(stage[:, slot, 0:kn * P].rearrange("p (k m) -> p k m", m=P),
                             src.rearrange("(k p) m -> p k m", p=P)[:, k0:k0 + kn, c0]
                             ).then_inc(w_loaded[slot], 16)

            def stream(b0, src, c0):
                def pair(i):
                    for j in range(2):
                        b = b0 + 2 * i + j
                        sp.wait_ge(w_lo, b - 1)
                        load(b, (b0 + j) % 2, src, ds(c0 + 256 * i + 128 * j, P))
                with sp.Fori(0, 4) as i:
                    pair(i)

            xp, xs, meta = a["x_prompt"][0], a["x_sample"].rearrange("b l d -> (b l) d"), a["meta_tokens"]

            def load_x(dst, sems):
                sp.dma_start(dst[0:META, 0], meta).then_inc(sems[0], 16)
                sp.dma_start(dst[META:P, 0], xp[0:P - META]).then_inc(sems[0], 16)
                sp.dma_start(dst[:, 1:TT - 1], xp[P - META:P - META + 3 * P].rearrange("(i p) d -> p i d", p=P)
                             ).then_inc(sems[1], 16)
                sp.dma_start(dst[0:TAIL, TT - 1], xp[SEQ - TAIL:SEQ]).then_inc(sems[2], 16)
                sp.dma_start(dst[TAIL:LAST, TT - 1], xs).then_inc(sems[2], 16)

            load_x(x_tok, x_in)
            sp.wait_ge(gate_zero, 1)
            g0 = stage[:, 0, 0:D].rearrange("p (k m) -> p k m", m=P)
            for c0, at in ((COL_I, 0), (COL_F, 32)):
                sp.dma_start(g0[:, :, at:at + HEADS],
                             w_in.rearrange("(k p) m -> p k m", p=P)[:, :, c0:c0 + HEADS]
                             ).then_inc(w_loaded[0], 16)
            load(1, 1, w_in, slice(0, P))
            sp.wait_ge(w_lo, 1)
            load(2, 0, w_in, slice(P, 2 * P))
            with sp.Fori(1, 4) as i:
                for j in range(2):
                    b = B_U + 2 * i + j
                    sp.wait_ge(w_lo, b - 1)
                    load(b, (B_U + j) % 2, w_in, ds(256 * i + 128 * j, P))
            sp.wait_ge(bd_zero, 1)

            def ga_load(i):
                for j in range(2):
                    b = B_GA + 2 * i + j
                    sp.wait_ge(w_lo, b - 1)
                    load(b, (B_GA + j) % 2, w_in, ds(COL_GA + 256 * i + 128 * j, P))
                    if not isinstance(i, int):
                        sp.wait_ge(lru_ps, 2 * i)
                    for g, w in enumerate((a["lru_w_r"][0], a["lru_w_i"][0])):
                        for hf in range(2):
                            sp.dma_start(bd[BW * hf:BW * hf + BW, j, g, BW * hf:BW * hf + BW],
                                         w[ds(4 * i + 2 * j + hf, 1)].rearrange("o c d -> (o c) d")
                                         ).then_inc(bd_in[j], 16)
            ga_load(0)
            with sp.Fori(1, 4) as i:
                ga_load(i)
            stream(B_WA, a["w_branch_a"][0], 0)
            sp.wait_ge(tile_evicted, T_LC + 2)
            sp.dma_start(o["p_lru_conv"][0, 0], conv_out[0:3, :]).then_inc(lru_out, 16)
            sp.dma_start(o["s_lru_conv"][0].rearrange("b j c -> (b j) c"), conv_out[3:27, :]).then_inc(lru_out, 16)
            sp.dma_start(o["p_lru_h"].rearrange("l b (f c) -> (l b f) c", c=P), h_out[0:8, :]).then_inc(lru_out, 16)
            sp.dma_start(o["s_lru_h"].rearrange("l b (f c) -> (l b f) c", c=P), h_out[8:72, :]).then_inc(lru_out, 16)

            def head_load(n):
                b = B_HEAD + n
                if n < 8 * HEADS:
                    h, part, j = n // 8, n % 8 // 2, n % 2
                    c0 = D * (1 + part) + DH * h + P * j
                else:
                    c0 = COL_GB + P * (n - 8 * HEADS)
                sp.wait_ge(w_lo, b - 1)
                load(b, b % 2, w_in, slice(c0, c0 + P))

            def c_load(n):
                if n >= 4:
                    sp.wait_ge(c_out[n % 4], 16 * (n // 4))
                sp.dma_start(cs[:, n % 4], a["state_mlstm_C"][0, n % NB, n // NB].rearrange("(i p) v -> p i v", p=P)
                             ).then_inc(c_in[n % 4], 16)

            def c_store(n):
                sp.wait_ge(z_evicted, 13 * (n // NB) + 5 + n % NB + 1)
                sp.dma_start(o["s_mlstm_C"][0, n % NB, n // NB].rearrange("(i p) v -> p i v", p=P), cs[:, n % 4]
                             ).then_inc(c_out[n % 4], 16)

            for n in range(8):
                head_load(n)
            sp.wait_ge(gates_ready, 1)
            sp.dma_start(o["p_mlstm_m"][0].rearrange("b h -> h b"), mout[:, 0:1]).then_inc(m_out, 16)
            with nc.allow_non_contiguous_dma(reason="32 single values"):
                sp.dma_start(o["s_mlstm_m"][0].rearrange("b h -> h b"), mout[:, 1:NS]).then_inc(m_out, 16)
            sp.wait_ge(tile_done, T_WA + 8)
            for n in range(4):
                c_load(n)
            for h in range(HEADS):
                for n in range(6):
                    head_load(8 * (h + 1) + n)
                for n in range(4):
                    c_store(NB * h + n)
                    c_load(NB * h + 4 + n)
                head_load(8 * (h + 1) + 6)
                head_load(8 * (h + 1) + 7)
                sp.wait_ge(z_evicted, 13 * h + 5)
                sp.dma_start(o["p_mlstm_C"][0, 0, h].rearrange("(i p) v -> p i v", p=P), cp[h % 2][:, :, :]
                             ).then_inc(cp_out, 16)
                for n in range(4, 8):
                    c_store(NB * h + n)
                    if h + 1 < HEADS:
                        c_load(NB * h + 4 + n)
            wb = a["w_branch_b"][0]
            for j in range(2):
                sp.wait_ge(w_lo, B_WB + j - 1)
                load(B_WB + j, (B_WB + j) % 2, wb, slice(P * j, P * j + P))
            sp.wait_ge(head_done, HEADS)
            sp.wait_ge(cp_out, 16 * HEADS)
            for n in range(4):
                sp.wait_ge(c_out[n], 16 * 8)
            sp.wait_ge(tile_evicted, T_NOUT + 1)
            load_x(x_tok2, [x2_in] * 3)
            sp.dma_start(o["p_mlstm_n"].rearrange("l b h (i p) -> (l b h i) p", p=P), n_rows[0:8, :]).then_inc(n_out, 16)
            sp.dma_start(o["s_mlstm_n"].rearrange("l b h (i p) -> (l b h i) p", p=P), n_rows[8:72, :]).then_inc(n_out, 16)
            with sp.Fori(1, 4) as i:
                for j in range(2):
                    b = B_WB + 2 * i + j
                    sp.wait_ge(w_lo, b - 1)
                    load(b, (B_WB + j) % 2, wb, ds(256 * i + 128 * j, P))
            stream(B_OUT, a["w_out"][0], 0)
            for h in range(2):
                b0 = B_FFN + B_HALF * h
                with sp.Fori(0, HK) as i:
                    for j in range(2):
                        b = b0 + 2 * i + j
                        sp.wait_ge(w_lo, b - 1)
                        load(b, (b0 + j) % 2, a["w_up"][0], ds(FF * j + P * (HK * h) + P * i, P))
                if h == 0:
                    sp.wait_ge(tile_evicted, T_OUT + 8)
                    sp.dma_start(fgb[:, :], a["final_g"].rearrange("(o d) -> o d", o=1).to_broadcast([P, D])
                                 ).then_inc(fg_in, 16)
                b1 = b0 + 2 * HK
                with sp.Fori(0, 4) as i:
                    for j in range(2):
                        b = b1 + 2 * i + j
                        sp.wait_ge(w_lo, b - 1)
                        load(b, (b1 + j) % 2, a["w_down"][0], ds(256 * i + 128 * j, P), HK * h, HK)
            for n in range(6):
                sp.wait_ge(tile_evicted, T_FC + n + 1)
                w_ = min(D, 2 * FF - D * n)
                sp.dma_start(o["p_ffn_conv"][0, 0, :, D * n:D * n + w_], fout[0:2, n % 2, 0:w_]).then_inc(f_out[n % 2], 16)
                sp.dma_start(o["s_ffn_conv"][0].rearrange("b j c -> (b j) c")[:, D * n:D * n + w_],
                             fout[2:18, n % 2, 0:w_]).then_inc(f_out[n % 2], 16)
            yp, ys = o["y_prompt"][0], o["y_sample"].rearrange("b l d -> (b l) d")
            for i in range(TT):
                sp.wait_ge(tile_evicted, T_FIN + i + 1)
                s = y_out[i % 2]
                if i == 0:
                    sp.dma_start(yp[0:P - META], y[META:P, 0]).then_inc(s, 16)
                elif i < TT - 1:
                    sp.dma_start(yp[P * i - META:P * i - META + P], y[:, i % 2]).then_inc(s, 16)
                else:
                    sp.dma_start(yp[SEQ - TAIL:SEQ], y[0:TAIL, i % 2]).then_inc(s, 16)
                    sp.dma_start(ys, y[TAIL:LAST, i % 2]).then_inc(s, 16)
            for s, n in ((lru_out, 4), (m_out, 2), (cp_out, 4), (n_out, 2), (f_out[0], 6), (f_out[1], 6),
                         (y_out[0], 4), (y_out[1], 2)):
                sp.wait_ge(s, 16 * n)

        @block.gpsimd
        def _(pool):
            st = Chain(pool, pool_step)
            pool.memset(stage[:, 0, 0:D], 0.0).then_inc(gate_zero, 1)
            st.link(pool.memset(ident[:, :], 0.0))
            st.link(pool.memset(sel[:, :, :], 0.0))
            st.link(pool.memset(mask[:, :, :], 0.0))
            st.link(pool.memset(misc[:, :], 1.0))
            st.wait()
            st.link(pool.memset(eps, EPS))
            pool.memset(ones[:, :], 1.0).then_inc(const_done, 1)
            pool.wait_ge(const_done, 1)
            st.link(pool.affine_select(out=ident[:, :], in_=ident[:, :], compare_op=ALU.not_equal, fill=1.0, base=0,
                                  pattern=[[-1, P]], channel_multiplier=1))
            for g in range(4):
                rr = slice(32 * g, 32 * g + HEADS)
                st.link(pool.affine_select(out=sel[rr, :, :], in_=sel[rr, :, :], compare_op=ALU.not_equal, fill=1.0,
                                      base=0, pattern=[[-1, HEADS], [0, P]], channel_multiplier=1))
            st.link(pool.affine_select(out=mask[:, :, :], in_=mask[:, :, :], compare_op=ALU.is_ge, fill=NEG, base=0,
                                  pattern=[[0, 2], [1, P]], channel_multiplier=-1))
            st.wait()
            for b in range(NB):
                c0 = TAIL + LS * b
                m = mask[:, 1, c0:c0 + LS]
                st.link(pool.affine_select(out=m, in_=m, compare_op=ALU.is_ge, fill=NEG, base=-c0,
                                      pattern=[[0, LS]], channel_multiplier=1))
            st.wait()
            pool.memset(bd[:, :, :, :], 0.0).then_inc(bd_zero, 1)
            pool.wait_ge(bd_zero, 1)
            st.wait()
            pool.memset(misc[:, 200:201], 0.0).then_inc(const_done, 1)

            def lo(b, slot, n):
                pool.wait_ge(w_hi, b + 1)
                pool.tensor_tensor(wlo[:, slot, 0:n], stage[:, slot, 0:n], whi[:, slot, 0:n].bitcast(F32),
                                   ALU.subtract).then_inc(w_lo, 1)

            def los(b0, n, size):
                with pool.Fori(0, n // 2) as i:
                    for j in range(2):
                        lo(b0 + 2 * i + j, (b0 + j) % 2, size)

            lo(0, 0, D)
            los(1, B_FFN - 1, D)
            for h in range(2):
                b0 = B_FFN + B_HALF * h
                los(b0, 2 * HK, D)
                los(b0 + 2 * HK, 8, HK * P)

        @block.scalar
        def _(act):
            st = Chain(act, act_step)

            def aview(ap):
                return ap.rearrange("(r c) -> r c", c=P)

            for rtile, r0, src in (
                    (0, 0, aview(a["norm1_g"][0])), (0, 8, aview(a["norm2_g"][0])),
                    (0, 16, aview(b_in[0:5 * D])), (0, 56, aview(b_in[COL_GA:COL_GA + 2 * D])),
                    (0, 72, a["lru_conv_w"][0].rearrange("j (f c) -> (j f) c", c=P)),
                    (0, 104, aview(a["lru_conv_b"][0])), (0, 112, aview(a["lru_b_r"][0])),
                    (0, 120, aview(a["lru_b_i"][0])), (1, 0, aview(a["lru_lambda"][0])),
                    (1, 8, aview(a["mlstm_head_g"][0])),
                    (1, 16, a["state_lru_h"][0].rearrange("b (f c) -> (b f) c", c=P)),
                    (2, 0, a["state_mlstm_n"][0].rearrange("b h (i c) -> (b h i) c", c=P)),
                    (2, 64, aview(a["ffn_conv_b"][0])),
                    (3, 0, a["ffn_conv_w"][0, 0:2].rearrange("j (f c) -> (j f) c", c=P)),
                    (4, 0, aview(a["ffn_conv_w"][0, 2])),
                    (5, 0, a["state_lru_conv"][0, 0:4].rearrange("b j (f c) -> (b j f) c", c=P)),
                    (6, 0, a["state_lru_conv"][0, 4:8].rearrange("b j (f c) -> (b j f) c", c=P)),
                    *((7 + b, 0, a["state_ffn_conv"][0, b].rearrange("j (f c) -> (j f) c", c=P)) for b in range(NB))):
                act.dma_start(rows[r0:r0 + src.shape[0], rtile], src).then_inc(rows_in, 16)
            act.wait_ge(const_done, 2)
            act.dma_start(gbias[:, 0:1], b_in[COL_I:COL_F].rearrange("(h o) -> h o", o=1)).then_inc(gate_rows_in, 16)
            act.dma_start(gbias[:, 1:2], b_in[COL_F:COL_GA].rearrange("(h o) -> h o", o=1)).then_inc(gate_rows_in, 16)
            with nc.allow_non_contiguous_dma(reason="32 single values"):
                act.dma_start(mst, a["state_mlstm_m"][0].rearrange("b h -> h b")).then_inc(gate_rows_in, 16)

            def hi(b, slot, n, t, loaded):
                act.wait_ge(w_loaded[slot], loaded)
                if t is not None:
                    act.wait_ge(tile_done, t)
                act.activation(whi[:, slot, 0:n], stage[:, slot, 0:n], ACT.Copy).then_inc(w_hi, 1)

            def loads_of(b):
                return 16 * (b // 2 + 1) + 16 * (1 - b % 2)

            def past():
                act.wait_ge(const_done, 1)

            def evict(t, out, in_, func, **kw_):
                act.wait_ge(tile_evicted, t)
                act.wait_ge(tile_done, t + 1)
                if not isinstance(t, int):
                    past()
                act.activation(out, in_, func, **kw_).then_inc(tile_evicted, 1)

            act.wait_ge(const_done, 1)
            for i in range(TT):
                n = P if i < TT - 1 else LAST
                if i != 2 and i != 3:
                    act.wait_ge(x_in[min(i, 1) if i < 4 else 2], 32 if i in (0, 4) else 16)
                if i:
                    st.wait()
                st(act.activation(sq_tok[0:n, :], x_tok[0:n, i], ACT.Square, accum_out=ss[0:n, i:i + 1]))
                st.wait()
                act.activation(rms[0:n, i:i + 1], ss[0:n, i:i + 1], ACT.Sqrt, scale=1.0 / D,
                               bias=eps[0:n]).then_inc(rms_done, 1)
            for g in range(4):
                act.wait_ge(tile_done, T_COLS + g + 1)
                ms = range(4 * g, min(4 * g + 4, NROW))
                for m in ms:
                    ins = act.activation(cols[:, P * m:P * m + ROWS[m]],
                                         wide[g % 2][:, P * (m % 4):P * (m % 4) + ROWS[m]], ACT.Copy)
                    if m < ms[-1]:
                        st(ins)
                    else:
                        ins.then_inc(tile_evicted, 1)
            hi(0, 0, D, None, 32)
            for f in range(8):
                t = T_XN + f
                act.wait_ge(tile_done, t + 1)
                act.activation(xh[:, f], wide[t % 2][:, 0:T], ACT.Copy, scale=cols[:, C_N1 + f:C_N1 + f + 1]
                               ).then_inc(xn_hi, 1)
            hi(1, 1, D, None, 16)
            t = T_GATE
            act.wait_ge(gate_rows_in, 48)
            act.wait_ge(tile_done, t + 1)
            st(act.activation(h2(gs[:, 0, :]), rt(t % 2, slice(0, HEADS)), ACT.Identity, bias=gbias[:, 0:1]))
            act.wait_ge(tile_evicted, t)
            act.activation(h2(gs[:, 1, :]), rt(t % 2, slice(32, 32 + HEADS)), ACT.Copy).then_inc(tile_evicted, 1)

            act.wait_ge(gate_abs, 1)
            act.activation(gs[:, 2, :], gs[:, 2, :], ACT.Exp, scale=-1.0).then_inc(gate_exp, 1)
            act.wait_ge(gate_abs, 2)
            act.activation(lam[0], lam[0], ACT.Exp, scale=-1.0).then_inc(gate_exp, 1)

            def u_pair(i):
                for j in range(2):
                    b, t = B_U + 2 * i + j, T_U + 2 * i + j
                    s = (B_U + j + 1) % 2
                    hi(b + 1, s, D, t, 16 * i + loads_of(B_U + j + 1))
                    evict(t, h2o(u[:, ds(2 * i + j, 1), LW - 1:UW]), rt((T_U + j) % 2), ACT.Identity,
                          bias=cols[:, ds(2 * i + (C_BIN + j), 1)])
            with act.Fori(0, 4) as i:
                u_pair(i)

            def ga_pair(i):
                for j in range(2):
                    b, t = B_GA + 2 * i + j, T_GA + 2 * i + j
                    f = 2 * i + j
                    s = (B_GA + j + 1) % 2
                    hi(b + 1, s, D, t, 16 * i + loads_of(B_GA + j + 1))
                    evict(t, h2o(merged[:, ds(f, 1), :]), rt((T_GA + j) % 2), ACT.Sigmoid,
                          bias=cols[:, ds(f + C_BGA, 1)])
                    act.wait_ge(lru_ps, f + 1)
                    past()
                    st(act.activation(h2(ri[:, j, 0]), bank[:, 0:2, 0:HALF], ACT.Sigmoid,
                                      bias=cols[:, ds(f + C_BR, 1)]))
                    act.activation(h2(ri[:, j, 1]), bank[:, 2:4, 0:HALF], ACT.Sigmoid,
                                   bias=cols[:, ds(f + C_BI, 1)]).then_inc(lru_act, 1)
                    st.wait()
                    past()
                    st(act.activation(th[:, j], ri[:, j, 0], ACT.Tanh, scale=negc_at(f)))
                    act.activation(flat(u[:, ds(f, 1), 0:T]), ri[:, j, 0], ACT.Exp, scale=negc_at(f)
                                   ).then_inc(lru_act, 1)
                    act.wait_ge(lru_q, f + 1)
                    act.activation(th[:, j], th[:, j], ACT.Sqrt, scale=-1.0).then_inc(lru_sq, 1)
                    act.wait_ge(lru_h, f + 1)
                    past()
                    act.activation(flat(hh[:, ds(f, 1), :]), flat(uc[:, ds(f, 1), :]), ACT.Copy).then_inc(lru_hi, 1)

            def negc_at(f):
                return negc[:, ds(f, 1)]

            act.wait_ge(gates_ready, 1)
            st.loop(0, 4, 4, ga_pair)
            evict(T_LC, conv_out[:, :], wide[T_LC % 2][0:27, :], ACT.Copy)
            evict(T_LC + 1, h_out[:, :], wide[(T_LC + 1) % 2][0:72, 0:P], ACT.Copy)
            with act.Fori(0, 4) as i:
                for j in range(2):
                    b, t = B_WA + 2 * i + j, T_WA + 2 * i + j
                    hi(b + 1, (B_WA + j + 1) % 2, D, t, 16 * i + loads_of(B_WA + j + 1))

            def project(n, t):
                b = B_HEAD + n
                hi(b + 1, (b + 1) % 2, D, t, loads_of(b + 1))
                h, part, j = n // 8, n % 8 // 2, n % 2
                s = h % 2
                if n >= 8 * HEADS:
                    jj = n - 8 * HEADS
                    evict(t, h2(gbs[:, jj]), rt(t % 2), ACT.Sigmoid, bias=cols[:, C_BGB + jj:C_BGB + jj + 1])
                    return
                dst = (q[s], k[s], vf, so[s])[part]
                bias = cols[:, C_BIN + 8 * (part + 1) + 2 * h + j:][:, 0:1]
                if n % 8 == 0 and h >= 2:
                    act.wait_ge(head_done, h - 1)
                if part == 0:
                    evict(t, h2(dst[:, j]), rt(t % 2), ACT.Identity, scale=1.0 / 16, bias=qb[:, 2 * h + j:2 * h + j + 1])
                else:
                    evict(t, h2(dst[:, j]), rt(t % 2), ACT.Sigmoid if part == 3 else ACT.Identity, bias=bias)

            for n in range(8):
                project(n, T_HEAD0 + n)
            for h in range(HEADS):
                s, t0 = h % 2, T_HEAD + HT * h
                if h:
                    act.wait_ge(head_done, h)
                evict(t0, h2(ebc[:, :]), rt(t0 % 2), ACT.Exp)
                evict(t0 + 1, h2(gbc[:, :]), rt((t0 + 1) % 2), ACT.Exp, scale=-1.0)
                for m in range(3):
                    t = t0 + 2 + m
                    w2 = wide[t % 2].rearrange("p (c w d) -> p c w d", w=2, d=DH)
                    act.wait_ge(tile_done, t + 1)
                    if m < 2:
                        st(act.activation(kt[s][:, 2 * m:2 * m + 2], w2[:, :, 0], ACT.Copy))
                        act.wait_ge(tile_evicted, t)
                        act.activation(vt[s][:, 2 * m:2 * m + 2], w2[:, :, 1], ACT.Copy).then_inc(tile_evicted, 1)
                    else:
                        st(act.activation(kt[s][0:LAST, 4], w2[0:LAST, 0, 0], ACT.Copy))
                        act.wait_ge(tile_evicted, t)
                        act.activation(vt[s][0:LAST, 4], w2[0:LAST, 0, 1], ACT.Copy).then_inc(tile_evicted, 1)
                for c in range(TT):
                    n, L = 5 * h + c, P if c < 4 else LAST
                    act.wait_ge(arg_done, n + 1)
                    if n >= 2:
                        act.wait_ge(y_done, n - 1)
                        act.wait_ge(kw_done, 13 * ((n - 2) // 5) + (13 if (n - 2) % 5 == 4 else (n - 2) % 5 + 1))
                    act.activation(wt[0:L, n % 2, 0:L], argm[0:L, 0:L], ACT.Exp).then_inc(w_done, 1)
                    project(8 * (h + 1) + c, t0 + 5 + c)
                project(8 * (h + 1) + 5, t0 + 10)
                act.wait_ge(hn_done, h + 1)
                act.activation(hsq[:, :, :], hb[:, 2 * h:2 * h + 2, :], ACT.Square).then_inc(hsq_done, 1)
                for m in (6, 7):
                    project(8 * (h + 1) + m, t0 + 5 + m)
                act.wait_ge(hsq_done, h + 1)
                evict(t0 + 13, h2(hsq[:, 0]), rt((t0 + 13) % 2), ACT.Sqrt, scale=1.0 / DH, bias=eps)
            evict(T_NOUT, n_rows[:, :], wide[T_NOUT % 2][0:72, 0:P], ACT.Copy)
            act.wait_ge(head_done, HEADS)
            for f in range(8):
                act.activation(xh[:, f], hb[:, f], ACT.Copy).then_inc(hb_hi, 1)

            def wb_pair(i):
                for j in range(2):
                    b, t, f = B_WB + 2 * i + j, T_WB + 4 * i + 2 * j, 2 * i + j
                    hi(b + 1, (B_WB + j + 1) % 2, D, t, 16 * i + loads_of(B_WB + j + 1))
                    act.wait_ge(m_done, f + 1)
                    past()
                    act.activation(flat(mh[:, ds(f, 1), :]), flat(merged[:, ds(f, 1), :]), ACT.Copy).then_inc(m_hi, 1)
                    evict(t + 1, flat(resid[:, ds(f, 1), :]), wide[(T_WB + 1) % 2][:, 0:T], ACT.Copy)
            with act.Fori(0, 4) as i:
                wb_pair(i)

            act.wait_ge(m_lo, 8)

            def out_pair(i):
                for j in range(2):
                    b, t, f = B_OUT + 2 * i + j, T_OUT + 2 * i + j, 2 * i + j
                    hi(b + 1, (B_OUT + j + 1) % 2, D, t, 16 * i + loads_of(B_OUT + j + 1))
                    act.wait_ge(tile_evicted, t + 1)
                    past()
                    act.activation(flat(xh[:, ds(f, 1), :]), flat(resid[:, ds(f, 1), :]), ACT.Copy,
                                   scale=cols[:, ds(f + C_N2, 1)]).then_inc(x2_hi, 1)
                    act.activation(xsq[:, j], flat(resid[:, ds(f, 1), :]), ACT.Square).then_inc(xsq_done, 1)
            with act.Fori(0, 4) as i:
                out_pair(i)
            act.wait_ge(ssum_part, 8)
            act.activation(h2(rbc[:, :]), bank[:, 0:2, 0:HALF], ACT.Sqrt, scale=1.0 / D, bias=eps).then_inc(frms, 1)

            for h in range(2):
                b0, t0 = B_FFN + B_HALF * h, T_FFN + B_HALF * h

                def up_pair(i, last):
                    for j in range(2):
                        b, t = b0 + 2 * i + j, t0 + 2 * i + j
                        n = HK * P if last and j else D
                        hi(b + 1, (b0 + j + 1) % 2, n, t, 16 * i + loads_of(b0 + j + 1))
                    g = HK * h + i
                    act.wait_ge(gate_conv, g + 1)
                    act.activation(cv[:, 1], cv[:, 1], ACT.Gelu_apprx_tanh).then_inc(gelu_done, 1)
                    act.wait_ge(prod_done, g + 1)
                    past()
                    act.activation(flat(gh[:, ds(i, 1), :]) if not last else gh[:, i], cv[:, 0], ACT.Copy
                                   ).then_inc(g_hi, 1)
                if h:
                    act.wait_ge(tile_done, t0)
                with act.Fori(0, HK - 1) as i:
                    up_pair(i, False)
                up_pair(HK - 1, True)
                b1, t1 = b0 + 2 * HK, t0 + 2 * HK
                with act.Fori(0, 3) as i:
                    for j in range(2):
                        hi(b1 + 2 * i + j + 1, (b1 + j + 1) % 2, HK * P, t1 + 2 * i + j, 16 * i + loads_of(b1 + j + 1))
                hi(b1 + 7, (b1 + 7) % 2, HK * P, t1 + 6, loads_of(b1 + 7))
                if h == 0:
                    hi(b1 + 8, (b1 + 8) % 2, D, t1 + 7, loads_of(b1 + 8))
            for n in range(6):
                w_ = min(D, 2 * FF - D * n)
                if n >= 2:
                    act.wait_ge(f_out[n % 2], 32 * (n // 2))
                evict(T_FC + n, fout[:, n % 2, 0:w_], wide[(T_FC + n) % 2][0:18, 0:w_], ACT.Copy)
            for i in range(TT):
                n, t = P if i < TT - 1 else LAST, T_FIN + i
                act.wait_ge(tile_done, t + 1)
                if i:
                    st.wait()
                st(act.activation(fsq[0:n, :], wide[t % 2][0:n, :], ACT.Square,
                                  accum_out=ssf[0:n, i:i + 1]))
                st.wait()
                act.activation(rmsf[0:n, i:i + 1], ssf[0:n, i:i + 1], ACT.Sqrt, scale=1.0 / D, bias=eps[0:n]
                               ).then_inc(fin_rms, 1)

        @block.vector
        def _(dve):
            st = Chain(dve, dve_step)
            stt, ts, tt, cpy = dve.scalar_tensor_tensor, dve.tensor_scalar, dve.tensor_tensor, dve.tensor_copy

            def mul_add(out, in0, scalar, in1, op0=ALU.mult, op1=ALU.add):
                return stt(out=out, in0=in0, scalar=scalar, in1=in1, op0=op0, op1=op1)

            for i in range(TT):
                n = P if i < TT - 1 else LAST
                dve.wait_ge(rms_done, i + 1)
                st.link(dve.reciprocal(rms[0:n, i:i + 1], rms[0:n, i:i + 1]))
                ts(x_tok[0:n, i], x_tok[0:n, i], rms[0:n, i:i + 1], None, ALU.mult).then_inc(x_scaled, 1)
            dve.wait_ge(tile_evicted, T_XN)
            for f in range(8):
                dve.wait_ge(xn_hi, f + 1)
                mul_add(xl[:, f], wide[(T_XN + f) % 2][:, 0:T], cols[:, C_N1 + f:C_N1 + f + 1], xh[:, f].bitcast(F32),
                        ALU.mult, ALU.subtract).then_inc(tile_evicted, 1)
            st(ts(qb, cols[:, C_BIN + 8:C_BIN + 16], 1.0 / 16, None, ALU.mult))
            st(dve.memset(u[:, :, 0:LW - 1], 0.0))
            st(cpy(nst[:, 1:NS, :], cols[:, C_NS:C_NS + 64].rearrange("p (b n) -> p b n", n=8)))

            def log1p_exp(y, z, z2, p, tmp):
                st.link(ts(z, y, 2.0, None, ALU.add))
                st.link(dve.reciprocal(z2, z))
                st.link(tt(z, y, z2, ALU.mult))
                st.link(tt(z2, z, z, ALU.mult))
                st.link(ts(p, z2, 1.0 / (2 * LSE_TERMS + 1), None, ALU.mult))
                for m in range(LSE_TERMS - 1, 0, -1):
                    st.link(mul_add(p, p, 1.0 / (2 * m + 1), z2, ALU.add, ALU.mult))
                st.link(mul_add(p, p, 1.0, z, ALU.add, ALU.mult))
                st.link(ts(z, p, 2.0, None, ALU.mult))

            ig, f_, yy, s3, s4, s5 = (gs[:, m, :] for m in range(6))
            dve.wait_ge(tile_evicted, T_GATE + 1)
            st.link(ts(f_, f_, gbias[:, 1:2], None, ALU.add))
            mul_add(yy, f_, -1.0, f_, ALU.mult, ALU.max).then_inc(gate_abs, 1)
            L_ = cols[:, C_LAM:C_LAM + 8]
            mul_add(lam[0], L_, -1.0, L_, ALU.mult, ALU.max).then_inc(gate_abs, 1)

            def conv_pair(i):
                for j in range(2):
                    f = 2 * i + j
                    dve.wait_ge(tile_evicted, T_U + 1 + f)
                    uf, cf = u[:, ds(f, 1), :], uc[:, ds(f, 1), :]
                    w = [cols[:, ds(f + (C_CW + 8 * m), 1)] for m in range(LW)]
                    us = usamp[:, j]
                    for g in range(2):
                        hist = cols[:, C_LC[g]:C_LC[g] + 96].rearrange("p (b l f) -> p b l f", l=LW - 1, f=8)
                        st(cpy(us[:, 4 * g:4 * g + 4, 0:LW - 1],
                               hist[:, :, :, ds(f, 1)].rearrange("p b l o -> p b (l o)")))
                    st(cpy(us[:, :, LW - 1:], flat(uf)[:, LW - 1 + TP:UW].rearrange("p (b l) -> p b l", l=LS)))
                    ul = flat(ulast[:, ds(f, 1), :])
                    st(cpy(ul[:, 0:3], flat(uf)[:, TP:TP + 3]))
                    st(cpy(ul[:, 3:27].rearrange("p (b l) -> p b l", l=3),
                           flat(uf)[:, LW - 1 + TP:UW].rearrange("p (b l) -> p b l", l=LS)[:, :, LS - 3:]))
                    cP = flat(cf)[:, 0:TP]
                    cS = flat(cf)[:, TP:T].rearrange("p (b l) -> p b l", l=LS)
                    st(ts(cP, flat(uf)[:, 0:TP], w[0], cols[:, ds(f + C_CB, 1)], ALU.mult, ALU.add))
                    st.wait()
                    st(ts(cS, us[:, :, 0:LS], w[0], cols[:, ds(f + C_CB, 1)], ALU.mult, ALU.add))
                    for m in range(1, LW):
                        st(mul_add(cP, flat(uf)[:, m:m + TP], w[m], cP))
                        st.wait()
                        ins = mul_add(cS, us[:, :, m:m + LS], w[m], cS)
                        if m < LW - 1:
                            st(ins)
                        else:
                            ins.then_inc(conv_done, 1)

            dve.wait_ge(gate_exp, 2)
            log1p_exp(lam[0], lam[1], lam[2], lam[3], None)
            st.link(mul_add(lam[4], L_, -1.0, L_, ALU.mult, ALU.min))
            st.link(ts(lam[4], L_, -1.0, 0.0, ALU.mult, ALU.max))
            st.link(tt(lam[4], lam[4], lam[1], ALU.add))
            st.link(ts(negc, lam[4], -LRU_C, None, ALU.mult))
            log1p_exp(yy, s3, s4, s5, None)
            st.link(ts(yy, f_, 0.0, None, ALU.min))
            st.link(tt(f_, yy, s3, ALU.subtract))
            sam = slice(TP, T)

            def first(ap):
                return ap[:, sam].rearrange("p (b l) -> p b l", l=LS)[:, :, 0]

            st.link(cpy(yy, f_))
            st.link(cpy(s3, ig))
            st.link(tt(first(s4), first(f_), mst, ALU.add))
            st.link(tt(first(s3), first(s4), first(ig), ALU.max))
            st.link(dve.memset(first(yy), NEG))
            M = s4
            st.link(dve.tensor_tensor_scan(out=M, data0=yy, data1=s3, initial=0.0, op0=ALU.add, op1=ALU.max))
            st.link(dve.memset(yy, 1.0))
            st.link(dve.memset(yy[:, 0:P * (TT - 1) + 1:P], 0.0))
            st.link(dve.memset(first(yy), 0.0))
            Bc = s3
            st.link(dve.tensor_tensor_scan(out=Bc, data0=yy, data1=f_, initial=0.0, op0=ALU.mult, op1=ALU.add))
            A = yy
            st.link(tt(A, Bc, M, ALU.subtract))
            st(cpy(gq[0:HEADS, :], A))
            st(tt(gq[32:32 + HEADS, :], ig, Bc, ALU.subtract))
            st(cpy(gq[96:96 + HEADS, :], M))
            st(cpy(gq[64:64 + HEADS, 0:P], A[:, 0:P]))
            for c in range(1, TT):
                e = P * c + (P if c < 4 else TAIL)
                st(ts(gq[64:64 + HEADS, P * c:e], A[:, P * c:e], M[:, P * c - 1:P * c], None, ALU.add))
            st(tt(gq[64:64 + HEADS, sam].rearrange("p (b l) -> p b l", l=LS),
                  A[:, sam].rearrange("p (b l) -> p b l", l=LS),
                  mst.rearrange("p (b o) -> p b o", o=1).to_broadcast([HEADS, NB, LS]), ALU.add))
            st(cpy(mout, M[:, TP - 1:T:LS]))
            st.wait()
            dve.memset(misc[:, 202:203], 0.0).then_inc(gates_ready, 1)
            st.loop(0, 4, 2 * (5 + 2 + 3 + 2), conv_pair)

            def lru_pair(i):
                for j in range(2):
                    f = 2 * i + j
                    a_, ucf = flat(u[:, ds(f, 1), 0:T]), flat(uc[:, ds(f, 1), :])
                    r_, i_ = ri[:, j, 0], ri[:, j, 1]
                    dve.wait_ge(lru_act, 2 * f + 1)
                    st(tt(i_, i_, ucf, ALU.mult))
                    dve.wait_ge(lru_act, 2 * f + 2)
                    st(tt(r_, a_, a_, ALU.mult))
                    st.wait()
                    mul_add(th[:, j], r_, 1.0, th[:, j], ALU.add, ALU.mult).then_inc(lru_q, 1)
                    dve.wait_ge(lru_sq, f + 1)
                    st(tt(i_, i_, th[:, j], ALU.mult))
                    h0 = cols[:, C_H0:C_H0 + 64].rearrange("p (b f) -> p b f", f=8)[:, :, ds(f, 1)].rearrange(
                        "p b o -> p (b o)")
                    a1, i1 = (x[:, sam].rearrange("p (b l) -> p b l", l=LS)[:, :, 0] for x in (a_, i_))
                    st(tt(r_[:, 0:NB], a1, h0, ALU.mult))
                    st.wait()
                    st(tt(i1, i1, r_[:, 0:NB], ALU.add))
                    st(ts(a1, a1, 0.0, None, ALU.mult))
                    st.wait()
                    dve.tensor_tensor_scan(out=ucf, data0=a_, data1=i_, initial=0.0, op0=ALU.mult, op1=ALU.add
                                           ).then_inc(lru_h, 1)
                    dve.wait_ge(lru_h, f + 1)
                    st(cpy(hlast[:, :, ds(f, 1)].rearrange("p b o -> p (b o)"),
                           flat(uc[:, ds(f, 1), TP - 1:T])[:, 0:65:LS]))
                    dve.wait_ge(lru_hi, f + 1)
                    tt(flat(hl[:, ds(f, 1), :]), ucf, flat(hh[:, ds(f, 1), :]).bitcast(F32), ALU.subtract
                       ).then_inc(lru_lo, 1)
            st.loop(0, 4, 14, lru_pair)

            dve.wait_ge(tile_evicted, T_WA)
            with dve.Fori(0, 4) as i:
                for j in range(2):
                    f = 2 * i + j
                    dve.wait_ge(tile_done, T_WA + f + 1)
                    m_ = merged[:, ds(f, 1), :]
                    tt(h2o(m_), rt((T_WA + j) % 2), h2o(m_), ALU.mult).then_inc(tile_evicted, 1)

            dve.wait_ge(lru_out, 64)
            for h in range(HEADS):
                s, t0 = h % 2, T_HEAD + HT * h
                dve.wait_ge(tile_evicted, t0 + 1)
                for j in range(2):
                    tt(qe[:, j], q[s][:, j], ebc[:, :], ALU.mult).then_inc(qe_done, 1)
                cpr = cp[s]
                if h >= 2:
                    dve.wait_ge(cp_out, 16 * (h - 1))
                for c in range(TT):
                    n, L, c0 = 5 * h + c, P if c < 4 else LAST, P * c
                    X = bx[n % 2]
                    w = wt[0:L, n % 2, 0:L]
                    dve.wait_ge(scores, n + 1)
                    if n:
                        dve.wait_ge(w_done, n)
                    tt(argm[0:L, 0:L], X[0:L, P:P + L], mask[0:L, c // 4, 0:L], ALU.add).then_inc(arg_done, 1)
                    dve.wait_ge(w_done, n + 1)
                    if n:
                        dve.wait_ge(y_done, n)
                    tt(pt[0:L, 0:L], w, X[0:L, 0:L], ALU.mult).then_inc(p_done, 1)
                    kap = 13 * h + c
                    nu = 1 if c < 4 else NS

                    def keys(m):
                        if kap + m >= 2:
                            dve.wait_ge(z_done, kap + m - 1)
                        col = L - 1 if c < 4 else TAIL - 1 + LS * m
                        ts(kw[0:L, (kap + m) % 2], kt[s][0:L, c], w[:, col:col + 1], None, ALU.mult
                           ).then_inc(kw_done, 1)

                    def update(m):
                        dve.wait_ge(z_done, kap + m + 1)
                        Z = bz if (m % 2 == 0) else bx[(n + 1) % 2]
                        if m == 0:
                            C = cpr[:, :, :].rearrange("p i v -> p (i v)")
                        else:
                            nb = NB * h + m - 1
                            C = cs[:, nb % 4].rearrange("p i v -> p (i v)")
                        if c == 0:
                            cpy(C, Z).then_inc(z_evicted, 1)
                            return
                        col = c0 + (L - 1 if c < 4 else TAIL - 1 + LS * m)
                        if kap + m:
                            dve.wait_ge(z_evicted, kap + m)
                        mul_add(C, C, ebc[:, col:col + 1], Z).then_inc(z_evicted, 1)

                    keys(0)
                    if nu > 1:
                        keys(1)
                        for m in range(nu):
                            update(m)
                            if m + 2 < nu:
                                keys(m + 2)
                    dve.wait_ge(y_done, n + 1)
                    st(cpy(hb[:, 2 * h:2 * h + 2, c0:c0 + L],
                           by[:, 0:256].rearrange("p (j t) -> p j t", j=2)[:, :, 0:L]))
                    st(cpy(den[:, c0:c0 + L], by[:, 256:256 + L]))
                    npr = nst[:, 0, 2 * h:2 * h + 2]
                    if c == 0:
                        cpy(npr, by[:, 384:386]).then_inc(y_evicted, 1)
                    elif c < 4:
                        dve.wait_ge(y_evicted, n)
                        mul_add(npr, npr, ebc[:, c0 + L - 1:c0 + L], by[:, 384:386]).then_inc(y_evicted, 1)
                    else:
                        dec = ebc[:, TP - 1:T:LS].rearrange("p (b o) -> p b o", o=1)
                        nall = nst[:, :, 2 * h:2 * h + 2]
                        dve.wait_ge(y_evicted, n)
                        st.link(tt(ntmp[:, :, :], nall, dec.to_broadcast([P, NS, 2]), ALU.mult))
                        tt(nall, ntmp[:, :, :], by[:, 384:384 + 2 * NS].rearrange("p (i b) -> p b i", b=NS),
                           ALU.add).then_inc(y_evicted, 1)
                    if nu == 1:
                        update(0)
                dve.wait_ge(tile_evicted, t0 + 2)
                st.wait()
                st.link(mul_add(qe[:, 0], den[:, :], -1.0, den[:, :], ALU.mult, ALU.max))
                st.link(tt(qe[:, 0], qe[:, 0], gbc[:, :], ALU.max))
                st.link(dve.reciprocal(den[:, :], qe[:, 0]))
                hv = hb[:, 2 * h:2 * h + 2, :]
                tt(hv, hv, den[:, :].rearrange("p (o t) -> p o t", o=1).to_broadcast([P, 2, T]), ALU.mult
                   ).then_inc(hn_done, 1)
                dve.wait_ge(tile_evicted, t0 + 14)
                st.link(dve.reciprocal(den[:, :], hsq[:, 0]))
                for j in range(2):
                    gcol = cols[:, C_HG + 2 * h + j:C_HG + 2 * h + j + 1]
                    st(mul_add(hb[:, 2 * h + j], hb[:, 2 * h + j], gcol, den[:, :], ALU.mult, ALU.mult))
                st.wait()
                tt(hv, hv, so[s][:, :, :], ALU.mult).then_inc(head_done, 1)

            for f in range(8):
                dve.wait_ge(hb_hi, f + 1)
                if f == 0:
                    dve.wait_ge(head_done, HEADS)
                tt(xl[:, f], hb[:, f], xh[:, f].bitcast(F32), ALU.subtract).then_inc(hb_lo, 1)

            def wb_pair(i):
                for j in range(2):
                    f, t = 2 * i + j, T_WB + 4 * i + 2 * j
                    g_, m_ = gbs[:, ds(f, 1), :], merged[:, ds(f, 1), :]
                    dve.wait_ge(tile_done, t + 1)
                    dve.wait_ge(tile_evicted, t)
                    tt(h2o(g_), rt(T_WB % 2), h2o(g_), ALU.mult).then_inc(tile_evicted, 1)
                    dve.wait_ge(tile_evicted, t + 1)
                    tt(flat(m_), flat(m_), flat(g_), ALU.add).then_inc(m_done, 1)
                    dve.wait_ge(m_hi, f + 1)
                    tt(flat(ml[:, ds(f, 1), :]), flat(m_), flat(mh[:, ds(f, 1), :]).bitcast(F32), ALU.subtract
                       ).then_inc(m_lo, 1)
            for n in range(4):
                dve.wait_ge(c_out[n], 16 * 8)
            with dve.Fori(0, 4) as i:
                wb_pair(i)

            dve.wait_ge(tile_evicted, T_OUT)

            def out_pair(i):
                for j in range(2):
                    f, t = 2 * i + j, T_OUT + 2 * i + j
                    r_ = resid[:, ds(f, 1), :]
                    dve.wait_ge(tile_done, t + 1)
                    tt(h2o(r_), rt((T_OUT + j) % 2), h2o(r_), ALU.add).then_inc(tile_evicted, 1)
                    dve.wait_ge(x2_hi, f + 1)
                    mul_add(flat(xl[:, ds(f, 1), :]), flat(r_), cols[:, ds(f + C_N2, 1)],
                            flat(xh[:, ds(f, 1), :]).bitcast(F32), ALU.mult, ALU.subtract).then_inc(x2_lo, 1)
            with dve.Fori(0, 4) as i:
                out_pair(i)
            dve.wait_ge(frms, 1)
            dve.reciprocal(rbc[:, :], rbc[:, :]).then_inc(rbc_done, 1)
            st(dve.memset(up[:, :, 0:FW - 1], 0.0))
            dve.wait_ge(rbc_done, 1)
            st.wait()

            for h in range(2):
                t0 = T_FFN + B_HALF * h

                def up_pair(i):
                    g = HK * h + i
                    for j in range(2):
                        t = t0 + 2 * i + j
                        ft = i + (HK * h + UPT // 2 * j)
                        U = up[:, j]
                        dve.wait_ge(tile_done, t + 1)
                        tt(h2(U[:, FW - 1:FP]), rt((t0 + j) % 2), h2(rbc[:, :]), ALU.mult).then_inc(tile_evicted, 1)
                        hist = cols[:, C_FC:C_FC + P * NB].rearrange("p (b c) -> p b c", c=P)
                        fs = fsamp[:, j]
                        for m in range(2):
                            st(cpy(fs[:, :, m:m + 1], hist[:, :, ds(ft + UPT * m, 1)]))
                        dve.wait_ge(tile_evicted, t + 1)
                        usm = U[:, FW - 1 + TP:FP].rearrange("p (b l) -> p b l", l=LS)
                        st(cpy(fs[:, :, FW - 1:], usm))
                        fl = flat(flast[:, ds(ft, 1), :])
                        st(cpy(fl[:, 0:2], U[:, TP:TP + 2]))
                        st(cpy(fl[:, 2:18].rearrange("p (b l) -> p b l", l=2), usm[:, :, LS - 2:]))
                        w = [cols[:, ds(ft + C_FCW[m], 1)] for m in range(FW)]
                        bias = cols[:, ds(ft + C_FCB, 1)]
                        cP = cv[:, j, 0:TP]
                        cS = cv[:, j, TP:T].rearrange("p (b l) -> p b l", l=LS)
                        st(ts(cP, U[:, 0:TP], w[0], bias, ALU.mult, ALU.add))
                        st.wait()
                        st(ts(cS, fs[:, :, 0:LS], w[0], bias, ALU.mult, ALU.add))
                        for m in range(1, FW):
                            st(mul_add(cP, U[:, m:m + TP], w[m], cP))
                            st.wait()
                            ins = mul_add(cS, fs[:, :, m:m + LS], w[m], cS)
                            if m == FW - 1 and j:
                                ins.then_inc(gate_conv, 1)
                            else:
                                st(ins)
                    st.wait()
                    dve.wait_ge(gelu_done, g + 1)
                    tt(cv[:, 0], cv[:, 0], cv[:, 1], ALU.mult).then_inc(prod_done, 1)
                    dve.wait_ge(g_hi, g + 1)
                    tt(flat(gl[:, ds(i, 1), :]), cv[:, 0], flat(gh[:, ds(i, 1), :]).bitcast(F32), ALU.subtract
                       ).then_inc(g_lo, 1)

                if h:
                    dve.wait_ge(tile_done, t0)
                st.loop(0, HK, 2 * (5 + 2 + 4) - 1, up_pair)
                t1 = t0 + 2 * HK
                with dve.Fori(0, 4) as i:
                    for j in range(2):
                        t = t1 + 2 * i + j
                        r_ = resid[:, ds(2 * i + j, 1), :]
                        dve.wait_ge(tile_done, t + 1)
                        tt(h2o(r_), rt((t1 + j) % 2), h2o(r_), ALU.add).then_inc(tile_evicted, 1)
            dve.wait_ge(fg_in, 16)
            for i in range(TT):
                n, t = P if i < TT - 1 else LAST, T_FIN + i
                dve.wait_ge(fin_rms, i + 1)
                st.link(dve.reciprocal(rmsf[0:n, i:i + 1], rmsf[0:n, i:i + 1]))
                if i >= 2:
                    dve.wait_ge(y_out[i % 2], 16 * (i // 2))
                mul_add(y[0:n, i % 2], wide[t % 2][0:n, :], rmsf[0:n, i:i + 1], fgb[0:n, :], ALU.mult, ALU.mult
                        ).then_inc(tile_evicted, 1)

        @block.tensor
        def _(pe):
            def begin(t):
                if not isinstance(t, int) or t >= 2:
                    pe.wait_ge(tile_evicted, t - 1)

            def split_product(out, slot, kn, xh_, xl_, wait_k=None):
                for kk in range(kn):
                    if wait_k:
                        wait_k(kk)
                    for m, (w, x) in enumerate(((whi, xh_), (whi, xl_), (wlo, xh_))):
                        for hf in range(2):
                            last = pe.matmul(out(hf), w[:, slot, kk * P:kk * P + P], x[:, kk, HALF * hf:HALF * hf + HALF],
                                             start=kk == 0 and m == 0, stop=kk == kn - 1 and m == 2)
                return last

            def gemm(b, t, bslot, tslot, kn, xh_, xl_, wait_k=None):
                pe.wait_ge(w_lo, b + 1)
                begin(t)
                split_product(lambda hf: ring[:, tslot, hf, 0:HALF], bslot, kn, xh_, xl_, wait_k).then_inc(tile_done, 1)

            pe.wait_ge(const_done, 2)
            pe.wait_ge(rows_in, 16 * 25)
            for g in range(4):
                t = T_COLS + g
                begin(t)
                for m in range(4 * g, min(4 * g + 4, NROW)):
                    last = pe.transpose(wide[t % 2][:, P * (m - 4 * g):P * (m - 4 * g) + ROWS[m]],
                                        rows[0:ROWS[m], m, :], ident[0:ROWS[m], 0:ROWS[m]])
                last.then_inc(tile_done, 1)
            pe.wait_ge(x_scaled, TT)

            def token_transposes(t, f, src):
                begin(t)
                for i in range(TT):
                    n = P if i < TT - 1 else LAST
                    last = pe.transpose(wide[t % 2][:, P * i:P * i + n], src[0:n, i, P * f:P * f + P], ident[0:n, 0:n])
                last.then_inc(tile_done, 1)

            for f in range(8):
                token_transposes(T_XN + f, f, x_tok)
            pe.wait_ge(tile_evicted, T_XN + 8)
            gemm(B_GATE, T_GATE, 0, T_GATE % 2, KT, xh, xl)
            with pe.Fori(0, 4) as i:
                for j in range(2):
                    gemm(B_U + 2 * i + j, T_U + 2 * i + j, (B_U + j) % 2, (T_U + j) % 2, KT, xh, xl)
            def ga_pair(i):
                for j in range(2):
                    gemm(B_GA + 2 * i + j, T_GA + 2 * i + j, (B_GA + j) % 2, (T_GA + j) % 2, KT, xh, xl)
                    f = 2 * i + j
                    pe.wait_ge(conv_done, f + 1)
                    pe.wait_ge(bd_in[j], 64 * (i + 1))
                    if not isinstance(f, int) or f:
                        pe.wait_ge(lru_act, 2 * f)
                    for g in range(2):
                        for hf in range(2):
                            last = pe.matmul(bank[:, 2 * g + hf, 0:HALF], bd[:, j, g, :],
                                             flat(uc[:, ds(f, 1), HALF * hf:HALF * hf + HALF]), start=True, stop=True)
                    last.then_inc(lru_ps, 1)
            ga_pair(0)
            with pe.Fori(1, 4) as i:
                ga_pair(i)
            pe.wait_ge(lru_lo, 8)
            t = T_LC
            begin(t)
            for f in range(8):
                last = pe.transpose(wide[t % 2][0:27, P * f:P * f + P], ulast[:, f, :], ident[:, :])
            last.then_inc(tile_done, 1)
            begin(t + 1)
            pe.transpose(wide[(t + 1) % 2][0:72, 0:P], stage[:, 0, D + 224:D + 224 + 72], ident[:, :]).then_inc(tile_done, 1)
            with pe.Fori(0, 4) as i:
                for j in range(2):
                    gemm(B_WA + 2 * i + j, T_WA + 2 * i + j, (B_WA + j) % 2, (T_WA + j) % 2, KT, hh, hl)
            for n in range(8):
                gemm(B_HEAD + n, T_HEAD0 + n, (B_HEAD + n) % 2, (T_HEAD0 + n) % 2, KT, xh, xl)

            def fill(h, n):
                b, t = B_HEAD + 8 * (h + 1) + n, T_HEAD + HT * h + 5 + n
                gemm(b, t, b % 2, t % 2, KT, xh, xl)

            pe.wait_ge(gates_ready, 1)
            for h in range(HEADS):
                s, t0 = h % 2, T_HEAD + HT * h
                for m, r0 in enumerate((64, 96)):
                    begin(t0 + m)
                    for hf in range(2):
                        last = pe.matmul(ring[:, (t0 + m) % 2, hf, 0:HALF], sel[r0:r0 + HEADS, h, :],
                                         gq[r0:r0 + HEADS, HALF * hf:HALF * hf + HALF], start=True, stop=True)
                    last.then_inc(tile_done, 1)
                for m in range(3):
                    t = t0 + 2 + m
                    begin(t)
                    for cc in range(2 if m < 2 else 1):
                        c = 2 * m + cc
                        L = P if c < 4 else LAST
                        for w_, src in enumerate((k[s], vf)):
                            for jj in range(2):
                                last = pe.transpose(wide[t % 2][0:L, 512 * cc + 256 * w_ + 128 * jj:][:, 0:P],
                                                    src[:, jj, P * c:P * c + L], ident[:, :])
                    last.then_inc(tile_done, 1)

                def score(c):
                    n, L, c0 = 5 * h + c, P if c < 4 else LAST, P * c
                    X = bx[n % 2]
                    if n >= 2:
                        pe.wait_ge(p_done, n - 1)
                    if h:
                        pe.wait_ge(z_evicted, 13 * h)
                    for jj in range(2):
                        pe.matmul(X[0:L, 0:L], k[s][:, jj, c0:c0 + L], q[s][:, jj, c0:c0 + L], start=jj == 0, stop=jj == 1)
                    pe.matmul(X[0:L, P:P + L], sel[0:HEADS, h, 0:L], gq[0:HEADS, c0:c0 + L], start=True, stop=False
                              ).then_inc(arg_part, 1)
                    pe.wait_ge(arg_part, n + 1)
                    pe.matmul(X[0:L, P:P + L], gq[32:32 + HEADS, c0:c0 + L], sel[32:32 + HEADS, h, 0:L],
                              start=False, stop=True).then_inc(scores, 1)

                def values(c):
                    n, L, c0 = 5 * h + c, P if c < 4 else LAST, P * c
                    kap = 13 * h + c
                    cpr = cp[s]
                    w = wt[0:L, n % 2]
                    pe.wait_ge(p_done, n + 1)
                    if n:
                        pe.wait_ge(y_evicted, n)
                    inter = c > 0
                    for jj in range(2):
                        pe.matmul(by[:, P * jj:P * jj + L], vt[s][0:L, c, P * jj:P * jj + P], pt[0:L, 0:L],
                                  start=jj == 0, stop=not inter, skip_group_check=True)
                    pe.matmul(by[:, 256:256 + L], ones[0:L, :], pt[0:L, 0:L], start=False, stop=not inter,
                              skip_group_check=True)
                    nu = 1 if c < 4 else NS
                    first_ = L - 1 if c < 4 else TAIL - 1
                    for jj in range(2):
                        last = pe.matmul(by[:, 384 + nu * jj:384 + nu * jj + nu], kt[s][0:L, c, P * jj:P * jj + P],
                                         w[:, first_:first_ + LS * (nu - 1) + 1:LS], start=False, stop=True,
                                         skip_group_check=True)

                    def across(cols_, C, ncol):
                        for jj in range(2):
                            for ii in range(2):
                                pe.matmul(by[:, P * jj + cols_.start:P * jj + cols_.stop], C[:, ii, P * jj:P * jj + P],
                                          qe[:, ii, c0 + cols_.start:c0 + cols_.stop], start=False, stop=ii == 1,
                                          skip_group_check=True)
                        for ii in range(2):
                            last = pe.matmul(by[:, 256 + cols_.start:256 + cols_.stop],
                                             ncol[:, ii:ii + 1].to_broadcast([P, P]),
                                             qe[:, ii, c0 + cols_.start:c0 + cols_.stop], start=False, stop=ii == 1,
                                             skip_group_check=True)
                        return last

                    def outer(m):
                        Z = bz if m % 2 == 0 else bx[(n + 1) % 2]
                        pe.wait_ge(kw_done, kap + m + 1)
                        if kap + m >= (2 if c == 4 else 1):
                            pe.wait_ge(z_evicted, kap + m - (1 if c == 4 and m > 1 else 0))
                        for ii in range(2):
                            lz = pe.matmul(Z[:, 256 * ii:256 * ii + 256], kw[0:L, (kap + m) % 2, P * ii:P * ii + P],
                                           vt[s][0:L, c, :], start=True, stop=True)
                        lz.then_inc(z_done, 1)

                    if inter:
                        pe.wait_ge(qe_done, 2 * h + 2)
                        pe.wait_ge(z_evicted, kap)
                        last = across(slice(0, L if c < 4 else TAIL), cpr, nst[:, 0, 2 * h:2 * h + 2])
                    if c < 4:
                        last.then_inc(y_done, 1)
                        outer(0)
                        return
                    outer(0)
                    for b in range(NB):
                        nb = NB * h + b
                        if b == 4:
                            fill(h, 5)
                        pe.wait_ge(c_in[nb % 4], 16 * (nb // 4 + 1))
                        last = across(slice(TAIL + LS * b, TAIL + LS * b + LS), cs[:, nb % 4],
                                      nst[:, 1 + b, 2 * h:2 * h + 2])
                        if b == NB - 1:
                            last.then_inc(y_done, 1)
                        outer(1 + b)

                score(0)
                fill(h, 0)
                for c in range(TT):
                    values(c)
                    if c < 4:
                        score(c + 1)
                        fill(h, c + 1)
                fill(h, 6)
                fill(h, 7)
                t = t0 + 13
                pe.wait_ge(hsq_done, h + 1)
                begin(t)
                for hf in range(2):
                    for jj in range(2):
                        last = pe.matmul(ring[:, t % 2, hf, 0:HALF], ones[:, :], hsq[:, jj, HALF * hf:HALF * hf + HALF],
                                         start=jj == 0, stop=jj == 1)
                last.then_inc(tile_done, 1)
            t = T_NOUT
            pe.wait_ge(y_evicted, 5 * HEADS)
            begin(t)
            pe.transpose(wide[t % 2][0:72, 0:P], nst[:, :, :].rearrange("p b n -> p (b n)"), ident[:, :]
                         ).then_inc(tile_done, 1)
            pe.wait_ge(hb_lo, 8)
            for f in range(8):
                t = T_WB + 2 * f
                gemm(B_WB + f, t, (B_WB + f) % 2, t % 2, KT, xh, xl)
                if f == 0:
                    pe.wait_ge(x2_in, 80)
                token_transposes(t + 1, f, x_tok2)
            pe.wait_ge(m_lo, 8)

            def sum_squares(f):
                pe.wait_ge(xsq_done, f + 1)
                for hf in range(2):
                    last = pe.matmul(bank[:, hf, 0:HALF], ones[:, :], xsq[:, f % 2, HALF * hf:HALF * hf + HALF],
                                     start=f == 0, stop=f == 7)
                last.then_inc(ssum_part, 1)

            for f in range(8):
                gemm(B_OUT + f, T_OUT + f, (B_OUT + f) % 2, (T_OUT + f) % 2, KT, mh, ml)
                if f:
                    sum_squares(f - 1)
            sum_squares(7)
            pe.wait_ge(x2_lo, 8)
            for h in range(2):
                b0, t0 = B_FFN + B_HALF * h, T_FFN + B_HALF * h
                with pe.Fori(0, HK) as i:
                    for j in range(2):
                        gemm(b0 + 2 * i + j, t0 + 2 * i + j, (b0 + j) % 2, (t0 + j) % 2, KT, xh, xl)
                b1, t1 = b0 + 2 * HK, t0 + 2 * HK

                def arrived(kk):
                    pe.wait_ge(g_lo, HK * h + kk + 1)
                for m in range(8):
                    gemm(b1 + m, t1 + m, (b1 + m) % 2, (t1 + m) % 2, HK, gh, gl, arrived if m == 0 else None)
            for n in range(6):
                t = T_FC + n
                begin(t)
                for m in range(8 * n, min(8 * n + 8, UPT)):
                    last = pe.transpose(wide[t % 2][0:18, P * (m - 8 * n):P * (m - 8 * n) + P], flast[:, m, :], ident[:, :])
                last.then_inc(tile_done, 1)
            pe.wait_ge(tile_evicted, T_FC)
            for i in range(TT):
                n, t = P if i < TT - 1 else LAST, T_FIN + i
                begin(t)
                for f in range(8):
                    last = pe.transpose(wide[t % 2][0:n, P * f:P * f + P], resid[:, f, P * i:P * i + n], ident[:, :])
                last.then_inc(tile_done, 1)


_INS = ["x_prompt", "x_sample", "state_lru_conv", "state_lru_h", "state_mlstm_C", "state_mlstm_n",
        "state_mlstm_m", "state_ffn_conv", "meta_tokens", "norm1_g", "w_in", "b_in", "lru_conv_w", "lru_conv_b",
        "lru_w_r", "lru_b_r", "lru_w_i", "lru_b_i", "lru_lambda", "mlstm_head_g", "w_branch_a", "w_branch_b",
        "w_out", "norm2_g", "w_up", "ffn_conv_w", "ffn_conv_b", "w_down", "final_g"]
_OUTS = [("y_prompt", (1, SEQ, D)), ("y_sample", (NB, LS, D)),
         ("p_lru_conv", (1, 1, 3, D)), ("p_lru_h", (1, 1, D)), ("p_mlstm_C", (1, 1, HEADS, DH, DH)),
         ("p_mlstm_n", (1, 1, HEADS, DH)), ("p_mlstm_m", (1, 1, HEADS)), ("p_ffn_conv", (1, 1, 2, 2 * FF)),
         ("s_lru_conv", (1, NB, 3, D)), ("s_lru_h", (1, NB, D)), ("s_mlstm_C", (1, NB, HEADS, DH, DH)),
         ("s_mlstm_n", (1, NB, HEADS, DH)), ("s_mlstm_m", (1, NB, HEADS)), ("s_ffn_conv", (1, NB, 2, 2 * FF))]


def kernel(**inputs):
    import concourse.bacc as bacc
    from concourse.bass_utils import run_bass_kernel_spmd

    nc = bacc.Bacc("TRN2", target_bir_lowering=False, num_devices=1)
    arrays, a, o = {}, {}, {}
    for name in _INS:
        x = np.ascontiguousarray(inputs[name])
        arrays[f"in_{name}"] = x
        a[name] = nc.dram_tensor(f"in_{name}", x.shape, mybir.dt.from_np(x.dtype), kind="ExternalInput").ap()
    for name, shape in _OUTS:
        o[name] = nc.dram_tensor(f"out_{name}", shape, F32, kind="ExternalOutput").ap()
    hybrid_layer(nc, a, o)
    r = run_bass_kernel_spmd(nc, [arrays], core_ids=[0])
    return tuple(r.results[0][f"out_{name}"] for name, _ in _OUTS)
```

```python
import numpy as np
import concourse.bass as bass
from concourse import mybir
from contextlib import ExitStack

F32 = mybir.dt.float32
F32R = mybir.dt.float32r
ALU = mybir.AluOpType
ACT = mybir.ActivationFunctionType
ds = bass.ds

D = 1024
P = 128
KT = D // P
SEQ, META = 512, 16
TP = SEQ + META
NB, LS = 8, 8
T = TP + NB * LS
HALF = T // 2
TT = -(-T // P)
LAST = T - (TT - 1) * P
TAIL = LAST - NB * LS
NS = NB + 1
HEADS, DH = 4, 256
LW, FW = 4, 3
FF = 2816
UPT = 2 * FF // P
HK = FF // P // 2
BW = 64
EPS = 1e-6
LRU_C = 8.0
LSE_TERMS = 8
NEG = -1.0e30
COL_I = D + 4 * D
COL_F = COL_I + HEADS
COL_GA = COL_F + HEADS
COL_GB = COL_GA + D

C_N1, C_N2, C_BIN, C_BGA, C_BGB, C_CW, C_CB, C_BR, C_BI = 0, 8, 16, 56, 64, 72, 104, 112, 120
C_LAM, C_HG, C_H0 = 128, 136, 144
C_NS, C_FCB = 256, 320
C_FCW = (384, 384 + UPT, 512)
C_LC = (640, 768)
C_FC = 896
NROW = 15
ROWS = [128, 80, 108, 88, 44, 96, 96] + [88] * 8

B_GATE, B_U, B_GA, B_WA, B_HEAD = 0, 1, 9, 17, 25
B_GB = B_HEAD + 8 * HEADS
B_WB = B_GB + 8
B_OUT = B_WB + 8
B_FFN = B_OUT + 8
B_HALF = 2 * HK + 8
B_END = B_FFN + 2 * B_HALF
T_COLS = 0
T_XN = 4
T_GATE = T_XN + 8
T_U = T_GATE + 1
T_GA = T_U + 8
T_LC = T_GA + 8
T_WA = T_LC + 2
T_HEAD0 = T_WA + 8
T_HEAD = T_HEAD0 + 8
HT = 14
T_NOUT = T_HEAD + HT * HEADS
T_WB = T_NOUT + 1
T_OUT = T_WB + 16
T_FFN = T_OUT + 8
T_FC = T_FFN + 2 * B_HALF
T_FIN = T_FC + 6

TB = 4 * T
SLOT = 4 * HK * P


class Chain:

    def __init__(self, eng, sem):
        self.eng, self.sem, self.base, self.n = eng, sem, 0, 0

    def __call__(self, ins):
        ins.then_inc(self.sem, 1)
        self.n += 1
        return ins

    def wait(self):
        self.eng.wait_ge(self.sem, self.base + self.n)

    def link(self, ins):
        self(ins)
        self.wait()

    def loop(self, first, last, per, body):
        start = self.n
        with self.eng.Fori(first, last) as i:
            self.base = start + per * (i - first)
            self.n = 0
            body(i)
            assert self.n == per, (self.n, per)
        self.base, self.n = 0, start + per * (last - first)


def flat(ap):
    return ap.rearrange("p o t -> p (o t)")


def hybrid_layer(nc, a, o):
    w_in, b_in = a["w_in"][0], a["b_in"][0]
    ctx = ExitStack()
    with ctx:
        base = 16512

        def sb(name, shape, off, dt=F32):
            return nc.alloc_sbuf_tensor_at(name, shape, dt, offset=base + off)

        def sem(name):
            return ctx.enter_context(nc.semaphore(name))

        o_a = 6 * SLOT
        o_c = o_a + 16 * TB
        o_b = o_c + 8 * TB
        o_h = o_b + 8 * TB
        o_p = o_h + 85568
        stage = sb("stage", [P, 2, HK * P], 0)
        whi = sb("whi", [P, 2, HK * P], 2 * SLOT, F32R)
        wlo = sb("wlo", [P, 2, HK * P], 4 * SLOT, F32R)
        ulast = stage[:, 0, D:D + 8 * 27].rearrange("p (f n) -> p f n", n=27)
        hlast = stage[:, 0, D + 224:D + 224 + 72].rearrange("p (b f) -> p b f", f=8)
        usamp = stage[:, 1, D:D + 176].rearrange("p (s b l) -> p s b l", s=2, l=LW - 1 + LS)
        xh = sb("xh", [P, 8, T], o_a, F32R)
        xl = sb("xl", [P, 8, T], o_a + 8 * TB, F32R)
        merged = sb("merged", [P, 8, T], o_c)
        hb = sb("hb", [P, 8, T], o_b)
        gs = sb("gate_scratch", [HEADS, 6, T], o_b)
        th = sb("lru_tanh", [P, T], o_b + 6 * TB)
        sq_tok = sb("sq_tok", [P, D], o_b)
        conv_out = sb("conv_out", [27, D], o_h)
        h_out = sb("h_out", [72, P], o_h + 4096)
        resid = sb("resid", [P, 8, T], o_b)
        x_tok = sb("x_tok", [P, TT, D], o_h)
        rows = sb("rows", [P, NROW, P], o_h + 20480)
        UW = LW - 1 + T
        u = sb("u", [P, 8, UW], o_h)
        uc = sb("uc", [P, 8, T], o_h + 32 * UW)
        hh = sb("hh", [P, 8, T], o_h + 32 * UW + 8 * TB, F32R)
        hl = sb("hl", [P, 8, T], o_h + 32 * UW + 16 * TB, F32R)
        ri = sb("ri", [P, 2, T], o_h + 32 * UW + 24 * TB)
        SB = 6 * TB + 10240

        def head_slot(name, shape, off):
            return [sb(f"{name}{s}", shape, o_h + SB * s + off) for s in range(2)]

        q = head_slot("q", [P, 2, T], 0)
        k = head_slot("k", [P, 2, T], 2 * TB)
        so = head_slot("sig_o", [P, 2, T], 4 * TB)
        kt = head_slot("k_tok", [P, TT, DH], 6 * TB)
        vt = head_slot("v_tok", [P, TT, DH], 6 * TB + 5120)
        r = o_h + 2 * SB
        vf = sb("v_feat", [P, 2, T], r)
        qe = sb("q_e", [P, 2, T], r + 2 * TB)
        cs = sb("c_sample", [P, 4, 2, DH], r + 4 * TB)
        r += 4 * TB + 8192
        cp0 = sb("c_prompt0", [P, 2, DH], r)
        ebc = sb("e_int", [P, T], r + 2048)
        gbc = sb("guard", [P, T], r + 2048 + TB)
        den = sb("den", [P, T], r + 2048 + 2 * TB)
        hsq = sb("h_sq", [P, 2, T], r + 2048 + 3 * TB)
        r += 2048 + 5 * TB
        argm = sb("arg", [P, P], r)
        wt = sb("w_t", [P, 2, P], r + 512)
        pt = sb("p_t", [P, P], r + 1536)
        kw = sb("k_w", [P, 2, DH], r + 2048)
        ntmp = sb("n_tmp", [P, NS, 2], r + 4096)
        n_rows = sb("n_rows", [72, P], r + 4096 + 96)
        gbs = sb("sig_gb", [P, 8, T], o_h)
        mh = sb("mh", [P, 8, T], o_h + SB, F32R)
        ml = sb("ml", [P, 8, T], o_h + SB + 8 * TB, F32R)
        x_tok2 = sb("x_tok2", [P, TT, D], o_h + SB + 16 * TB)
        xsq = sb("x_sq", [P, 2, T], o_c)
        rbc = sb("rstd", [P, T], o_c + 2 * TB)
        fout = sb("f_out", [18, 2, D], o_c + 3 * TB)
        gh = sb("gh", [P, HK, T], o_h, F32R)
        gl = sb("gl", [P, HK, T], o_h + HK * TB, F32R)
        r = o_h + 2 * HK * TB
        FP = FW - 1 + T
        up = sb("up", [P, 2, FP], r)
        cv = sb("conv", [P, 2, T], r + 4768)
        r += 4768 + 2 * TB
        fsamp = sb("f_samp", [P, 2, NB, FW - 1 + LS], r)
        flast = sb("f_last", [P, UPT, 18], r + 640)
        fgb = sb("final_g_b", [P, D], r + 640 + 72 * UPT)
        y = sb("y", [P, 2, D], o_h)
        fsq = sb("fin_sq", [P, D], o_h + 8192)
        cols = sb("cols", [P, NROW * P], o_p)
        r = o_p + 512 * NROW
        ident = sb("ident", [P, P], r)
        ones = sb("ones", [P, P], r + 512)
        mask = sb("mask", [P, 2, P], r + 1024)
        sel = sb("sel", [P, HEADS, P], r + 2048)
        gq = sb("gate_rows", [P, T], r + 4096)
        r += 4096 + TB
        nst = sb("n_state", [P, NS, 8], r)
        misc = sb("misc", [P, 256], r + 288)
        bd = sb("lru_gate_w", [P, 2, P], r + 1312)
        cp = [cp0, sb("c_prompt1", [P, 2, DH], r + 1312)]
        ss, rms, eps, one = misc[:, 0:5], misc[:, 8:13], misc[:, 16:17], misc[:, 17:18]
        qb, negc = misc[:, 24:32], misc[:, 32:40]
        lam = [misc[:, 40 + 8 * n:48 + 8 * n] for n in range(6)]
        ssf, rmsf = misc[:, 96:101], misc[:, 104:109]
        gbias = misc[0:HEADS, 112:114]
        mst = misc[0:HEADS, 120:128]
        mout = misc[0:HEADS, 128:137]

        ring = ctx.enter_context(nc.psum_tensor("ring", [P, 2, 2, 512], F32))
        bank = ctx.enter_context(nc.psum_tensor("bank", [P, 4, 512], F32))
        wide = [ring[:, s].rearrange("p h t -> p (h t)") for s in range(2)]
        bx = [bank[:, 0], bank[:, 1]]
        by = bank[:, 2]
        bz = bank[:, 3]

        def rt(s, rows_=slice(0, P)):
            return ring[rows_, s, :, 0:HALF]

        def h2(ap):
            return ap.rearrange("p (h t) -> p h t", h=2)

        def h2o(ap):
            return ap.rearrange("p o (h t) -> p (o h) t", h=2)

        w_loaded = [sem("w_loaded0"), sem("w_loaded1")]
        w_hi, w_lo = sem("w_hi"), sem("w_lo")
        tile_done, tile_evicted = sem("tile_done"), sem("tile_evicted")
        x_in = [sem(f"x_in{i}") for i in range(3)]
        rows_in, gate_rows_in, x2_in = sem("rows_in"), sem("gate_in"), sem("x2_in")
        const_done, gate_zero, sq_done, x_scaled, xn_hi = (
            sem("const_done"), sem("gate_zero"), sem("sq_done"), sem("x_scaled"), sem("xn_hi"))
        rms_done = sem("rms_done")
        lam_abs, lam_exp, gate_abs, gate_exp, gates_ready = (
            sem("lam_abs"), sem("lam_exp"), sem("gate_abs"), sem("gate_exp"), sem("gates_ready"))
        bd_in, negc_ready = sem("bd_in"), sem("negc_ready")
        bd_zero, conv_done, lru_ps, lru_act, lru_q, lru_sq, lru_h, lru_hi, lru_lo_ = (
            sem("bd_zero"), sem("conv_done"), sem("lru_ps"), sem("lru_act"), sem("lru_q"),
            sem("lru_sq"), sem("lru_h"), sem("lru_hi"), sem("lru_lo"))
        c_in = [sem(f"c_in{n}") for n in range(4)]
        c_out = [sem(f"c_out{n}") for n in range(4)]
        cp_out = sem("cp_out")
        arg_part = sem("arg_part")
        scores, arg_done, w_done, p_done = sem("scores"), sem("arg_done"), sem("w_done"), sem("p_done")
        qe_done, kw_done, y_done, y_evicted, z_done, z_evicted = (
            sem("qe_done"), sem("kw_done"), sem("y_done"), sem("y_evicted"), sem("z_done"),
            sem("z_evicted"))
        hn_done, hsq_done, hrms_done, head_done = (
            sem("hn_done"), sem("hsq_done"), sem("hrms_done"), sem("head_done"))
        hb_hi, hb_lo, m_done, m_hi, m_lo = (
            sem("hb_hi"), sem("hb_lo"), sem("m_done"), sem("m_hi"), sem("m_lo"))
        xsq_done, ssum_part, x2_hi, x2_lo, frms, rbc_done = (
            sem("xsq_done"), sem("ssum_part"), sem("x2_hi"), sem("x2_lo"),
            sem("frms"), sem("rbc_done"))
        gate_conv, gelu_done, prod_done, g_hi, g_lo = (
            sem("gate_conv"), sem("gelu_done"), sem("prod_done"), sem("g_hi"), sem("g_lo"))
        fin_rms = sem("fin_rms")
        fg_in = sem("fg_in")
        y_out = [sem("y_out0"), sem("y_out1")]
        lru_out, n_out, m_out, f_out = sem("lru_out"), sem("n_out"), sem("m_out"), [sem("f_out0"), sem("f_out1")]
        act_step, dve_step, pool_step = sem("act_step"), sem("dve_step"), sem("pool_step")

        def half_lo(h):
            return HK * h

        block = ctx.enter_context(nc.Block())

        @block.sync
        def _(sp):
            def kview(w, kt_):
                return w.rearrange("(k p) m -> p k m", p=P)

            def load(b, slot, src, c0, k0=0, kn=KT):
                sp.dma_start(stage[:, slot, 0:kn * P].rearrange("p (k m) -> p k m", m=P),
                             src.rearrange("(k p) m -> p k m", p=P)[:, k0:k0 + kn, c0]
                             ).then_inc(w_loaded[slot], 16)

            def stream(b0, src, c0):
                def pair(i):
                    for j in range(2):
                        b = b0 + 2 * i + j
                        sp.wait_ge(w_lo, b - 1)
                        load(b, (b0 + j) % 2, src, ds(c0 + 256 * i + 128 * j, P))
                with sp.Fori(0, 4) as i:
                    pair(i)

            xp, xs, meta = a["x_prompt"][0], a["x_sample"].rearrange("b l d -> (b l) d"), a["meta_tokens"]

            def load_x(dst, sems):
                sp.dma_start(dst[0:META, 0], meta).then_inc(sems[0], 16)
                sp.dma_start(dst[META:P, 0], xp[0:P - META]).then_inc(sems[0], 16)
                sp.dma_start(dst[:, 1:TT - 1], xp[P - META:P - META + 3 * P].rearrange("(i p) d -> p i d", p=P)
                             ).then_inc(sems[1], 16)
                sp.dma_start(dst[0:TAIL, TT - 1], xp[SEQ - TAIL:SEQ]).then_inc(sems[2], 16)
                sp.dma_start(dst[TAIL:LAST, TT - 1], xs).then_inc(sems[2], 16)

            load_x(x_tok, x_in)
            sp.wait_ge(gate_zero, 1)
            g0 = stage[:, 0, 0:D].rearrange("p (k m) -> p k m", m=P)
            for c0, at in ((COL_I, 0), (COL_F, 32)):
                sp.dma_start(g0[:, :, at:at + HEADS],
                             w_in.rearrange("(k p) m -> p k m", p=P)[:, :, c0:c0 + HEADS]
                             ).then_inc(w_loaded[0], 16)
            load(1, 1, w_in, slice(0, P))
            sp.wait_ge(w_lo, 1)
            load(2, 0, w_in, slice(P, 2 * P))

            def lru_load(p):
                for g, w in enumerate((a["lru_w_r"][0], a["lru_w_i"][0])):
                    for hf in range(2):
                        sp.dma_start(bd[BW * hf:BW * hf + BW, g, BW * hf:BW * hf + BW],
                                     w[ds(2 * p + hf, 1)].rearrange("o c d -> (o c) d")).then_inc(bd_in, 16)

            sp.wait_ge(bd_zero, 1)
            lru_load(0)

            def with_lru(b0, c0, i, p):
                for j in range(2):
                    b = b0 + 2 * i + j
                    sp.wait_ge(w_lo, b - 1)
                    load(b, (b0 + j) % 2, w_in, ds(c0 + 256 * i + 128 * j, P))
                sp.wait_ge(lru_ps, p)
                lru_load(p)
            with sp.Fori(1, 4) as i:
                with_lru(B_U, 0, i, i)
            with sp.Fori(0, 4) as i:
                with_lru(B_GA, COL_GA, i, i + 4)
            stream(B_WA, a["w_branch_a"][0], 0)
            sp.wait_ge(tile_evicted, T_LC + 2)
            sp.dma_start(o["p_lru_conv"][0, 0], conv_out[0:3, :]).then_inc(lru_out, 16)
            sp.dma_start(o["s_lru_conv"][0].rearrange("b j c -> (b j) c"), conv_out[3:27, :]).then_inc(lru_out, 16)
            sp.dma_start(o["p_lru_h"].rearrange("l b (f c) -> (l b f) c", c=P), h_out[0:8, :]).then_inc(lru_out, 16)
            sp.dma_start(o["s_lru_h"].rearrange("l b (f c) -> (l b f) c", c=P), h_out[8:72, :]).then_inc(lru_out, 16)

            def head_load(n):
                b = B_HEAD + n
                if n < 8 * HEADS:
                    h, part, j = n // 8, n % 8 // 2, n % 2
                    c0 = D * (1 + part) + DH * h + P * j
                else:
                    c0 = COL_GB + P * (n - 8 * HEADS)
                sp.wait_ge(w_lo, b - 1)
                load(b, b % 2, w_in, slice(c0, c0 + P))

            def c_load(n):
                if n >= 4:
                    sp.wait_ge(c_out[n % 4], 16 * (n // 4))
                sp.dma_start(cs[:, n % 4], a["state_mlstm_C"][0, n % NB, n // NB].rearrange("(i p) v -> p i v", p=P)
                             ).then_inc(c_in[n % 4], 16)

            def c_store(n):
                sp.wait_ge(z_evicted, 13 * (n // NB) + 5 + n % NB + 1)
                sp.dma_start(o["s_mlstm_C"][0, n % NB, n // NB].rearrange("(i p) v -> p i v", p=P), cs[:, n % 4]
                             ).then_inc(c_out[n % 4], 16)

            for n in range(8):
                head_load(n)
            sp.wait_ge(gates_ready, 1)
            sp.dma_start(o["p_mlstm_m"][0].rearrange("b h -> h b"), mout[:, 0:1]).then_inc(m_out, 16)
            with nc.allow_non_contiguous_dma(reason="32 single values"):
                sp.dma_start(o["s_mlstm_m"][0].rearrange("b h -> h b"), mout[:, 1:NS]).then_inc(m_out, 16)
            sp.wait_ge(tile_done, T_WA + 8)
            for n in range(4):
                c_load(n)
            for h in range(HEADS):
                for n in range(6):
                    head_load(8 * (h + 1) + n)
                for n in range(4):
                    c_store(NB * h + n)
                    c_load(NB * h + 4 + n)
                head_load(8 * (h + 1) + 6)
                head_load(8 * (h + 1) + 7)
                sp.wait_ge(z_evicted, 13 * h + 5)
                sp.dma_start(o["p_mlstm_C"][0, 0, h].rearrange("(i p) v -> p i v", p=P), cp[h % 2][:, :, :]
                             ).then_inc(cp_out, 16)
                for n in range(4, 8):
                    c_store(NB * h + n)
                    if h + 1 < HEADS:
                        c_load(NB * h + 4 + n)
            wb = a["w_branch_b"][0]
            for j in range(2):
                sp.wait_ge(w_lo, B_WB + j - 1)
                load(B_WB + j, (B_WB + j) % 2, wb, slice(P * j, P * j + P))
            sp.wait_ge(head_done, HEADS)
            sp.wait_ge(cp_out, 16 * HEADS)
            for n in range(4):
                sp.wait_ge(c_out[n], 16 * 8)
            sp.wait_ge(tile_evicted, T_NOUT + 1)
            load_x(x_tok2, [x2_in] * 3)
            sp.dma_start(o["p_mlstm_n"].rearrange("l b h (i p) -> (l b h i) p", p=P), n_rows[0:8, :]).then_inc(n_out, 16)
            sp.dma_start(o["s_mlstm_n"].rearrange("l b h (i p) -> (l b h i) p", p=P), n_rows[8:72, :]).then_inc(n_out, 16)
            with sp.Fori(1, 4) as i:
                for j in range(2):
                    b = B_WB + 2 * i + j
                    sp.wait_ge(w_lo, b - 1)
                    load(b, (B_WB + j) % 2, wb, ds(256 * i + 128 * j, P))
            stream(B_OUT, a["w_out"][0], 0)
            for h in range(2):
                b0 = B_FFN + B_HALF * h
                with sp.Fori(0, HK) as i:
                    for j in range(2):
                        b = b0 + 2 * i + j
                        sp.wait_ge(w_lo, b - 1)
                        load(b, (b0 + j) % 2, a["w_up"][0], ds(FF * j + P * (HK * h) + P * i, P))
                if h == 0:
                    sp.wait_ge(tile_evicted, T_OUT + 8)
                    sp.dma_start(fgb[:, :], a["final_g"].rearrange("(o d) -> o d", o=1).to_broadcast([P, D])
                                 ).then_inc(fg_in, 16)
                b1 = b0 + 2 * HK
                with sp.Fori(0, 4) as i:
                    for j in range(2):
                        b = b1 + 2 * i + j
                        sp.wait_ge(w_lo, b - 1)
                        load(b, (b1 + j) % 2, a["w_down"][0], ds(256 * i + 128 * j, P), HK * h, HK)
            for n in range(6):
                sp.wait_ge(tile_evicted, T_FC + n + 1)
                w_ = min(D, 2 * FF - D * n)
                sp.dma_start(o["p_ffn_conv"][0, 0, :, D * n:D * n + w_], fout[0:2, n % 2, 0:w_]).then_inc(f_out[n % 2], 16)
                sp.dma_start(o["s_ffn_conv"][0].rearrange("b j c -> (b j) c")[:, D * n:D * n + w_],
                             fout[2:18, n % 2, 0:w_]).then_inc(f_out[n % 2], 16)
            yp, ys = o["y_prompt"][0], o["y_sample"].rearrange("b l d -> (b l) d")
            for i in range(TT):
                sp.wait_ge(tile_evicted, T_FIN + i + 1)
                s = y_out[i % 2]
                if i == 0:
                    sp.dma_start(yp[0:P - META], y[META:P, 0]).then_inc(s, 16)
                elif i < TT - 1:
                    sp.dma_start(yp[P * i - META:P * i - META + P], y[:, i % 2]).then_inc(s, 16)
                else:
                    sp.dma_start(yp[SEQ - TAIL:SEQ], y[0:TAIL, i % 2]).then_inc(s, 16)
                    sp.dma_start(ys, y[TAIL:LAST, i % 2]).then_inc(s, 16)
            for s, n in ((lru_out, 4), (m_out, 2), (cp_out, 4), (n_out, 2), (f_out[0], 6), (f_out[1], 6),
                         (y_out[0], 4), (y_out[1], 2)):
                sp.wait_ge(s, 16 * n)

        @block.gpsimd
        def _(pool):
            st = Chain(pool, pool_step)
            pool.memset(stage[:, 0, 0:D], 0.0).then_inc(gate_zero, 1)
            st.link(pool.memset(ident[:, :], 0.0))
            st.link(pool.memset(sel[:, :, :], 0.0))
            st.link(pool.memset(mask[:, :, :], 0.0))
            st.link(pool.memset(misc[:, :], 1.0))
            st.wait()
            st.link(pool.memset(eps, EPS))
            pool.memset(ones[:, :], 1.0).then_inc(const_done, 1)
            pool.wait_ge(const_done, 1)
            st.link(pool.affine_select(out=ident[:, :], in_=ident[:, :], compare_op=ALU.not_equal, fill=1.0, base=0,
                                  pattern=[[-1, P]], channel_multiplier=1))
            for g in range(4):
                rr = slice(32 * g, 32 * g + HEADS)
                st.link(pool.affine_select(out=sel[rr, :, :], in_=sel[rr, :, :], compare_op=ALU.not_equal, fill=1.0,
                                      base=0, pattern=[[-1, HEADS], [0, P]], channel_multiplier=1))
            st.link(pool.affine_select(out=mask[:, :, :], in_=mask[:, :, :], compare_op=ALU.is_ge, fill=NEG, base=0,
                                  pattern=[[0, 2], [1, P]], channel_multiplier=-1))
            st.wait()
            for b in range(NB):
                c0 = TAIL + LS * b
                m = mask[:, 1, c0:c0 + LS]
                st.link(pool.affine_select(out=m, in_=m, compare_op=ALU.is_ge, fill=NEG, base=-c0,
                                      pattern=[[0, LS]], channel_multiplier=1))
            st.wait()
            pool.memset(bd[:, :, :], 0.0).then_inc(bd_zero, 1)
            pool.wait_ge(bd_zero, 1)
            st.wait()
            pool.memset(misc[:, 200:201], 0.0).then_inc(const_done, 1)

            def lo(b, slot, n):
                pool.wait_ge(w_hi, b + 1)
                pool.tensor_tensor(wlo[:, slot, 0:n], stage[:, slot, 0:n], whi[:, slot, 0:n].bitcast(F32),
                                   ALU.subtract).then_inc(w_lo, 1)

            def los(b0, n, size):
                with pool.Fori(0, n // 2) as i:
                    for j in range(2):
                        lo(b0 + 2 * i + j, (b0 + j) % 2, size)

            lo(0, 0, D)
            los(1, B_FFN - 1, D)
            for h in range(2):
                b0 = B_FFN + B_HALF * h
                los(b0, 2 * HK, D)
                los(b0 + 2 * HK, 8, HK * P)

        @block.scalar
        def _(act):
            st = Chain(act, act_step)

            def aview(ap):
                return ap.rearrange("(r c) -> r c", c=P)

            for rtile, r0, src in (
                    (0, 0, aview(a["norm1_g"][0])), (0, 8, aview(a["norm2_g"][0])),
                    (0, 16, aview(b_in[0:5 * D])), (0, 56, aview(b_in[COL_GA:COL_GA + 2 * D])),
                    (0, 72, a["lru_conv_w"][0].rearrange("j (f c) -> (j f) c", c=P)),
                    (0, 104, aview(a["lru_conv_b"][0])), (0, 112, aview(a["lru_b_r"][0])),
                    (0, 120, aview(a["lru_b_i"][0])), (1, 0, aview(a["lru_lambda"][0])),
                    (1, 8, aview(a["mlstm_head_g"][0])),
                    (1, 16, a["state_lru_h"][0].rearrange("b (f c) -> (b f) c", c=P)),
                    (2, 0, a["state_mlstm_n"][0].rearrange("b h (i c) -> (b h i) c", c=P)),
                    (2, 64, aview(a["ffn_conv_b"][0])),
                    (3, 0, a["ffn_conv_w"][0, 0:2].rearrange("j (f c) -> (j f) c", c=P)),
                    (4, 0, aview(a["ffn_conv_w"][0, 2])),
                    (5, 0, a["state_lru_conv"][0, 0:4].rearrange("b j (f c) -> (b j f) c", c=P)),
                    (6, 0, a["state_lru_conv"][0, 4:8].rearrange("b j (f c) -> (b j f) c", c=P)),
                    *((7 + b, 0, a["state_ffn_conv"][0, b].rearrange("j (f c) -> (j f) c", c=P)) for b in range(NB))):
                act.dma_start(rows[r0:r0 + src.shape[0], rtile], src).then_inc(rows_in, 16)
            act.wait_ge(const_done, 2)
            act.dma_start(gbias[:, 0:1], b_in[COL_I:COL_F].rearrange("(h o) -> h o", o=1)).then_inc(gate_rows_in, 16)
            act.dma_start(gbias[:, 1:2], b_in[COL_F:COL_GA].rearrange("(h o) -> h o", o=1)).then_inc(gate_rows_in, 16)
            with nc.allow_non_contiguous_dma(reason="32 single values"):
                act.dma_start(mst, a["state_mlstm_m"][0].rearrange("b h -> h b")).then_inc(gate_rows_in, 16)

            def hi(b, slot, n, t, loaded):
                act.wait_ge(w_loaded[slot], loaded)
                if t is not None:
                    act.wait_ge(tile_done, t)
                act.activation(whi[:, slot, 0:n], stage[:, slot, 0:n], ACT.Copy).then_inc(w_hi, 1)

            def loads_of(b):
                return 16 * (b // 2 + 1) + 16 * (1 - b % 2)

            def past():
                act.wait_ge(const_done, 1)

            def evict(t, out, in_, func, **kw_):
                act.wait_ge(tile_evicted, t)
                act.wait_ge(tile_done, t + 1)
                if not isinstance(t, int):
                    past()
                act.activation(out, in_, func, **kw_).then_inc(tile_evicted, 1)

            act.wait_ge(const_done, 1)
            for i in range(TT):
                n = P if i < TT - 1 else LAST
                if i != 2 and i != 3:
                    act.wait_ge(x_in[min(i, 1) if i < 4 else 2], 32 if i in (0, 4) else 16)
                if i:
                    st.wait()
                st(act.activation(sq_tok[0:n, :], x_tok[0:n, i], ACT.Square, accum_out=ss[0:n, i:i + 1]))
                st.wait()
                act.activation(rms[0:n, i:i + 1], ss[0:n, i:i + 1], ACT.Sqrt, scale=1.0 / D,
                               bias=eps[0:n]).then_inc(rms_done, 1)
            for g in range(4):
                act.wait_ge(tile_done, T_COLS + g + 1)
                ms = range(4 * g, min(4 * g + 4, NROW))
                for m in ms:
                    ins = act.activation(cols[:, P * m:P * m + ROWS[m]],
                                         wide[g % 2][:, P * (m % 4):P * (m % 4) + ROWS[m]], ACT.Copy)
                    if m < ms[-1]:
                        st(ins)
                    else:
                        ins.then_inc(tile_evicted, 1)
            hi(0, 0, D, None, 32)
            for f in range(8):
                t = T_XN + f
                act.wait_ge(tile_done, t + 1)
                act.activation(xh[:, f], wide[t % 2][:, 0:T], ACT.Copy, scale=cols[:, C_N1 + f:C_N1 + f + 1]
                               ).then_inc(xn_hi, 1)
            hi(1, 1, D, None, 16)
            act.wait_ge(lam_abs, 1)
            act.activation(lam[0], lam[0], ACT.Exp, scale=-1.0).then_inc(lam_exp, 1)
            t = T_GATE
            act.wait_ge(gate_rows_in, 48)
            act.wait_ge(tile_done, t + 1)
            st(act.activation(h2(gs[:, 0, :]), rt(t % 2, slice(0, HEADS)), ACT.Identity, bias=gbias[:, 0:1]))
            act.wait_ge(tile_evicted, t)
            act.activation(h2(gs[:, 1, :]), rt(t % 2, slice(32, 32 + HEADS)), ACT.Copy).then_inc(tile_evicted, 1)

            def lru_gates(p):
                act.wait_ge(lru_ps, p + 1)
                past()
                st(act.activation(h2(ri[:, 0]), bank[:, 0:2, 0:HALF], ACT.Sigmoid, bias=cols[:, ds(p + C_BR, 1)]))
                act.activation(h2(ri[:, 1]), bank[:, 2:4, 0:HALF], ACT.Sigmoid, bias=cols[:, ds(p + C_BI, 1)]
                               ).then_inc(lru_act, 1)
                st.wait()
                past()
                st(act.activation(th[:, :], ri[:, 0], ACT.Tanh, scale=negc[:, ds(p, 1)]))
                act.activation(flat(u[:, ds(p, 1), 0:T]), ri[:, 0], ACT.Exp, scale=negc[:, ds(p, 1)]
                               ).then_inc(lru_act, 1)

            def lru_root(p):
                act.wait_ge(lru_q, p + 1)
                act.activation(th[:, :], th[:, :], ACT.Sqrt, scale=-1.0).then_inc(lru_sq, 1)

            def lru_split(p):
                act.wait_ge(lru_h, p + 1)
                past()
                act.activation(flat(hh[:, ds(p, 1), :]), flat(uc[:, ds(p, 1), :]), ACT.Copy).then_inc(lru_hi, 1)

            def with_lru(b0, t0, i, p, dst, func, c0, split=True):
                for j in range(2):
                    b, t, f = b0 + 2 * i + j, t0 + 2 * i + j, 2 * i + j
                    hi(b + 1, (b0 + j + 1) % 2, D, t, 16 * i + loads_of(b0 + j + 1))
                    if j == 0 and split:
                        lru_split(p - 1)
                    if j == 1:
                        lru_gates(p)
                        lru_root(p)
                    evict(t, h2o(dst(f)), rt((t0 + j) % 2), func, bias=cols[:, ds(f + c0, 1)])

            act.wait_ge(negc_ready, 1)
            u_of = lambda f: u[:, ds(f, 1), LW - 1:UW]
            with_lru(B_U, T_U, 0, 0, u_of, ACT.Identity, C_BIN, False)
            st.loop(1, 4, 2, lambda i: with_lru(B_U, T_U, i, i, u_of, ACT.Identity, C_BIN))
            st.loop(0, 4, 2, lambda i: with_lru(B_GA, T_GA, i, i + 4, lambda f: merged[:, ds(f, 1), :],
                                                ACT.Sigmoid, C_BGA))
            lru_split(7)
            evict(T_LC, conv_out[:, :], wide[T_LC % 2][0:27, :], ACT.Copy)
            evict(T_LC + 1, h_out[:, :], wide[(T_LC + 1) % 2][0:72, 0:P], ACT.Copy)
            with act.Fori(0, 4) as i:
                for j in range(2):
                    b, t = B_WA + 2 * i + j, T_WA + 2 * i + j
                    hi(b + 1, (B_WA + j + 1) % 2, D, t, 16 * i + loads_of(B_WA + j + 1))

            def project(n, t):
                b = B_HEAD + n
                hi(b + 1, (b + 1) % 2, D, t, loads_of(b + 1))
                h, part, j = n // 8, n % 8 // 2, n % 2
                s = h % 2
                if n >= 8 * HEADS:
                    jj = n - 8 * HEADS
                    evict(t, h2(gbs[:, jj]), rt(t % 2), ACT.Sigmoid, bias=cols[:, C_BGB + jj:C_BGB + jj + 1])
                    return
                dst = (q[s], k[s], vf, so[s])[part]
                bias = cols[:, C_BIN + 8 * (part + 1) + 2 * h + j:][:, 0:1]
                if n % 8 == 0 and h >= 2:
                    act.wait_ge(head_done, h - 1)
                if part == 0:
                    evict(t, h2(dst[:, j]), rt(t % 2), ACT.Identity, scale=1.0 / 16, bias=qb[:, 2 * h + j:2 * h + j + 1])
                else:
                    evict(t, h2(dst[:, j]), rt(t % 2), ACT.Sigmoid if part == 3 else ACT.Identity, bias=bias)

            act.wait_ge(lru_out, 64)
            for n in range(8):
                project(n, T_HEAD0 + n)
                if n == 0:
                    act.wait_ge(gate_abs, 1)
                    act.activation(gs[:, 2, :], gs[:, 2, :], ACT.Exp, scale=-1.0).then_inc(gate_exp, 1)
            for h in range(HEADS):
                s, t0 = h % 2, T_HEAD + HT * h
                if h:
                    act.wait_ge(head_done, h)
                evict(t0, h2(ebc[:, :]), rt(t0 % 2), ACT.Exp)
                evict(t0 + 1, h2(gbc[:, :]), rt((t0 + 1) % 2), ACT.Exp, scale=-1.0)
                for m in range(3):
                    t = t0 + 2 + m
                    w2 = wide[t % 2].rearrange("p (c w d) -> p c w d", w=2, d=DH)
                    act.wait_ge(tile_done, t + 1)
                    if m < 2:
                        st(act.activation(kt[s][:, 2 * m:2 * m + 2], w2[:, :, 0], ACT.Copy))
                        act.wait_ge(tile_evicted, t)
                        act.activation(vt[s][:, 2 * m:2 * m + 2], w2[:, :, 1], ACT.Copy).then_inc(tile_evicted, 1)
                    else:
                        st(act.activation(kt[s][0:LAST, 4], w2[0:LAST, 0, 0], ACT.Copy))
                        act.wait_ge(tile_evicted, t)
                        act.activation(vt[s][0:LAST, 4], w2[0:LAST, 0, 1], ACT.Copy).then_inc(tile_evicted, 1)
                for c in range(TT):
                    n, L = 5 * h + c, P if c < 4 else LAST
                    act.wait_ge(arg_done, n + 1)
                    if n >= 2:
                        act.wait_ge(y_done, n - 1)
                        act.wait_ge(kw_done, 13 * ((n - 2) // 5) + (13 if (n - 2) % 5 == 4 else (n - 2) % 5 + 1))
                    act.activation(wt[0:L, n % 2, 0:L], argm[0:L, 0:L], ACT.Exp).then_inc(w_done, 1)
                    project(8 * (h + 1) + c, t0 + 5 + c)
                project(8 * (h + 1) + 5, t0 + 10)
                act.wait_ge(hn_done, h + 1)
                act.activation(hsq[:, :, :], hb[:, 2 * h:2 * h + 2, :], ACT.Square).then_inc(hsq_done, 1)
                for m in (6, 7):
                    project(8 * (h + 1) + m, t0 + 5 + m)
                act.wait_ge(hsq_done, h + 1)
                evict(t0 + 13, h2(hsq[:, 0]), rt((t0 + 13) % 2), ACT.Sqrt, scale=1.0 / DH, bias=eps)
            evict(T_NOUT, n_rows[:, :], wide[T_NOUT % 2][0:72, 0:P], ACT.Copy)
            act.wait_ge(head_done, HEADS)
            for f in range(8):
                act.activation(xh[:, f], hb[:, f], ACT.Copy).then_inc(hb_hi, 1)

            def wb_pair(i):
                for j in range(2):
                    b, t, f = B_WB + 2 * i + j, T_WB + 4 * i + 2 * j, 2 * i + j
                    hi(b + 1, (B_WB + j + 1) % 2, D, t, 16 * i + loads_of(B_WB + j + 1))
                    act.wait_ge(m_done, f + 1)
                    past()
                    act.activation(flat(mh[:, ds(f, 1), :]), flat(merged[:, ds(f, 1), :]), ACT.Copy).then_inc(m_hi, 1)
                    evict(t + 1, flat(resid[:, ds(f, 1), :]), wide[(T_WB + 1) % 2][:, 0:T], ACT.Copy)
            with act.Fori(0, 4) as i:
                wb_pair(i)

            act.wait_ge(m_lo, 8)

            def out_pair(i):
                for j in range(2):
                    b, t, f = B_OUT + 2 * i + j, T_OUT + 2 * i + j, 2 * i + j
                    hi(b + 1, (B_OUT + j + 1) % 2, D, t, 16 * i + loads_of(B_OUT + j + 1))
                    act.wait_ge(tile_evicted, t + 1)
                    past()
                    act.activation(flat(xh[:, ds(f, 1), :]), flat(resid[:, ds(f, 1), :]), ACT.Copy,
                                   scale=cols[:, ds(f + C_N2, 1)]).then_inc(x2_hi, 1)
                    act.activation(xsq[:, j], flat(resid[:, ds(f, 1), :]), ACT.Square).then_inc(xsq_done, 1)
            with act.Fori(0, 4) as i:
                out_pair(i)
            act.wait_ge(ssum_part, 8)
            act.activation(h2(rbc[:, :]), bank[:, 0:2, 0:HALF], ACT.Sqrt, scale=1.0 / D, bias=eps).then_inc(frms, 1)

            for h in range(2):
                b0, t0 = B_FFN + B_HALF * h, T_FFN + B_HALF * h

                def activate(i):
                    g = HK * h + i
                    act.wait_ge(gate_conv, g + 1)
                    act.activation(cv[:, 1], cv[:, 1], ACT.Gelu_apprx_tanh).then_inc(gelu_done, 1)
                    act.wait_ge(prod_done, g + 1)
                    if not isinstance(i, int):
                        past()
                    act.activation(flat(gh[:, ds(i, 1), :]), cv[:, 0], ACT.Copy).then_inc(g_hi, 1)

                def up_pair(i, first=False, last=False):
                    for j in range(2):
                        b, t = b0 + 2 * i + j, t0 + 2 * i + j
                        n = HK * P if last and j else D
                        hi(b + 1, (b0 + j + 1) % 2, n, t, 16 * i + loads_of(b0 + j + 1))
                        if j == 0 and not first:
                            activate(i - 1)
                up_pair(0, first=True)
                with act.Fori(1, HK - 1) as i:
                    up_pair(i)
                up_pair(HK - 1, last=True)
                b1, t1 = b0 + 2 * HK, t0 + 2 * HK
                hi(b1 + 1, (b1 + 1) % 2, HK * P, t1, loads_of(b1 + 1))
                activate(HK - 1)
                with act.Fori(0, 3) as i:
                    for j in range(2):
                        hi(b1 + 2 * i + j + 2, (b1 + j) % 2, HK * P, t1 + 2 * i + j + 1,
                           16 * i + 16 + loads_of(b1 + j))
                if h == 0:
                    hi(b1 + 8, (b1 + 8) % 2, D, t1 + 7, loads_of(b1 + 8))
            for n in range(6):
                w_ = min(D, 2 * FF - D * n)
                if n >= 2:
                    act.wait_ge(f_out[n % 2], 32 * (n // 2))
                evict(T_FC + n, fout[:, n % 2, 0:w_], wide[(T_FC + n) % 2][0:18, 0:w_], ACT.Copy)
            for i in range(TT):
                n, t = P if i < TT - 1 else LAST, T_FIN + i
                act.wait_ge(tile_done, t + 1)
                if i:
                    st.wait()
                st(act.activation(fsq[0:n, :], wide[t % 2][0:n, :], ACT.Square,
                                  accum_out=ssf[0:n, i:i + 1]))
                st.wait()
                act.activation(rmsf[0:n, i:i + 1], ssf[0:n, i:i + 1], ACT.Sqrt, scale=1.0 / D, bias=eps[0:n]
                               ).then_inc(fin_rms, 1)

        @block.vector
        def _(dve):
            st = Chain(dve, dve_step)
            stt, ts, tt, cpy = dve.scalar_tensor_tensor, dve.tensor_scalar, dve.tensor_tensor, dve.tensor_copy

            def mul_add(out, in0, scalar, in1, op0=ALU.mult, op1=ALU.add):
                return stt(out=out, in0=in0, scalar=scalar, in1=in1, op0=op0, op1=op1)

            for i in range(TT):
                n = P if i < TT - 1 else LAST
                dve.wait_ge(rms_done, i + 1)
                st.link(dve.reciprocal(rms[0:n, i:i + 1], rms[0:n, i:i + 1]))
                ts(x_tok[0:n, i], x_tok[0:n, i], rms[0:n, i:i + 1], None, ALU.mult).then_inc(x_scaled, 1)
            dve.wait_ge(tile_evicted, T_XN)
            for f in range(8):
                dve.wait_ge(xn_hi, f + 1)
                mul_add(xl[:, f], wide[(T_XN + f) % 2][:, 0:T], cols[:, C_N1 + f:C_N1 + f + 1], xh[:, f].bitcast(F32),
                        ALU.mult, ALU.subtract).then_inc(tile_evicted, 1)
            st(ts(qb, cols[:, C_BIN + 8:C_BIN + 16], 1.0 / 16, None, ALU.mult))
            st(dve.memset(u[:, :, 0:LW - 1], 0.0))
            st(cpy(nst[:, 1:NS, :], cols[:, C_NS:C_NS + 64].rearrange("p (b n) -> p b n", n=8)))

            def log1p_exp(y, z, z2, p):
                st.link(ts(z, y, 2.0, None, ALU.add))
                st.link(dve.reciprocal(z2, z))
                st.link(tt(z, y, z2, ALU.mult))
                st.link(tt(z2, z, z, ALU.mult))
                st.link(ts(p, z2, 1.0 / (2 * LSE_TERMS + 1), None, ALU.mult))
                for m in range(LSE_TERMS - 1, 0, -1):
                    st.link(mul_add(p, p, 1.0 / (2 * m + 1), z2, ALU.add, ALU.mult))
                st.link(mul_add(p, p, 1.0, z, ALU.add, ALU.mult))
                st.link(ts(z, p, 2.0, None, ALU.mult))

            L_ = cols[:, C_LAM:C_LAM + 8]
            mul_add(lam[0], L_, -1.0, L_, ALU.mult, ALU.max).then_inc(lam_abs, 1)
            dve.wait_ge(lam_exp, 1)
            log1p_exp(*lam[0:4])
            st.link(ts(lam[4], L_, -1.0, 0.0, ALU.mult, ALU.max))
            st.link(tt(lam[4], lam[4], lam[1], ALU.add))
            ts(negc, lam[4], -LRU_C, None, ALU.mult).then_inc(negc_ready, 1)

            def conv(f, j):
                if True:
                    dve.wait_ge(tile_evicted, T_U + 1 + f)
                    uf, cf = u[:, ds(f, 1), :], uc[:, ds(f, 1), :]
                    w = [cols[:, ds(f + (C_CW + 8 * m), 1)] for m in range(LW)]
                    us = usamp[:, j]
                    for g in range(2):
                        hist = cols[:, C_LC[g]:C_LC[g] + 96].rearrange("p (b l f) -> p b l f", l=LW - 1, f=8)
                        st(cpy(us[:, 4 * g:4 * g + 4, 0:LW - 1],
                               hist[:, :, :, ds(f, 1)].rearrange("p b l o -> p b (l o)")))
                    st(cpy(us[:, :, LW - 1:], flat(uf)[:, LW - 1 + TP:UW].rearrange("p (b l) -> p b l", l=LS)))
                    ul = flat(ulast[:, ds(f, 1), :])
                    st(cpy(ul[:, 0:3], flat(uf)[:, TP:TP + 3]))
                    st(cpy(ul[:, 3:27].rearrange("p (b l) -> p b l", l=3),
                           flat(uf)[:, LW - 1 + TP:UW].rearrange("p (b l) -> p b l", l=LS)[:, :, LS - 3:]))
                    cP = flat(cf)[:, 0:TP]
                    cS = flat(cf)[:, TP:T].rearrange("p (b l) -> p b l", l=LS)
                    st(ts(cP, flat(uf)[:, 0:TP], w[0], cols[:, ds(f + C_CB, 1)], ALU.mult, ALU.add))
                    st.wait()
                    st(ts(cS, us[:, :, 0:LS], w[0], cols[:, ds(f + C_CB, 1)], ALU.mult, ALU.add))
                    for m in range(1, LW):
                        st(mul_add(cP, flat(uf)[:, m:m + TP], w[m], cP))
                        st.wait()
                        ins = mul_add(cS, us[:, :, m:m + LS], w[m], cS)
                        if m < LW - 1:
                            st(ins)
                        else:
                            ins.then_inc(conv_done, 1)

            sam = slice(TP, T)

            def first(ap):
                return ap[:, sam].rearrange("p (b l) -> p b l", l=LS)[:, :, 0]

            def lru_tile(p):
                return flat(u[:, ds(p, 1), 0:T]), flat(uc[:, ds(p, 1), :])

            def lru_square(p):
                a_, x = lru_tile(p)
                dve.wait_ge(lru_act, 2 * p + 1)
                st(tt(ri[:, 1], ri[:, 1], x, ALU.mult))
                dve.wait_ge(lru_act, 2 * p + 2)
                st(tt(ri[:, 0], a_, a_, ALU.mult))
                st.wait()
                mul_add(th[:, :], ri[:, 0], 1.0, th[:, :], ALU.add, ALU.mult).then_inc(lru_q, 1)

            def lru_scan(p):
                a_, x = lru_tile(p)
                r_, i_ = ri[:, 0], ri[:, 1]
                dve.wait_ge(lru_sq, p + 1)
                st(tt(i_, i_, th[:, :], ALU.mult))
                h0 = cols[:, C_H0:C_H0 + 64].rearrange("p (b f) -> p b f", f=8)[:, :, ds(p, 1)].rearrange(
                    "p b o -> p (b o)")
                st(tt(r_[:, 0:NB], first(a_), h0, ALU.mult))
                st.wait()
                st(tt(first(i_), first(i_), r_[:, 0:NB], ALU.add))
                st(ts(first(a_), first(a_), 0.0, None, ALU.mult))
                st.wait()
                dve.tensor_tensor_scan(out=x, data0=a_, data1=i_, initial=0.0, op0=ALU.mult, op1=ALU.add
                                       ).then_inc(lru_h, 1)
                dve.wait_ge(lru_h, p + 1)
                st(cpy(hlast[:, :, ds(p, 1)].rearrange("p b o -> p (b o)"), flat(uc[:, ds(p, 1), TP - 1:T])[:, 0:65:LS]))

            def lru_lo(p):
                dve.wait_ge(lru_hi, p + 1)
                tt(flat(hl[:, ds(p, 1), :]), flat(uc[:, ds(p, 1), :]), flat(hh[:, ds(p, 1), :]).bitcast(F32),
                   ALU.subtract).then_inc(lru_lo_, 1)

            def u_pair(i, before=True):
                conv(2 * i, 0)
                if before:
                    lru_lo(i - 1)
                lru_square(i)
                conv(2 * i + 1, 1)
                lru_scan(i)

            def ga_pair(i):
                lru_lo(i + 3)
                lru_square(i + 4)
                lru_scan(i + 4)
            st.wait()
            u_pair(0, False)
            st.loop(1, 4, 2 * 12 + 2 + 5, u_pair)
            st.loop(0, 4, 2 + 5, ga_pair)
            lru_lo(7)

            dve.wait_ge(tile_evicted, T_WA)
            with dve.Fori(0, 4) as i:
                for j in range(2):
                    f = 2 * i + j
                    dve.wait_ge(tile_done, T_WA + f + 1)
                    m_ = merged[:, ds(f, 1), :]
                    tt(h2o(m_), rt((T_WA + j) % 2), h2o(m_), ALU.mult).then_inc(tile_evicted, 1)

            ig, f_, yy, s3, s4, s5 = (gs[:, m, :] for m in range(6))
            st.link(ts(f_, f_, gbias[:, 1:2], None, ALU.add))
            mul_add(yy, f_, -1.0, f_, ALU.mult, ALU.max).then_inc(gate_abs, 1)
            dve.wait_ge(gate_exp, 1)
            log1p_exp(yy, s3, s4, s5)
            st.link(ts(yy, f_, 0.0, None, ALU.min))
            st.link(tt(f_, yy, s3, ALU.subtract))
            st.link(cpy(yy, f_))
            st.link(cpy(s3, ig))
            st.link(tt(first(s4), first(f_), mst, ALU.add))
            st.link(tt(first(s3), first(s4), first(ig), ALU.max))
            st.link(dve.memset(first(yy), NEG))
            M = s4
            st.link(dve.tensor_tensor_scan(out=M, data0=yy, data1=s3, initial=0.0, op0=ALU.add, op1=ALU.max))
            st.link(dve.memset(yy, 1.0))
            st.link(dve.memset(yy[:, 0:P * (TT - 1) + 1:P], 0.0))
            st.link(dve.memset(first(yy), 0.0))
            Bc = s3
            st.link(dve.tensor_tensor_scan(out=Bc, data0=yy, data1=f_, initial=0.0, op0=ALU.mult, op1=ALU.add))
            A = yy
            st.link(tt(A, Bc, M, ALU.subtract))
            st(cpy(gq[0:HEADS, :], A))
            st(tt(gq[32:32 + HEADS, :], ig, Bc, ALU.subtract))
            st(cpy(gq[96:96 + HEADS, :], M))
            st(cpy(gq[64:64 + HEADS, 0:P], A[:, 0:P]))
            for c in range(1, TT):
                e = P * c + (P if c < 4 else TAIL)
                st(ts(gq[64:64 + HEADS, P * c:e], A[:, P * c:e], M[:, P * c - 1:P * c], None, ALU.add))
            st(tt(gq[64:64 + HEADS, sam].rearrange("p (b l) -> p b l", l=LS),
                  A[:, sam].rearrange("p (b l) -> p b l", l=LS),
                  mst.rearrange("p (b o) -> p b o", o=1).to_broadcast([HEADS, NB, LS]), ALU.add))
            st(cpy(mout, M[:, TP - 1:T:LS]))
            st.wait()
            dve.memset(misc[:, 202:203], 0.0).then_inc(gates_ready, 1)

            for h in range(HEADS):
                s, t0 = h % 2, T_HEAD + HT * h
                dve.wait_ge(tile_evicted, t0 + 1)
                for j in range(2):
                    tt(qe[:, j], q[s][:, j], ebc[:, :], ALU.mult).then_inc(qe_done, 1)
                cpr = cp[s]
                if h >= 2:
                    dve.wait_ge(cp_out, 16 * (h - 1))
                for c in range(TT):
                    n, L, c0 = 5 * h + c, P if c < 4 else LAST, P * c
                    X = bx[n % 2]
                    w = wt[0:L, n % 2, 0:L]
                    dve.wait_ge(scores, n + 1)
                    if n:
                        dve.wait_ge(w_done, n)
                    tt(argm[0:L, 0:L], X[0:L, P:P + L], mask[0:L, c // 4, 0:L], ALU.add).then_inc(arg_done, 1)
                    dve.wait_ge(w_done, n + 1)
                    if n:
                        dve.wait_ge(y_done, n)
                    tt(pt[0:L, 0:L], w, X[0:L, 0:L], ALU.mult).then_inc(p_done, 1)
                    kap = 13 * h + c
                    nu = 1 if c < 4 else NS

                    def keys(m):
                        if kap + m >= 2:
                            dve.wait_ge(z_done, kap + m - 1)
                        col = L - 1 if c < 4 else TAIL - 1 + LS * m
                        ts(kw[0:L, (kap + m) % 2], kt[s][0:L, c], w[:, col:col + 1], None, ALU.mult
                           ).then_inc(kw_done, 1)

                    def update(m):
                        dve.wait_ge(z_done, kap + m + 1)
                        Z = bz if (m % 2 == 0) else bx[(n + 1) % 2]
                        if m == 0:
                            C = cpr[:, :, :].rearrange("p i v -> p (i v)")
                        else:
                            nb = NB * h + m - 1
                            C = cs[:, nb % 4].rearrange("p i v -> p (i v)")
                        if c == 0:
                            cpy(C, Z).then_inc(z_evicted, 1)
                            return
                        col = c0 + (L - 1 if c < 4 else TAIL - 1 + LS * m)
                        if kap + m:
                            dve.wait_ge(z_evicted, kap + m)
                        mul_add(C, C, ebc[:, col:col + 1], Z).then_inc(z_evicted, 1)

                    keys(0)
                    if nu > 1:
                        keys(1)
                        for m in range(nu):
                            update(m)
                            if m + 2 < nu:
                                keys(m + 2)
                    dve.wait_ge(y_done, n + 1)
                    st(cpy(hb[:, 2 * h:2 * h + 2, c0:c0 + L],
                           by[:, 0:256].rearrange("p (j t) -> p j t", j=2)[:, :, 0:L]))
                    st(cpy(den[:, c0:c0 + L], by[:, 256:256 + L]))
                    npr = nst[:, 0, 2 * h:2 * h + 2]
                    if c == 0:
                        cpy(npr, by[:, 384:386]).then_inc(y_evicted, 1)
                    elif c < 4:
                        dve.wait_ge(y_evicted, n)
                        mul_add(npr, npr, ebc[:, c0 + L - 1:c0 + L], by[:, 384:386]).then_inc(y_evicted, 1)
                    else:
                        dec = ebc[:, TP - 1:T:LS].rearrange("p (b o) -> p b o", o=1)
                        nall = nst[:, :, 2 * h:2 * h + 2]
                        dve.wait_ge(y_evicted, n)
                        st.link(tt(ntmp[:, :, :], nall, dec.to_broadcast([P, NS, 2]), ALU.mult))
                        tt(nall, ntmp[:, :, :], by[:, 384:384 + 2 * NS].rearrange("p (i b) -> p b i", b=NS),
                           ALU.add).then_inc(y_evicted, 1)
                    if nu == 1:
                        update(0)
                dve.wait_ge(tile_evicted, t0 + 2)
                st.wait()
                st.link(mul_add(qe[:, 0], den[:, :], -1.0, den[:, :], ALU.mult, ALU.max))
                st.link(tt(qe[:, 0], qe[:, 0], gbc[:, :], ALU.max))
                st.link(dve.reciprocal(den[:, :], qe[:, 0]))
                hv = hb[:, 2 * h:2 * h + 2, :]
                tt(hv, hv, den[:, :].rearrange("p (o t) -> p o t", o=1).to_broadcast([P, 2, T]), ALU.mult
                   ).then_inc(hn_done, 1)
                dve.wait_ge(tile_evicted, t0 + 14)
                st.link(dve.reciprocal(den[:, :], hsq[:, 0]))
                for j in range(2):
                    gcol = cols[:, C_HG + 2 * h + j:C_HG + 2 * h + j + 1]
                    st(mul_add(hb[:, 2 * h + j], hb[:, 2 * h + j], gcol, den[:, :], ALU.mult, ALU.mult))
                st.wait()
                tt(hv, hv, so[s][:, :, :], ALU.mult).then_inc(head_done, 1)

            for f in range(8):
                dve.wait_ge(hb_hi, f + 1)
                if f == 0:
                    dve.wait_ge(head_done, HEADS)
                tt(xl[:, f], hb[:, f], xh[:, f].bitcast(F32), ALU.subtract).then_inc(hb_lo, 1)

            def wb_pair(i):
                for j in range(2):
                    f, t = 2 * i + j, T_WB + 4 * i + 2 * j
                    g_, m_ = gbs[:, ds(f, 1), :], merged[:, ds(f, 1), :]
                    dve.wait_ge(tile_done, t + 1)
                    dve.wait_ge(tile_evicted, t)
                    tt(h2o(g_), rt(T_WB % 2), h2o(g_), ALU.mult).then_inc(tile_evicted, 1)
                    dve.wait_ge(tile_evicted, t + 1)
                    tt(flat(m_), flat(m_), flat(g_), ALU.add).then_inc(m_done, 1)
                    dve.wait_ge(m_hi, f + 1)
                    tt(flat(ml[:, ds(f, 1), :]), flat(m_), flat(mh[:, ds(f, 1), :]).bitcast(F32), ALU.subtract
                       ).then_inc(m_lo, 1)
            for n in range(4):
                dve.wait_ge(c_out[n], 16 * 8)
            with dve.Fori(0, 4) as i:
                wb_pair(i)

            dve.wait_ge(tile_evicted, T_OUT)

            def out_pair(i):
                for j in range(2):
                    f, t = 2 * i + j, T_OUT + 2 * i + j
                    r_ = resid[:, ds(f, 1), :]
                    dve.wait_ge(tile_done, t + 1)
                    tt(h2o(r_), rt((T_OUT + j) % 2), h2o(r_), ALU.add).then_inc(tile_evicted, 1)
                    dve.wait_ge(x2_hi, f + 1)
                    mul_add(flat(xl[:, ds(f, 1), :]), flat(r_), cols[:, ds(f + C_N2, 1)],
                            flat(xh[:, ds(f, 1), :]).bitcast(F32), ALU.mult, ALU.subtract).then_inc(x2_lo, 1)
            with dve.Fori(0, 4) as i:
                out_pair(i)
            dve.wait_ge(frms, 1)
            dve.reciprocal(rbc[:, :], rbc[:, :]).then_inc(rbc_done, 1)
            st(dve.memset(up[:, :, 0:FW - 1], 0.0))
            dve.wait_ge(rbc_done, 1)
            st.wait()

            for h in range(2):
                t0 = T_FFN + B_HALF * h

                def gated(i):
                    g = HK * h + i
                    st.wait()
                    dve.wait_ge(gelu_done, g + 1)
                    tt(cv[:, 0], cv[:, 0], cv[:, 1], ALU.mult).then_inc(prod_done, 1)
                    dve.wait_ge(g_hi, g + 1)
                    tt(flat(gl[:, ds(i, 1), :]), cv[:, 0], flat(gh[:, ds(i, 1), :]).bitcast(F32), ALU.subtract
                       ).then_inc(g_lo, 1)

                def up_pair(i, first=False):
                    if not first:
                        gated(i - 1)
                    for j in range(2):
                        t = t0 + 2 * i + j
                        ft = i + (HK * h + UPT // 2 * j)
                        U = up[:, j]
                        dve.wait_ge(tile_done, t + 1)
                        tt(h2(U[:, FW - 1:FP]), rt((t0 + j) % 2), h2(rbc[:, :]), ALU.mult).then_inc(tile_evicted, 1)
                        hist = cols[:, C_FC:C_FC + P * NB].rearrange("p (b c) -> p b c", c=P)
                        fs = fsamp[:, j]
                        for m in range(2):
                            st(cpy(fs[:, :, m:m + 1], hist[:, :, ds(ft + UPT * m, 1)]))
                        dve.wait_ge(tile_evicted, t + 1)
                        usm = U[:, FW - 1 + TP:FP].rearrange("p (b l) -> p b l", l=LS)
                        st(cpy(fs[:, :, FW - 1:], usm))
                        fl = flat(flast[:, ds(ft, 1), :])
                        st(cpy(fl[:, 0:2], U[:, TP:TP + 2]))
                        st(cpy(fl[:, 2:18].rearrange("p (b l) -> p b l", l=2), usm[:, :, LS - 2:]))
                        w = [cols[:, ds(ft + C_FCW[m], 1)] for m in range(FW)]
                        bias = cols[:, ds(ft + C_FCB, 1)]
                        cP = cv[:, j, 0:TP]
                        cS = cv[:, j, TP:T].rearrange("p (b l) -> p b l", l=LS)
                        st(ts(cP, U[:, 0:TP], w[0], bias, ALU.mult, ALU.add))
                        st.wait()
                        st(ts(cS, fs[:, :, 0:LS], w[0], bias, ALU.mult, ALU.add))
                        for m in range(1, FW):
                            st(mul_add(cP, U[:, m:m + TP], w[m], cP))
                            st.wait()
                            ins = mul_add(cS, fs[:, :, m:m + LS], w[m], cS)
                            if m == FW - 1 and j:
                                ins.then_inc(gate_conv, 1)
                            else:
                                st(ins)

                if h:
                    dve.wait_ge(tile_done, t0)
                up_pair(0, True)
                st.loop(1, HK, 2 * (5 + 2 + 4) - 1, up_pair)
                gated(HK - 1)
                t1 = t0 + 2 * HK
                with dve.Fori(0, 4) as i:
                    for j in range(2):
                        t = t1 + 2 * i + j
                        r_ = resid[:, ds(2 * i + j, 1), :]
                        dve.wait_ge(tile_done, t + 1)
                        tt(h2o(r_), rt((t1 + j) % 2), h2o(r_), ALU.add).then_inc(tile_evicted, 1)
            dve.wait_ge(fg_in, 16)
            for i in range(TT):
                n, t = P if i < TT - 1 else LAST, T_FIN + i
                dve.wait_ge(fin_rms, i + 1)
                st.link(dve.reciprocal(rmsf[0:n, i:i + 1], rmsf[0:n, i:i + 1]))
                if i >= 2:
                    dve.wait_ge(y_out[i % 2], 16 * (i // 2))
                mul_add(y[0:n, i % 2], wide[t % 2][0:n, :], rmsf[0:n, i:i + 1], fgb[0:n, :], ALU.mult, ALU.mult
                        ).then_inc(tile_evicted, 1)

        @block.tensor
        def _(pe):
            def begin(t):
                if not isinstance(t, int) or t >= 2:
                    pe.wait_ge(tile_evicted, t - 1)

            def split_product(out, slot, kn, xh_, xl_, wait_k=None):
                for kk in range(kn):
                    if wait_k:
                        wait_k(kk)
                    for m, (w, x) in enumerate(((whi, xh_), (whi, xl_), (wlo, xh_))):
                        for hf in range(2):
                            last = pe.matmul(out(hf), w[:, slot, kk * P:kk * P + P], x[:, kk, HALF * hf:HALF * hf + HALF],
                                             start=kk == 0 and m == 0, stop=kk == kn - 1 and m == 2)
                return last

            def gemm(b, t, bslot, tslot, kn, xh_, xl_, wait_k=None):
                pe.wait_ge(w_lo, b + 1)
                begin(t)
                split_product(lambda hf: ring[:, tslot, hf, 0:HALF], bslot, kn, xh_, xl_, wait_k).then_inc(tile_done, 1)

            pe.wait_ge(const_done, 2)
            pe.wait_ge(rows_in, 16 * 25)
            for g in range(4):
                t = T_COLS + g
                begin(t)
                for m in range(4 * g, min(4 * g + 4, NROW)):
                    last = pe.transpose(wide[t % 2][:, P * (m - 4 * g):P * (m - 4 * g) + ROWS[m]],
                                        rows[0:ROWS[m], m, :], ident[0:ROWS[m], 0:ROWS[m]])
                last.then_inc(tile_done, 1)
            pe.wait_ge(x_scaled, TT)

            def token_transposes(t, f, src):
                begin(t)
                for i in range(TT):
                    n = P if i < TT - 1 else LAST
                    last = pe.transpose(wide[t % 2][:, P * i:P * i + n], src[0:n, i, P * f:P * f + P], ident[0:n, 0:n])
                last.then_inc(tile_done, 1)

            for f in range(8):
                token_transposes(T_XN + f, f, x_tok)
            pe.wait_ge(tile_evicted, T_XN + 8)
            gemm(B_GATE, T_GATE, 0, T_GATE % 2, KT, xh, xl)

            def lru_gates(p):
                pe.wait_ge(conv_done, p + 1)
                pe.wait_ge(bd_in, 64 * (p + 1))
                if not isinstance(p, int):
                    pe.wait_ge(lru_act, 2 * p)
                for g in range(2):
                    for hf in range(2):
                        last = pe.matmul(bank[:, 2 * g + hf, 0:HALF], bd[:, g, :],
                                         flat(uc[:, ds(p, 1), HALF * hf:HALF * hf + HALF]), start=True, stop=True)
                last.then_inc(lru_ps, 1)

            def with_lru(b0, t0, i, p):
                for j in range(2):
                    gemm(b0 + 2 * i + j, t0 + 2 * i + j, (b0 + j) % 2, (t0 + j) % 2, KT, xh, xl)
                    if j == 0:
                        lru_gates(p)
            with_lru(B_U, T_U, 0, 0)
            with pe.Fori(1, 4) as i:
                with_lru(B_U, T_U, i, i)
            with pe.Fori(0, 4) as i:
                with_lru(B_GA, T_GA, i, i + 4)
            pe.wait_ge(lru_lo_, 8)
            t = T_LC
            begin(t)
            for f in range(8):
                last = pe.transpose(wide[t % 2][0:27, P * f:P * f + P], ulast[:, f, :], ident[:, :])
            last.then_inc(tile_done, 1)
            begin(t + 1)
            pe.transpose(wide[(t + 1) % 2][0:72, 0:P], stage[:, 0, D + 224:D + 224 + 72], ident[:, :]).then_inc(tile_done, 1)
            with pe.Fori(0, 4) as i:
                for j in range(2):
                    gemm(B_WA + 2 * i + j, T_WA + 2 * i + j, (B_WA + j) % 2, (T_WA + j) % 2, KT, hh, hl)
            for n in range(8):
                gemm(B_HEAD + n, T_HEAD0 + n, (B_HEAD + n) % 2, (T_HEAD0 + n) % 2, KT, xh, xl)

            def fill(h, n):
                b, t = B_HEAD + 8 * (h + 1) + n, T_HEAD + HT * h + 5 + n
                gemm(b, t, b % 2, t % 2, KT, xh, xl)

            pe.wait_ge(gates_ready, 1)
            for h in range(HEADS):
                s, t0 = h % 2, T_HEAD + HT * h
                for m, r0 in enumerate((64, 96)):
                    begin(t0 + m)
                    for hf in range(2):
                        last = pe.matmul(ring[:, (t0 + m) % 2, hf, 0:HALF], sel[r0:r0 + HEADS, h, :],
                                         gq[r0:r0 + HEADS, HALF * hf:HALF * hf + HALF], start=True, stop=True)
                    last.then_inc(tile_done, 1)
                for m in range(3):
                    t = t0 + 2 + m
                    begin(t)
                    for cc in range(2 if m < 2 else 1):
                        c = 2 * m + cc
                        L = P if c < 4 else LAST
                        for w_, src in enumerate((k[s], vf)):
                            for jj in range(2):
                                last = pe.transpose(wide[t % 2][0:L, 512 * cc + 256 * w_ + 128 * jj:][:, 0:P],
                                                    src[:, jj, P * c:P * c + L], ident[:, :])
                    last.then_inc(tile_done, 1)

                def score(c):
                    n, L, c0 = 5 * h + c, P if c < 4 else LAST, P * c
                    X = bx[n % 2]
                    if n >= 2:
                        pe.wait_ge(p_done, n - 1)
                    if h:
                        pe.wait_ge(z_evicted, 13 * h)
                    for jj in range(2):
                        pe.matmul(X[0:L, 0:L], k[s][:, jj, c0:c0 + L], q[s][:, jj, c0:c0 + L], start=jj == 0, stop=jj == 1)
                    pe.matmul(X[0:L, P:P + L], sel[0:HEADS, h, 0:L], gq[0:HEADS, c0:c0 + L], start=True, stop=False
                              ).then_inc(arg_part, 1)
                    pe.wait_ge(arg_part, n + 1)
                    pe.matmul(X[0:L, P:P + L], gq[32:32 + HEADS, c0:c0 + L], sel[32:32 + HEADS, h, 0:L],
                              start=False, stop=True).then_inc(scores, 1)

                def values(c):
                    n, L, c0 = 5 * h + c, P if c < 4 else LAST, P * c
                    kap = 13 * h + c
                    cpr = cp[s]
                    w = wt[0:L, n % 2]
                    pe.wait_ge(p_done, n + 1)
                    if n:
                        pe.wait_ge(y_evicted, n)
                    inter = c > 0
                    for jj in range(2):
                        pe.matmul(by[:, P * jj:P * jj + L], vt[s][0:L, c, P * jj:P * jj + P], pt[0:L, 0:L],
                                  start=jj == 0, stop=not inter, skip_group_check=True)
                    pe.matmul(by[:, 256:256 + L], ones[0:L, :], pt[0:L, 0:L], start=False, stop=not inter,
                              skip_group_check=True)
                    nu = 1 if c < 4 else NS
                    first_ = L - 1 if c < 4 else TAIL - 1
                    for jj in range(2):
                        last = pe.matmul(by[:, 384 + nu * jj:384 + nu * jj + nu], kt[s][0:L, c, P * jj:P * jj + P],
                                         w[:, first_:first_ + LS * (nu - 1) + 1:LS], start=False, stop=True,
                                         skip_group_check=True)

                    def across(cols_, C, ncol):
                        for jj in range(2):
                            for ii in range(2):
                                pe.matmul(by[:, P * jj + cols_.start:P * jj + cols_.stop], C[:, ii, P * jj:P * jj + P],
                                          qe[:, ii, c0 + cols_.start:c0 + cols_.stop], start=False, stop=ii == 1,
                                          skip_group_check=True)
                        for ii in range(2):
                            last = pe.matmul(by[:, 256 + cols_.start:256 + cols_.stop],
                                             ncol[:, ii:ii + 1].to_broadcast([P, P]),
                                             qe[:, ii, c0 + cols_.start:c0 + cols_.stop], start=False, stop=ii == 1,
                                             skip_group_check=True)
                        return last

                    def outer(m):
                        Z = bz if m % 2 == 0 else bx[(n + 1) % 2]
                        pe.wait_ge(kw_done, kap + m + 1)
                        if kap + m >= (2 if c == 4 else 1):
                            pe.wait_ge(z_evicted, kap + m - (1 if c == 4 and m > 1 else 0))
                        for ii in range(2):
                            lz = pe.matmul(Z[:, 256 * ii:256 * ii + 256], kw[0:L, (kap + m) % 2, P * ii:P * ii + P],
                                           vt[s][0:L, c, :], start=True, stop=True)
                        lz.then_inc(z_done, 1)

                    if inter:
                        pe.wait_ge(qe_done, 2 * h + 2)
                        pe.wait_ge(z_evicted, kap)
                        last = across(slice(0, L if c < 4 else TAIL), cpr, nst[:, 0, 2 * h:2 * h + 2])
                    if c < 4:
                        last.then_inc(y_done, 1)
                        outer(0)
                        return
                    outer(0)
                    for b in range(NB):
                        nb = NB * h + b
                        if b == 4:
                            fill(h, 5)
                        pe.wait_ge(c_in[nb % 4], 16 * (nb // 4 + 1))
                        last = across(slice(TAIL + LS * b, TAIL + LS * b + LS), cs[:, nb % 4],
                                      nst[:, 1 + b, 2 * h:2 * h + 2])
                        if b == NB - 1:
                            last.then_inc(y_done, 1)
                        outer(1 + b)

                score(0)
                fill(h, 0)
                for c in range(TT):
                    values(c)
                    if c < 4:
                        score(c + 1)
                        fill(h, c + 1)
                fill(h, 6)
                fill(h, 7)
                t = t0 + 13
                pe.wait_ge(hsq_done, h + 1)
                begin(t)
                for hf in range(2):
                    for jj in range(2):
                        last = pe.matmul(ring[:, t % 2, hf, 0:HALF], ones[:, :], hsq[:, jj, HALF * hf:HALF * hf + HALF],
                                         start=jj == 0, stop=jj == 1)
                last.then_inc(tile_done, 1)
            t = T_NOUT
            pe.wait_ge(y_evicted, 5 * HEADS)
            begin(t)
            pe.transpose(wide[t % 2][0:72, 0:P], nst[:, :, :].rearrange("p b n -> p (b n)"), ident[:, :]
                         ).then_inc(tile_done, 1)
            pe.wait_ge(hb_lo, 8)
            for f in range(8):
                t = T_WB + 2 * f
                gemm(B_WB + f, t, (B_WB + f) % 2, t % 2, KT, xh, xl)
                if f == 0:
                    pe.wait_ge(x2_in, 80)
                token_transposes(t + 1, f, x_tok2)
            pe.wait_ge(m_lo, 8)

            def sum_squares(f):
                pe.wait_ge(xsq_done, f + 1)
                for hf in range(2):
                    last = pe.matmul(bank[:, hf, 0:HALF], ones[:, :], xsq[:, f % 2, HALF * hf:HALF * hf + HALF],
                                     start=f == 0, stop=f == 7)
                last.then_inc(ssum_part, 1)

            for f in range(8):
                gemm(B_OUT + f, T_OUT + f, (B_OUT + f) % 2, (T_OUT + f) % 2, KT, mh, ml)
                if f:
                    sum_squares(f - 1)
            sum_squares(7)
            pe.wait_ge(x2_lo, 8)
            for h in range(2):
                b0, t0 = B_FFN + B_HALF * h, T_FFN + B_HALF * h
                with pe.Fori(0, HK) as i:
                    for j in range(2):
                        gemm(b0 + 2 * i + j, t0 + 2 * i + j, (b0 + j) % 2, (t0 + j) % 2, KT, xh, xl)
                b1, t1 = b0 + 2 * HK, t0 + 2 * HK

                def arrived(kk):
                    pe.wait_ge(g_lo, HK * h + kk + 1)
                for m in range(8):
                    gemm(b1 + m, t1 + m, (b1 + m) % 2, (t1 + m) % 2, HK, gh, gl, arrived if m == 0 else None)
            for n in range(6):
                t = T_FC + n
                begin(t)
                for m in range(8 * n, min(8 * n + 8, UPT)):
                    last = pe.transpose(wide[t % 2][0:18, P * (m - 8 * n):P * (m - 8 * n) + P], flast[:, m, :], ident[:, :])
                last.then_inc(tile_done, 1)
            pe.wait_ge(tile_evicted, T_FC)
            for i in range(TT):
                n, t = P if i < TT - 1 else LAST, T_FIN + i
                begin(t)
                for f in range(8):
                    last = pe.transpose(wide[t % 2][0:n, P * f:P * f + P], resid[:, f, P * i:P * i + n], ident[:, :])
                last.then_inc(tile_done, 1)


_INS = ["x_prompt", "x_sample", "state_lru_conv", "state_lru_h", "state_mlstm_C", "state_mlstm_n",
        "state_mlstm_m", "state_ffn_conv", "meta_tokens", "norm1_g", "w_in", "b_in", "lru_conv_w", "lru_conv_b",
        "lru_w_r", "lru_b_r", "lru_w_i", "lru_b_i", "lru_lambda", "mlstm_head_g", "w_branch_a", "w_branch_b",
        "w_out", "norm2_g", "w_up", "ffn_conv_w", "ffn_conv_b", "w_down", "final_g"]
_OUTS = [("y_prompt", (1, SEQ, D)), ("y_sample", (NB, LS, D)),
         ("p_lru_conv", (1, 1, 3, D)), ("p_lru_h", (1, 1, D)), ("p_mlstm_C", (1, 1, HEADS, DH, DH)),
         ("p_mlstm_n", (1, 1, HEADS, DH)), ("p_mlstm_m", (1, 1, HEADS)), ("p_ffn_conv", (1, 1, 2, 2 * FF)),
         ("s_lru_conv", (1, NB, 3, D)), ("s_lru_h", (1, NB, D)), ("s_mlstm_C", (1, NB, HEADS, DH, DH)),
         ("s_mlstm_n", (1, NB, HEADS, DH)), ("s_mlstm_m", (1, NB, HEADS)), ("s_ffn_conv", (1, NB, 2, 2 * FF))]


def kernel(**inputs):
    import concourse.bacc as bacc
    from concourse.bass_utils import run_bass_kernel_spmd

    nc = bacc.Bacc("TRN2", target_bir_lowering=False, num_devices=1)
    arrays, a, o = {}, {}, {}
    for name in _INS:
        x = np.ascontiguousarray(inputs[name])
        arrays[f"in_{name}"] = x
        a[name] = nc.dram_tensor(f"in_{name}", x.shape, mybir.dt.from_np(x.dtype), kind="ExternalInput").ap()
    for name, shape in _OUTS:
        o[name] = nc.dram_tensor(f"out_{name}", shape, F32, kind="ExternalOutput").ap()
    hybrid_layer(nc, a, o)
    r = run_bass_kernel_spmd(nc, [arrays], core_ids=[0])
    return tuple(r.results[0][f"out_{name}"] for name, _ in _OUTS)
```

```python
import numpy as np
import concourse.bass as bass
from concourse import mybir
from contextlib import ExitStack

F32 = mybir.dt.float32
F32R = mybir.dt.float32r
ALU = mybir.AluOpType
ACT = mybir.ActivationFunctionType
ds = bass.ds

D = 1024
P = 128
KT = D // P
SEQ, META = 512, 16
TP = SEQ + META
NB, LS = 8, 8
T = TP + NB * LS
HALF = T // 2
TT = -(-T // P)
LAST = T - (TT - 1) * P
TAIL = LAST - NB * LS
NS = NB + 1
HEADS, DH = 4, 256
LW, FW = 4, 3
FF = 2816
UPT = 2 * FF // P
HK = FF // P // 2
BW = 64
EPS = 1e-6
LRU_C = 8.0
LSE_TERMS = 8
NEG = -1.0e30
D_MAX = 1.0e22
COL_I = D + 4 * D
COL_F = COL_I + HEADS
COL_GA = COL_F + HEADS
COL_GB = COL_GA + D

C_N1, C_N2, C_BIN, C_BGA, C_BGB, C_CW, C_CB, C_BR, C_BI = 0, 8, 16, 56, 64, 72, 104, 112, 120
C_LAM, C_HG, C_H0 = 128, 136, 144
C_NS, C_FCB = 256, 320
C_FCW = (384, 384 + UPT, 512)
C_LC = (640, 768)
C_FC = 896
NROW = 15
COL_GROUPS = ((0, 2), (2, 9), (9, NROW))
ROWS = [128, 80, 108, 88, 44, 96, 96] + [88] * 8

B_GATE, B_U, B_GA, B_WA, B_HEAD = 0, 1, 9, 17, 25
B_GB = B_HEAD + 8 * HEADS
B_WB = B_GB + 8
B_OUT = B_WB + 8
B_FFN = B_OUT + 8
B_HALF = 2 * HK + 8
B_END = B_FFN + 2 * B_HALF
T_COLS = 0
T_XN = 1
T_GATE = T_XN + 8
T_COLS2 = T_GATE + 1
T_U = T_COLS2 + 2
T_GA = T_U + 8
T_WA = T_GA + 8
T_LC = T_WA + 2
T_HEAD0 = T_WA + 10
T_PRE0 = T_HEAD0 + 8
T_HEAD = T_PRE0 + 5
HT = 14
T_NOUT = T_HEAD + HT * HEADS - 5
T_WB = T_NOUT + 1
T_OUT = T_WB + 8
T_FFN = T_OUT + 8
T_FIN = T_FFN + 2 * B_HALF
FC = -(-UPT // KT)

TB = 4 * T
SLOT = 4 * HK * P


class Chain:

    def __init__(self, eng, sem):
        self.eng, self.sem, self.base, self.n = eng, sem, 0, 0

    def __call__(self, ins):
        ins.then_inc(self.sem, 1)
        self.n += 1
        return ins

    def wait(self):
        self.eng.wait_ge(self.sem, self.base + self.n)

    def link(self, ins):
        self(ins)
        self.wait()

    def loop(self, first, last, per, body):
        start = self.n
        with self.eng.Fori(first, last) as i:
            self.base = start + per * (i - first)
            self.n = 0
            body(i)
            assert self.n == per, (self.n, per)
        self.base, self.n = 0, start + per * (last - first)


def flat(ap):
    return ap.rearrange("p o t -> p (o t)")


def hybrid_layer(nc, a, o):
    w_in, b_in = a["w_in"][0], a["b_in"][0]
    ctx = ExitStack()
    with ctx:
        base = 16512

        def sb(name, shape, off, dt=F32):
            return nc.alloc_sbuf_tensor_at(name, shape, dt, offset=base + off)

        def sem(name):
            return ctx.enter_context(nc.semaphore(name))

        o_a = 6 * SLOT
        o_c = o_a + 16 * TB
        o_b = o_c + 8 * TB
        o_h = o_b + 8 * TB
        o_p = o_h + 85568
        stage = sb("stage", [P, 2, HK * P], 0)
        whi = sb("whi", [P, 2, HK * P], 2 * SLOT, F32R)
        wlo = sb("wlo", [P, 2, HK * P], 4 * SLOT, F32R)
        ulast = stage[:, 0, D:D + 8 * 27].rearrange("p (f n) -> p f n", n=27)
        hlast = stage[:, 0, D + 224:D + 224 + 72].rearrange("p (b f) -> p b f", f=8)
        usamp = [sb(f"u_samp{j}", [P, 4, NB, LW - 1 + LS], SLOT * (1 + j) + 4 * D) for j in range(2)]
        xh = sb("xh", [P, 8, T], o_a, F32R)
        xl = sb("xl", [P, 8, T], o_a + 8 * TB, F32R)
        merged = sb("merged", [P, 8, T], o_c)
        hb = sb("hb", [P, 8, T], o_b)
        gs = sb("gate_scratch", [HEADS, 6, T], o_b)
        th = sb("lru_tanh", [P, T], o_b + 6 * TB)
        sq_tok = sb("sq_tok", [P, D], o_b)
        conv_out = sb("conv_out", [27, D], o_h)
        h_out = sb("h_out", [72, P], o_h + 4096)
        resid = sb("resid", [P, 8, T], o_b)
        x_tok = sb("x_tok", [P, TT, D], o_h)
        rows = sb("rows", [P, NROW, P], o_h + 20480)
        UW = LW - 1 + T
        u = sb("u", [P, 8, UW], o_h)
        uc = sb("uc", [P, 8, T], o_h + 32 * UW)
        hh = sb("hh", [P, 8, T], o_h + 32 * UW + 8 * TB, F32R)
        hl = sb("hl", [P, 8, T], o_h + 32 * UW + 16 * TB, F32R)
        ri = sb("ri", [P, 2, T], o_h + 32 * UW + 24 * TB)
        SB = 6 * TB + 10240

        def head_slot(name, shape, off):
            return [sb(f"{name}{s}", shape, o_h + SB * s + off) for s in range(2)]

        q = head_slot("q", [P, 2, T], 0)
        k = head_slot("k", [P, 2, T], 2 * TB)
        so = head_slot("sig_o", [P, 2, T], 4 * TB)
        kt = head_slot("k_tok", [P, TT, DH], 6 * TB)
        vt = head_slot("v_tok", [P, TT, DH], 6 * TB + 5120)
        r = o_h + 2 * SB
        vf = sb("v_feat", [P, 2, T], r)
        qe = sb("q_e", [P, 2, T], r + 2 * TB)
        cs = sb("c_sample", [P, 4, 2, DH], r + 4 * TB)
        r += 4 * TB + 8192
        cp0 = sb("c_prompt0", [P, 2, DH], r)
        ebcs = [sb(f"e_int{s}", [P, T], r + 2048 + s * TB) for s in range(2)]
        gbcs = [sb(f"guard{s}", [P, T], r + 2048 + (2 + s) * TB) for s in range(2)]
        den = sb("den", [P, T], r + 2048 + 4 * TB)
        hsq = sb("h_sq", [P, 2, T], r + 2048 + 5 * TB)
        end = [SLOT * n + 4 * D for n in range(6)]
        wt = sb("w_t", [P, 2, P], end[0])
        argm = sb("arg", [P, P], end[0] + 1024)
        pt = sb("p_t", [P, P], end[1])
        qn = sb("q_n", [P, 2, NB * LS], end[1] + 512)
        n_rows = sb("n_rows", [72, P], end[1] + 1024)
        kw = [sb(f"k_w{s}", [P, DH], end[2 + s]) for s in range(2)]
        ntmp = sb("n_tmp", [P, NS, 2], end[4])
        gbs = sb("sig_gb", [P, 8, T], o_h)
        mh = sb("mh", [P, 8, T], o_h + SB, F32R)
        ml = sb("ml", [P, 8, T], o_h + SB + 8 * TB, F32R)
        x_tok2 = sb("x_tok2", [P, TT, D], o_h + SB + 16 * TB)
        xsq = sb("x_sq", [P, 2, T], o_c)
        rbc = sb("rstd", [P, T], o_c + 2 * TB)
        fout = sb("f_out", [18, 2, D], o_c + 3 * TB)
        gh = sb("gh", [P, HK, T], o_h, F32R)
        gl = sb("gl", [P, HK, T], o_h + HK * TB, F32R)
        r = o_h + 2 * HK * TB
        FP = FW - 1 + T
        up = sb("up", [P, 2, FP], r)
        cv = sb("conv", [P, 2, T], r + 4768)
        r += 4768 + 2 * TB
        fsamp = sb("f_samp", [P, 2, NB, FW - 1 + LS], r)
        flast = sb("f_last", [P, UPT, 18], r + 640)
        fgb = sb("final_g_b", [P, D], r + 640 + 72 * UPT)
        y = sb("y", [P, TT, D], o_h)
        fsq = sb("fin_sq", [P, D], o_h + 4 * TT * D)
        cols = sb("cols", [P, NROW * P], o_p)
        r = o_p + 512 * NROW
        ident = sb("ident", [P, P], r)
        ones = sb("ones", [P, P], r + 512)
        mask = sb("mask", [P, 2, P], r + 1024)
        sel = sb("sel", [P, HEADS, P], r + 2048)
        gq = sb("gate_rows", [P, T], r + 4096)
        r += 4096 + TB
        nst = sb("n_state", [P, NS, 8], r)
        misc = sb("misc", [P, 256], r + 288)
        bd = sb("lru_gate_w", [P, 2, P], r + 1312)
        cp = [cp0, sb("c_prompt1", [P, 2, DH], r + 1312)]
        ss, rms, eps, one = misc[:, 0:5], misc[:, 8:13], misc[:, 16:17], misc[:, 17:18]
        qb, negc = misc[:, 24:32], misc[:, 32:40]
        lam = [misc[:, 40 + 8 * n:48 + 8 * n] for n in range(6)]
        ssf, rmsf = misc[:, 96:101], misc[:, 104:109]
        gbias = misc[0:HEADS, 112:114]
        mst = misc[0:HEADS, 120:128]
        mout = misc[0:HEADS, 128:137]

        ring = ctx.enter_context(nc.psum_tensor("ring", [P, 2, 2, 512], F32))
        bank = ctx.enter_context(nc.psum_tensor("bank", [P, 4, 512], F32))
        wide = [ring[:, s].rearrange("p h t -> p (h t)") for s in range(2)]
        bx = [bank[:, 0], bank[:, 1]]
        by = bank[:, 2]
        bz = bank[:, 3]

        def rt(s, rows_=slice(0, P)):
            return ring[rows_, s, :, 0:HALF]

        def bank2(s):
            return bank[:, 2 * s:2 * s + 2].rearrange("p h t -> p (h t)")

        final = [*wide, bank2(0), bank2(1)]

        def h2(ap):
            return ap.rearrange("p (h t) -> p h t", h=2)

        def h2o(ap):
            return ap.rearrange("p o (h t) -> p (o h) t", h=2)

        w_loaded = [sem("w_loaded0"), sem("w_loaded1")]
        w_hi, w_lo = sem("w_hi"), sem("w_lo")
        tile_done, tile_evicted = sem("tile_done"), sem("tile_evicted")
        x_in = [sem(f"x_in{i}") for i in range(TT)]
        rows_in = [sem("rows_in0"), sem("rows_in1")]
        gate_rows_in, x2_in = sem("gate_in"), sem("x2_in")
        const_done, gate_zero, x_scaled, xn_hi = (
            sem("const_done"), sem("gate_zero"), sem("x_scaled"), sem("xn_hi"))
        rms_done = sem("rms_done")
        lam_abs, lam_exp, gate_abs, gate_exp, gates_ready = (
            sem("lam_abs"), sem("lam_exp"), sem("gate_abs"), sem("gate_exp"), sem("gates_ready"))
        bd_in, negc_ready = sem("bd_in"), sem("negc_ready")
        bd_zero, conv_done, lru_ps, lru_act, lru_q, lru_sq, lru_h, lru_hi, lru_lo_ = (
            sem("bd_zero"), sem("conv_done"), sem("lru_ps"), sem("lru_act"), sem("lru_q"),
            sem("lru_sq"), sem("lru_h"), sem("lru_hi"), sem("lru_lo"))
        c_in = [sem(f"c_in{n}") for n in range(4)]
        c_out = [sem(f"c_out{n}") for n in range(4)]
        cp_out = sem("cp_out")
        arg_part = sem("arg_part")
        scores, arg_done, w_done, p_done = sem("scores"), sem("arg_done"), sem("w_done"), sem("p_done")
        qe_done, kw_done, y_done, y_evicted, z_done, z_evicted = (
            sem("qe_done"), sem("kw_done"), sem("y_done"), sem("y_evicted"), sem("z_done"),
            sem("z_evicted"))
        guard_used, hsq_done, var_done, root_done, head_done = (
            sem("guard_used"), sem("hsq_done"), sem("var_done"), sem("root_done"), sem("head_done"))
        hsum_done = sem("hsum_done")
        res_done, res_evicted, fc_done, fc_evicted = (
            sem("res_done"), sem("res_evicted"), sem("fc_done"), sem("fc_evicted"))
        hb_hi, hb_lo, m_done, m_hi, m_lo = (
            sem("hb_hi"), sem("hb_lo"), sem("m_done"), sem("m_hi"), sem("m_lo"))
        sq_sum = sem("sq_sum")
        xsq_done, ssum_done, x2_hi, x2_lo, frms, rbc_done = (
            sem("xsq_done"), sem("ssum_done"), sem("x2_hi"), sem("x2_lo"),
            sem("frms"), sem("rbc_done"))
        gate_conv, gelu_done, prod_done, g_hi, g_lo = (
            sem("gate_conv"), sem("gelu_done"), sem("prod_done"), sem("g_hi"), sem("g_lo"))
        fin_rms = sem("fin_rms")
        fg_in = sem("fg_in")
        y_out = sem("y_out")
        lru_out, n_out, m_out, f_out = sem("lru_out"), sem("n_out"), sem("m_out"), [sem("f_out0"), sem("f_out1")]
        act_step, dve_step, pool_step = sem("act_step"), sem("dve_step"), sem("pool_step")

        def prelude_tile(h):
            return T_HEAD + HT * (h - 1) + 7 if h else T_PRE0

        def fill_tile(h, n):
            return T_HEAD + HT * h + (n if n < 7 or h + 1 == HEADS else 12)

        def norm_tile(h):
            return T_HEAD + HT * h + (8 if h + 1 == HEADS else 13)

        block = ctx.enter_context(nc.Block())

        @block.sync
        def _(sp):
            def kview(w, kt_):
                return w.rearrange("(k p) m -> p k m", p=P)

            def load(b, slot, src, c0, k0=0, kn=KT):
                sp.dma_start(stage[:, slot, 0:kn * P].rearrange("p (k m) -> p k m", m=P),
                             src.rearrange("(k p) m -> p k m", p=P)[:, k0:k0 + kn, c0]
                             ).then_inc(w_loaded[slot], 16)

            def stream(b0, src, c0):
                def pair(i):
                    for j in range(2):
                        b = b0 + 2 * i + j
                        sp.wait_ge(w_lo, b - 1)
                        load(b, (b0 + j) % 2, src, ds(c0 + 256 * i + 128 * j, P))
                with sp.Fori(0, 4) as i:
                    pair(i)

            xp, xs, meta = a["x_prompt"][0], a["x_sample"].rearrange("b l d -> (b l) d"), a["meta_tokens"]

            def load_x(dst, sems):
                sp.dma_start(dst[0:META, 0], meta).then_inc(sems[0], 16)
                sp.dma_start(dst[META:P, 0], xp[0:P - META]).then_inc(sems[0], 16)
                for i in range(1, TT - 1):
                    sp.dma_start(dst[:, i], xp[P * i - META:P * i - META + P]).then_inc(sems[i], 16)
                sp.dma_start(dst[0:TAIL, TT - 1], xp[SEQ - TAIL:SEQ]).then_inc(sems[TT - 1], 16)
                sp.dma_start(dst[TAIL:LAST, TT - 1], xs).then_inc(sems[TT - 1], 16)

            load_x(x_tok, x_in)

            def aview(ap):
                return ap.rearrange("(r c) -> r c", c=P)

            def params(arrived, group):
                for rtile, r0, src in group:
                    sp.dma_start(rows[r0:r0 + src.shape[0], rtile], src).then_inc(arrived, 16)

            params(rows_in[0], ((0, 0, aview(a["norm1_g"][0])), (0, 8, aview(a["norm2_g"][0])),
                    (0, 16, aview(b_in[0:5 * D])), (0, 56, aview(b_in[COL_GA:COL_GA + 2 * D])),
                    (0, 72, a["lru_conv_w"][0].rearrange("j (f c) -> (j f) c", c=P)),
                    (0, 104, aview(a["lru_conv_b"][0])), (0, 112, aview(a["lru_b_r"][0])),
                    (0, 120, aview(a["lru_b_i"][0])), (1, 0, aview(a["lru_lambda"][0])),
                    (1, 8, aview(a["mlstm_head_g"][0])),
                    (1, 16, a["state_lru_h"][0].rearrange("b (f c) -> (b f) c", c=P))))
            sp.wait_ge(gate_zero, 1)
            g0 = stage[:, 0, 0:D].rearrange("p (k m) -> p k m", m=P)
            for c0, at in ((COL_I, 0), (COL_F, 32)):
                sp.dma_start(g0[:, :, at:at + HEADS],
                             w_in.rearrange("(k p) m -> p k m", p=P)[:, :, c0:c0 + HEADS]
                             ).then_inc(w_loaded[0], 16)
            load(1, 1, w_in, slice(0, P))
            params(rows_in[1], ((2, 0, a["state_mlstm_n"][0].rearrange("b h (i c) -> (b h i) c", c=P)),
                    (2, 64, aview(a["ffn_conv_b"][0])),
                    (3, 0, a["ffn_conv_w"][0, 0:2].rearrange("j (f c) -> (j f) c", c=P)),
                    (4, 0, aview(a["ffn_conv_w"][0, 2])),
                    (5, 0, a["state_lru_conv"][0, 0:4].rearrange("b j (f c) -> (b j f) c", c=P)),
                    (6, 0, a["state_lru_conv"][0, 4:8].rearrange("b j (f c) -> (b j f) c", c=P))))
            sp.dma_start(rows[0:2 * UPT, 7:7 + NB],
                         a["state_ffn_conv"][0].rearrange("b j (f c) -> (j f) b c", c=P)).then_inc(rows_in[1], 16)
            sp.wait_ge(const_done, 2)
            sp.dma_start(gbias[:, 0:1], b_in[COL_I:COL_F].rearrange("(h o) -> h o", o=1)).then_inc(gate_rows_in, 16)
            sp.dma_start(gbias[:, 1:2], b_in[COL_F:COL_GA].rearrange("(h o) -> h o", o=1)).then_inc(gate_rows_in, 16)
            with nc.allow_non_contiguous_dma(reason="32 single values"):
                sp.dma_start(mst, a["state_mlstm_m"][0].rearrange("b h -> h b")).then_inc(gate_rows_in, 16)
            sp.wait_ge(w_lo, 1)
            load(2, 0, w_in, slice(P, 2 * P))

            def lru_load(p):
                for g, w in enumerate((a["lru_w_r"][0], a["lru_w_i"][0])):
                    for hf in range(2):
                        sp.dma_start(bd[BW * hf:BW * hf + BW, g, BW * hf:BW * hf + BW],
                                     w[ds(2 * p + hf, 1)].rearrange("o c d -> (o c) d")).then_inc(bd_in, 16)

            sp.wait_ge(bd_zero, 1)
            lru_load(0)

            def with_lru(b0, c0, i, p):
                for j in range(2):
                    b = b0 + 2 * i + j
                    sp.wait_ge(w_lo, b - 1)
                    load(b, (b0 + j) % 2, w_in, ds(c0 + 256 * i + 128 * j, P))
                    if j == 0:
                        sp.wait_ge(lru_ps, p)
                        lru_load(p)
            with sp.Fori(1, 4) as i:
                with_lru(B_U, 0, i, i)
            with sp.Fori(0, 4) as i:
                with_lru(B_GA, COL_GA, i, i + 4)
            stream(B_WA, a["w_branch_a"][0], 0)
            sp.wait_ge(tile_evicted, T_LC + 2)
            sp.dma_start(o["p_lru_conv"][0, 0], conv_out[0:3, :]).then_inc(lru_out, 16)
            sp.dma_start(o["s_lru_conv"][0].rearrange("b j c -> (b j) c"), conv_out[3:27, :]).then_inc(lru_out, 16)
            sp.dma_start(o["p_lru_h"].rearrange("l b (f c) -> (l b f) c", c=P), h_out[0:8, :]).then_inc(lru_out, 16)
            sp.dma_start(o["s_lru_h"].rearrange("l b (f c) -> (l b f) c", c=P), h_out[8:72, :]).then_inc(lru_out, 16)

            def head_load(n):
                b = B_HEAD + n
                if n < 8 * HEADS:
                    h, part, j = n // 8, n % 8 // 2, n % 2
                    c0 = D * (1 + part) + DH * h + P * j
                else:
                    c0 = COL_GB + P * (n - 8 * HEADS)
                sp.wait_ge(w_lo, b - 1)
                load(b, b % 2, w_in, slice(c0, c0 + P))

            def c_load(n):
                if n >= 4:
                    sp.wait_ge(c_out[n % 4], 16 * (n // 4))
                sp.dma_start(cs[:, n % 4], a["state_mlstm_C"][0, n % NB, n // NB].rearrange("(i p) v -> p i v", p=P)
                             ).then_inc(c_in[n % 4], 16)

            def c_store(n):
                sp.wait_ge(z_evicted, 13 * (n // NB) + 5 + n % NB + 1)
                sp.dma_start(o["s_mlstm_C"][0, n % NB, n // NB].rearrange("(i p) v -> p i v", p=P), cs[:, n % 4]
                             ).then_inc(c_out[n % 4], 16)

            for n in range(10):
                head_load(n)
            sp.wait_ge(gates_ready, 1)
            sp.dma_start(o["p_mlstm_m"][0].rearrange("b h -> h b"), mout[:, 0:1]).then_inc(m_out, 16)
            with nc.allow_non_contiguous_dma(reason="32 single values"):
                sp.dma_start(o["s_mlstm_m"][0].rearrange("b h -> h b"), mout[:, 1:NS]).then_inc(m_out, 16)
            sp.wait_ge(tile_done, T_HEAD0)
            for n in range(4):
                c_load(n)
            wb = a["w_branch_b"][0]

            def next_load(h, j):
                if h + 1 < HEADS:
                    head_load(8 * (h + 2) + j)
                else:
                    sp.wait_ge(w_lo, B_WB + j - 1)
                    load(B_WB + j, (B_WB + j) % 2, wb, slice(P * j, P * j + P))

            for h in range(HEADS):
                for n in range(2, 8):
                    head_load(8 * (h + 1) + n)
                s0 = NB * h
                c_store(s0)
                for n in range(1, 4):
                    c_store(s0 + n)
                    c_load(s0 + 3 + n)
                next_load(h, 0)
                sp.dma_start(o["p_mlstm_C"][0, 0, h].rearrange("(i p) v -> p i v", p=P), cp[h % 2][:, :, :]
                             ).then_inc(cp_out, 16)
                c_store(s0 + 4)
                c_load(s0 + 7)
                for n in range(5, 8):
                    c_store(s0 + n)
                    if h + 1 < HEADS:
                        c_load(s0 + 3 + n)
                next_load(h, 1)
                if h + 1 < HEADS:
                    c_load(s0 + 11)
            sp.wait_ge(head_done, HEADS)
            sp.wait_ge(cp_out, 16 * HEADS)
            for n in range(4):
                sp.wait_ge(c_out[n], 16 * 8)
            sp.wait_ge(tile_evicted, T_NOUT + 1)
            load_x(x_tok2, [x2_in] * TT)
            sp.dma_start(o["p_mlstm_n"].rearrange("l b h (i p) -> (l b h i) p", p=P), n_rows[0:8, :]).then_inc(n_out, 16)
            sp.dma_start(o["s_mlstm_n"].rearrange("l b h (i p) -> (l b h i) p", p=P), n_rows[8:72, :]).then_inc(n_out, 16)
            with sp.Fori(1, 4) as i:
                for j in range(2):
                    b = B_WB + 2 * i + j
                    sp.wait_ge(w_lo, b - 1)
                    load(b, (B_WB + j) % 2, wb, ds(256 * i + 128 * j, P))
            stream(B_OUT, a["w_out"][0], 0)
            for h in range(2):
                b0 = B_FFN + B_HALF * h
                with sp.Fori(0, HK) as i:
                    for j in range(2):
                        b = b0 + 2 * i + j
                        sp.wait_ge(w_lo, b - 1)
                        load(b, (b0 + j) % 2, a["w_up"][0], ds(FF * j + P * (HK * h) + P * i, P))
                if h == 0:
                    sp.wait_ge(tile_evicted, T_OUT + 8)
                    sp.dma_start(fgb[:, :], a["final_g"].rearrange("(o d) -> o d", o=1).to_broadcast([P, D])
                                 ).then_inc(fg_in, 16)
                    sp.wait_ge(n_out, 32)
                b1 = b0 + 2 * HK

                def down(i, j):
                    b = b1 + 2 * i + j
                    sp.wait_ge(w_lo, b - 1)
                    load(b, (b1 + j) % 2, a["w_down"][0], ds(256 * i + 128 * j, P), HK * h, HK)

                def fc_store(n):
                    sp.wait_ge(fc_evicted, n + 1)
                    w_ = min(D, 2 * FF - D * n)
                    sp.dma_start(o["p_ffn_conv"][0, 0, :, D * n:D * n + w_], fout[0:2, n % 2, 0:w_]
                                 ).then_inc(f_out[n % 2], 16)
                    sp.dma_start(o["s_ffn_conv"][0].rearrange("b j c -> (b j) c")[:, D * n:D * n + w_],
                                 fout[2:18, n % 2, 0:w_]).then_inc(f_out[n % 2], 16)
                if h == 0:
                    with sp.Fori(0, 4) as i:
                        for j in range(2):
                            down(i, j)
                else:
                    for m in range(8):
                        down(m // 2, m % 2)
                        if m >= 4:
                            fc_store(m - 4)
                    for n in range(4, FC):
                        fc_store(n)
            yp, ys = o["y_prompt"][0], o["y_sample"].rearrange("b l d -> (b l) d")
            for i in range(TT):
                sp.wait_ge(tile_evicted, T_FIN + i + 1)
                if i == 0:
                    sp.dma_start(yp[0:P - META], y[META:P, 0]).then_inc(y_out, 16)
                elif i < TT - 1:
                    sp.dma_start(yp[P * i - META:P * i - META + P], y[:, i]).then_inc(y_out, 16)
                else:
                    sp.dma_start(yp[SEQ - TAIL:SEQ], y[0:TAIL, i]).then_inc(y_out, 16)
                    sp.dma_start(ys, y[TAIL:LAST, i]).then_inc(y_out, 16)
            for s, n in ((lru_out, 4), (m_out, 2), (cp_out, 4), (n_out, 2), (f_out[0], 6), (f_out[1], 6),
                         (y_out, 6)):
                sp.wait_ge(s, 16 * n)

        @block.gpsimd
        def _(pool):
            st = Chain(pool, pool_step)
            pool.memset(stage[:, 0, 0:D], 0.0).then_inc(gate_zero, 1)
            st.link(pool.memset(ident[:, :], 0.0))
            st.link(pool.memset(sel[:, :, :], 0.0))
            st.link(pool.memset(mask[:, :, :], 0.0))
            st.link(pool.memset(misc[:, :], 1.0))
            st.wait()
            st.link(pool.memset(eps, EPS))
            pool.memset(ones[:, :], 1.0).then_inc(const_done, 1)
            pool.wait_ge(const_done, 1)
            st.link(pool.affine_select(out=ident[:, :], in_=ident[:, :], compare_op=ALU.not_equal, fill=1.0, base=0,
                                  pattern=[[-1, P]], channel_multiplier=1))
            for g in range(4):
                rr = slice(32 * g, 32 * g + HEADS)
                st.link(pool.affine_select(out=sel[rr, :, :], in_=sel[rr, :, :], compare_op=ALU.not_equal, fill=1.0,
                                      base=0, pattern=[[-1, HEADS], [0, P]], channel_multiplier=1))
            st.link(pool.affine_select(out=mask[:, :, :], in_=mask[:, :, :], compare_op=ALU.is_ge, fill=NEG, base=0,
                                  pattern=[[0, 2], [1, P]], channel_multiplier=-1))
            st.wait()
            for b in range(NB):
                c0 = TAIL + LS * b
                m = mask[:, 1, c0:c0 + LS]
                st.link(pool.affine_select(out=m, in_=m, compare_op=ALU.is_ge, fill=NEG, base=-c0,
                                      pattern=[[0, LS]], channel_multiplier=1))
            st.wait()
            pool.memset(bd[:, :, :], 0.0).then_inc(bd_zero, 1)
            pool.wait_ge(bd_zero, 1)
            st.wait()
            pool.memset(misc[:, 200:201], 0.0).then_inc(const_done, 1)

            def lo(b, slot, n):
                pool.wait_ge(w_hi, b + 1)
                pool.tensor_tensor(wlo[:, slot, 0:n], stage[:, slot, 0:n], whi[:, slot, 0:n].bitcast(F32),
                                   ALU.subtract).then_inc(w_lo, 1)

            def los(b0, n, size):
                with pool.Fori(0, n // 2) as i:
                    for j in range(2):
                        lo(b0 + 2 * i + j, (b0 + j) % 2, size)

            lo(0, 0, D)
            los(1, B_FFN - 1, D)
            for h in range(2):
                b0 = B_FFN + B_HALF * h
                los(b0, 2 * HK, D)
                los(b0 + 2 * HK, 8, HK * P)

        @block.scalar
        def _(act):
            st = Chain(act, act_step)

            def hi(b, slot, n, t, loaded):
                act.wait_ge(w_loaded[slot], loaded)
                if t is not None:
                    act.wait_ge(tile_done, t)
                act.activation(whi[:, slot, 0:n], stage[:, slot, 0:n], ACT.Copy).then_inc(w_hi, 1)

            def loads_of(b):
                return 16 * (b // 2 + 1) + 16 * (1 - b % 2)

            def past():
                act.wait_ge(const_done, 1)

            def evict(t, out, in_, func, **kw_):
                act.wait_ge(tile_evicted, t)
                act.wait_ge(tile_done, t + 1)
                if not isinstance(t, int):
                    past()
                act.activation(out, in_, func, **kw_).then_inc(tile_evicted, 1)

            act.wait_ge(const_done, 1)
            for i in range(TT):
                n = P if i < TT - 1 else LAST
                act.wait_ge(x_in[i], 32 if i in (0, TT - 1) else 16)
                if i:
                    st.wait()
                st(act.activation(sq_tok[0:n, :], x_tok[0:n, i], ACT.Square, accum_out=ss[0:n, i:i + 1]))
                st.wait()
                act.activation(rms[0:n, i:i + 1], ss[0:n, i:i + 1], ACT.Sqrt, scale=1.0 / D,
                               bias=eps[0:n]).then_inc(rms_done, 1)
            hi(0, 0, D, None, 32)
            hi(1, 1, D, None, 16)

            def columns(t, m0, m1):
                act.wait_ge(tile_done, t + 1)
                for m in range(m0, m1):
                    ins = act.activation(cols[:, P * m:P * m + ROWS[m]],
                                         wide[t % 2][:, P * (m - m0):P * (m - m0) + ROWS[m]], ACT.Copy)
                    if m < m1 - 1:
                        st(ins)
                    else:
                        ins.then_inc(tile_evicted, 1)
            columns(T_COLS, *COL_GROUPS[0])
            st.wait()
            act.wait_ge(tile_evicted, T_XN)
            for f in range(8):
                t = T_XN + f
                act.wait_ge(tile_done, t + 1)
                act.activation(xh[:, f], wide[t % 2][:, 0:T], ACT.Copy, scale=cols[:, C_N1 + f:C_N1 + f + 1]
                               ).then_inc(xn_hi, 1)
            act.wait_ge(lam_abs, 1)
            act.activation(lam[0], lam[0], ACT.Exp, scale=-1.0).then_inc(lam_exp, 1)
            t = T_GATE
            act.wait_ge(gate_rows_in, 48)
            act.wait_ge(tile_done, t + 1)
            st(act.activation(h2(gs[:, 0, :]), bank[0:HEADS, 0:2, 0:HALF], ACT.Identity, bias=gbias[:, 0:1]))
            act.wait_ge(tile_evicted, t)
            act.activation(h2(gs[:, 1, :]), bank[32:32 + HEADS, 0:2, 0:HALF], ACT.Copy).then_inc(tile_evicted, 1)

            def lru_gates(p):
                if not isinstance(p, int):
                    act.wait_ge(lru_h, p)
                act.wait_ge(lru_ps, p + 1)
                past()
                st(act.activation(h2(ri[:, 0]), bank[:, 0:2, 0:HALF], ACT.Sigmoid, bias=cols[:, ds(p + C_BR, 1)]))
                act.activation(h2(ri[:, 1]), bank[:, 2:4, 0:HALF], ACT.Sigmoid, bias=cols[:, ds(p + C_BI, 1)]
                               ).then_inc(lru_act, 1)
                st.wait()
                past()
                st(act.activation(th[:, :], ri[:, 0], ACT.Tanh, scale=negc[:, ds(p, 1)]))
                act.activation(flat(u[:, ds(p, 1), 0:T]), ri[:, 0], ACT.Exp, scale=negc[:, ds(p, 1)]
                               ).then_inc(lru_act, 1)

            def lru_root(p):
                act.wait_ge(lru_q, p + 1)
                act.activation(th[:, :], th[:, :], ACT.Sqrt, scale=-1.0).then_inc(lru_sq, 1)

            def lru_split(p):
                act.wait_ge(lru_h, p + 1)
                past()
                act.activation(flat(hh[:, ds(p, 1), :]), flat(uc[:, ds(p, 1), :]), ACT.Copy).then_inc(lru_hi, 1)

            def u_pair(i, first=False):
                for j in range(2):
                    t, f = T_U + 2 * i + j, 2 * i + j
                    hi(B_U + f + 1, (B_U + j + 1) % 2, D, t, 16 * i + loads_of(B_U + j + 1))
                    if not first:
                        if j == 0:
                            lru_root(i - 1)
                        else:
                            lru_split(i - 1)
                            lru_gates(i)
                    evict(t, h2o(u[:, ds(f, 1), LW - 1:UW]), rt((T_U + j) % 2), ACT.Identity,
                          bias=cols[:, ds(f + C_BIN, 1)])
                if first:
                    lru_gates(i)

            def ga_pair(i):
                for j in range(2):
                    t, f = T_GA + 2 * i + j, 2 * i + j
                    hi(B_GA + f + 1, (B_GA + j + 1) % 2, D, t, 16 * i + loads_of(B_GA + j + 1))
                    if j == 0:
                        lru_root(i + 3)
                    else:
                        lru_split(i + 3)
                        lru_gates(i + 4)
                    evict(t, h2o(merged[:, ds(f, 1), :]), rt((T_GA + j) % 2), ACT.Sigmoid,
                          bias=cols[:, ds(f + C_BGA, 1)])

            for n in range(2):
                act.wait_ge(tile_evicted, T_COLS2 + n)
                columns(T_COLS2 + n, *COL_GROUPS[1 + n])
            act.wait_ge(negc_ready, 1)
            u_pair(0, True)
            st.loop(1, 4, 2, u_pair)
            st.loop(0, 4, 2, ga_pair)
            lru_root(7)

            def wa_pair(i, t0):
                for j in range(2):
                    hi(B_WA + 2 * i + j + 1, (B_WA + j + 1) % 2, D, t0 + j, 16 * i + loads_of(B_WA + j + 1))
                    if isinstance(i, int) and j == 0:
                        lru_split(7)
            wa_pair(0, T_WA)
            evict(T_LC, conv_out[:, :], wide[T_LC % 2][0:27, :], ACT.Copy)
            evict(T_LC + 1, h_out[:, :], wide[(T_LC + 1) % 2][0:72, 0:P], ACT.Copy)
            with act.Fori(1, 4) as i:
                wa_pair(i, T_WA + 2 + 2 * i)

            def project(n, t):
                b = B_HEAD + n
                hi(b + 1, (b + 1) % 2, D, t, loads_of(b + 1))
                h, part, j = n // 8, n % 8 // 2, n % 2
                s = h % 2
                if n >= 8 * HEADS:
                    jj = n - 8 * HEADS
                    if jj == 4:
                        act.wait_ge(head_done, HEADS - 1)
                    evict(t, h2(gbs[:, jj]), rt(t % 2), ACT.Sigmoid, bias=cols[:, C_BGB + jj:C_BGB + jj + 1])
                    return
                dst = (q[s], k[s], vf, so[s])[part]
                bias = cols[:, C_BIN + 8 * (part + 1) + 2 * h + j:][:, 0:1]
                if n % 8 == 6 and h >= 2:
                    act.wait_ge(head_done, h - 1)
                if part == 0:
                    evict(t, h2(dst[:, j]), rt(t % 2), ACT.Identity, scale=1.0 / 16, bias=qb[:, 2 * h + j:2 * h + j + 1])
                else:
                    evict(t, h2(dst[:, j]), rt(t % 2), ACT.Sigmoid if part == 3 else ACT.Identity, bias=bias)

            act.wait_ge(lru_out, 64)
            for n in range(8):
                project(n, T_HEAD0 + n)
                if n == 0:
                    act.wait_ge(gate_abs, 1)
                    act.activation(gs[:, 2, :], gs[:, 2, :], ACT.Exp, scale=-1.0).then_inc(gate_exp, 1)
            def prelude(h, t0):
                s = h % 2
                if h >= 2:
                    act.wait_ge(guard_used, h - 1)
                evict(t0, h2(ebcs[s][:, :]), rt(t0 % 2), ACT.Exp)
                evict(t0 + 1, h2(gbcs[s][:, :]), rt((t0 + 1) % 2), ACT.Exp, scale=-1.0)
                for m in range(3):
                    t = t0 + 2 + m
                    w2 = wide[t % 2].rearrange("p (c w d) -> p c w d", w=2, d=DH)
                    act.wait_ge(tile_done, t + 1)
                    if m < 2:
                        st(act.activation(kt[s][:, 2 * m:2 * m + 2], w2[:, :, 0], ACT.Copy))
                        act.wait_ge(tile_evicted, t)
                        act.activation(vt[s][:, 2 * m:2 * m + 2], w2[:, :, 1], ACT.Copy).then_inc(tile_evicted, 1)
                    else:
                        st(act.activation(kt[s][0:LAST, 4], w2[0:LAST, 0, 0], ACT.Copy))
                        act.wait_ge(tile_evicted, t)
                        act.activation(vt[s][0:LAST, 4], w2[0:LAST, 0, 1], ACT.Copy).then_inc(tile_evicted, 1)

            def squares(h):
                act.wait_ge(y_evicted, 5 * (h + 1))
                if h:
                    act.wait_ge(head_done, h)
                act.activation(hsq[:, :, :], hb[:, 2 * h:2 * h + 2, :], ACT.Square).then_inc(hsq_done, 1)

            def norm_root(h):
                act.wait_ge(var_done, h + 1)
                act.activation(hsq[:, 0], hsq[:, 0], ACT.Sqrt).then_inc(root_done, 1)

            prelude(0, T_PRE0)
            for h in range(HEADS):
                t0 = T_HEAD + HT * h
                for c in range(TT):
                    n, L = 5 * h + c, P if c < 4 else LAST
                    act.wait_ge(arg_done, n + 1)
                    if n >= 2:
                        act.wait_ge(y_done, n - 1)
                        act.wait_ge(kw_done, 13 * ((n - 2) // 5) + (13 if (n - 2) % 5 == 4 else (n - 2) % 5 + 1))
                    act.activation(wt[0:L, n % 2, 0:L], argm[0:L, 0:L], ACT.Exp).then_inc(w_done, 1)
                    project(8 * (h + 1) + c, t0 + c)
                project(8 * (h + 1) + 5, t0 + 5)
                project(8 * (h + 1) + 6, t0 + 6)
                if h + 1 < HEADS:
                    prelude(h + 1, t0 + 7)
                squares(h)
                project(8 * (h + 1) + 7, fill_tile(h, 7))
                if h + 1 < HEADS:
                    norm_root(h)

            for f in range(8):
                if f == 2:
                    norm_root(HEADS - 1)
                if f == 6:
                    act.wait_ge(head_done, HEADS)
                act.activation(xh[:, f], hb[:, f], ACT.Copy).then_inc(hb_hi, 1)
            evict(T_NOUT, n_rows[:, :], wide[T_NOUT % 2][0:72, 0:P], ACT.Copy)

            def wb_pair(i, residual):
                for j in range(2):
                    f = 2 * i + j
                    hi(B_WB + f + 1, (B_WB + j + 1) % 2, D, T_WB + f, 16 * i + loads_of(B_WB + j + 1))
                    act.wait_ge(m_done, f + 1)
                    past()
                    act.activation(flat(mh[:, ds(f, 1), :]), flat(merged[:, ds(f, 1), :]), ACT.Copy).then_inc(m_hi, 1)
                    for e in range(2 if residual else 0):
                        act.wait_ge(res_done, 2 * f - 8 + e + 1)
                        past()
                        act.activation(flat(resid[:, ds(2 * f - 8 + e, 1), :]),
                                       bank2(e)[:, 0:T], ACT.Copy
                                       ).then_inc(res_evicted, 1)
            with act.Fori(0, 2) as i:
                wb_pair(i, False)
            with act.Fori(2, 4) as i:
                wb_pair(i, True)

            act.wait_ge(m_lo, 8)

            def out_pair(i):
                for j in range(2):
                    b, t, f = B_OUT + 2 * i + j, T_OUT + 2 * i + j, 2 * i + j
                    hi(b + 1, (B_OUT + j + 1) % 2, D, t, 16 * i + loads_of(B_OUT + j + 1))
                    act.wait_ge(tile_evicted, t + 1)
                    past()
                    act.activation(flat(xh[:, ds(f, 1), :]), flat(resid[:, ds(f, 1), :]), ACT.Copy,
                                   scale=cols[:, ds(f + C_N2, 1)]).then_inc(x2_hi, 1)
                    act.activation(xsq[:, j], flat(resid[:, ds(f, 1), :]), ACT.Square).then_inc(xsq_done, 1)
            with act.Fori(0, 4) as i:
                out_pair(i)

            def rms_root():
                act.wait_ge(ssum_done, 1)
                act.activation(h2(rbc[:, :]), bank[:, 0:2, 0:HALF], ACT.Sqrt, scale=1.0 / D, bias=eps).then_inc(frms, 1)

            for h in range(2):
                b0, t0 = B_FFN + B_HALF * h, T_FFN + B_HALF * h

                def activate(i):
                    g = HK * h + i
                    act.wait_ge(gate_conv, g + 1)
                    act.activation(cv[:, 1], cv[:, 1], ACT.Gelu_apprx_tanh).then_inc(gelu_done, 1)
                    act.wait_ge(prod_done, g + 1)
                    if not isinstance(i, int):
                        past()
                    act.activation(flat(gh[:, ds(i, 1), :]), cv[:, 0], ACT.Copy).then_inc(g_hi, 1)

                def up_pair(i, first=False, last=False):
                    for j in range(2):
                        b, t = b0 + 2 * i + j, t0 + 2 * i + j
                        n = HK * P if last and j else D
                        hi(b + 1, (b0 + j + 1) % 2, n, t, 16 * i + loads_of(b0 + j + 1))
                        if j == 0 and not first:
                            activate(i - 1)
                        elif j == 0 and h == 0:
                            rms_root()
                up_pair(0, first=True)
                with act.Fori(1, HK - 1) as i:
                    up_pair(i)
                up_pair(HK - 1, last=True)
                b1, t1 = b0 + 2 * HK, t0 + 2 * HK
                hi(b1 + 1, (b1 + 1) % 2, HK * P, t1, loads_of(b1 + 1))
                activate(HK - 1)

                def down_hi(i, j):
                    hi(b1 + 2 * i + j + 2, (b1 + j) % 2, HK * P, t1 + 2 * i + j + 1, 16 * i + 16 + loads_of(b1 + j))
                if h == 0:
                    with act.Fori(0, 3) as i:
                        for j in range(2):
                            down_hi(i, j)
                    hi(b1 + 8, (b1 + 8) % 2, D, t1 + 7, loads_of(b1 + 8))
                else:
                    for m in range(FC):
                        down_hi(m // 2, m % 2)
                        w_ = min(D, 2 * FF - D * m)
                        if m >= 2:
                            act.wait_ge(f_out[m % 2], 32 * (m // 2))
                        act.wait_ge(fc_done, m + 1)
                        act.activation(fout[:, m % 2, 0:w_], bank2(m % 2)[0:18, 0:w_], ACT.Copy).then_inc(fc_evicted, 1)
            act.activation(misc[:, 205:206], eps, ACT.Sqrt)
            for i in range(TT):
                n, t = P if i < TT - 1 else LAST, T_FIN + i
                act.wait_ge(tile_done, t + 1)
                if i:
                    st.wait()
                st(act.activation(fsq[0:n, :], final[i % 4][0:n, :], ACT.Square,
                                  accum_out=ssf[0:n, i:i + 1]))
                st.wait()
                act.activation(rmsf[0:n, i:i + 1], ssf[0:n, i:i + 1], ACT.Sqrt, scale=1.0 / D, bias=eps[0:n]
                               ).then_inc(fin_rms, 1)

        @block.vector
        def _(dve):
            st = Chain(dve, dve_step)
            stt, ts, tt, cpy = dve.scalar_tensor_tensor, dve.tensor_scalar, dve.tensor_tensor, dve.tensor_copy

            def mul_add(out, in0, scalar, in1, op0=ALU.mult, op1=ALU.add):
                return stt(out=out, in0=in0, scalar=scalar, in1=in1, op0=op0, op1=op1)

            for i in range(TT):
                n = P if i < TT - 1 else LAST
                dve.wait_ge(rms_done, i + 1)
                st.link(dve.reciprocal(rms[0:n, i:i + 1], rms[0:n, i:i + 1]))
                ts(x_tok[0:n, i], x_tok[0:n, i], rms[0:n, i:i + 1], None, ALU.mult).then_inc(x_scaled, 1)
            dve.wait_ge(tile_evicted, T_XN)
            for f in range(8):
                dve.wait_ge(xn_hi, f + 1)
                mul_add(xl[:, f], wide[(T_XN + f) % 2][:, 0:T], cols[:, C_N1 + f:C_N1 + f + 1], xh[:, f].bitcast(F32),
                        ALU.mult, ALU.subtract).then_inc(tile_evicted, 1)
            st(ts(qb, cols[:, C_BIN + 8:C_BIN + 16], 1.0 / 16, None, ALU.mult))
            st(dve.memset(u[:, :, 0:LW - 1], 0.0))

            def log1p_exp(y, z, z2, p):
                st.link(ts(z, y, 2.0, None, ALU.add))
                st.link(dve.reciprocal(z2, z))
                st.link(tt(z, y, z2, ALU.mult))
                st.link(tt(z2, z, z, ALU.mult))
                st.link(ts(p, z2, 1.0 / (2 * LSE_TERMS + 1), None, ALU.mult))
                for m in range(LSE_TERMS - 1, 0, -1):
                    st.link(mul_add(p, p, 1.0 / (2 * m + 1), z2, ALU.add, ALU.mult))
                st.link(mul_add(p, p, 1.0, z, ALU.add, ALU.mult))
                st.link(ts(z, p, 2.0, None, ALU.mult))

            L_ = cols[:, C_LAM:C_LAM + 8]
            mul_add(lam[0], L_, -1.0, L_, ALU.mult, ALU.max).then_inc(lam_abs, 1)
            dve.wait_ge(lam_exp, 1)
            log1p_exp(*lam[0:4])
            st.link(ts(lam[4], L_, -1.0, 0.0, ALU.mult, ALU.max))
            st.link(tt(lam[4], lam[4], lam[1], ALU.add))
            ts(negc, lam[4], -LRU_C, None, ALU.mult).then_inc(negc_ready, 1)
            dve.wait_ge(tile_evicted, T_COLS2 + 2)
            st(cpy(nst[:, 1:NS, :], cols[:, C_NS:C_NS + 64].rearrange("p (b n) -> p b n", n=8)))

            for j in range(2):
                for g in range(2):
                    hist = cols[:, C_LC[g]:C_LC[g] + 96].rearrange("p (b l i j) -> p i b l j", l=LW - 1, i=4, j=2)
                    for b in range(4):
                        st(cpy(usamp[j][:, :, 4 * g + b, 0:LW - 1], hist[:, :, b, :, j]))

            def conv(i, j):
                f = 2 * i + j
                dve.wait_ge(tile_evicted, T_U + 1 + f)
                uf, cf = u[:, ds(f, 1), :], uc[:, ds(f, 1), :]
                w = [cols[:, ds(f + (C_CW + 8 * m), 1)] for m in range(LW)]
                us = usamp[j][:, ds(i, 1)].rearrange("p o b l -> p (o b) l")
                st(cpy(us[:, :, LW - 1:], flat(uf)[:, LW - 1 + TP:UW].rearrange("p (b l) -> p b l", l=LS)))
                st(cpy(flat(ulast[:, ds(f, 1), 0:3]), flat(uf)[:, TP:TP + 3]))
                cP = flat(cf)[:, 0:TP]
                cS = flat(cf)[:, TP:T].rearrange("p (b l) -> p b l", l=LS)
                st(ts(cP, flat(uf)[:, 0:TP], w[0], cols[:, ds(f + C_CB, 1)], ALU.mult, ALU.add))
                st.wait()
                st(ts(cS, us[:, :, 0:LS], w[0], cols[:, ds(f + C_CB, 1)], ALU.mult, ALU.add))
                for m in range(1, LW):
                    st(mul_add(cP, flat(uf)[:, m:m + TP], w[m], cP))
                    st.wait()
                    ins = mul_add(cS, us[:, :, m:m + LS], w[m], cS)
                    if m < LW - 1:
                        st(ins)
                    else:
                        ins.then_inc(conv_done, 1)

            sam = slice(TP, T)

            def first(ap):
                return ap[:, sam].rearrange("p (b l) -> p b l", l=LS)[:, :, 0]

            def lru_tile(p):
                return flat(u[:, ds(p, 1), 0:T]), flat(uc[:, ds(p, 1), :])

            def lru_square(p):
                a_, x = lru_tile(p)
                dve.wait_ge(lru_act, 2 * p + 1)
                st(tt(ri[:, 1], ri[:, 1], x, ALU.mult))
                dve.wait_ge(lru_act, 2 * p + 2)
                st(tt(ri[:, 0], a_, a_, ALU.mult))
                st.wait()
                mul_add(th[:, :], ri[:, 0], 1.0, th[:, :], ALU.add, ALU.mult).then_inc(lru_q, 1)

            def lru_scan(p):
                a_, x = lru_tile(p)
                r_, i_ = ri[:, 0], ri[:, 1]
                dve.wait_ge(lru_sq, p + 1)
                st(tt(i_, i_, th[:, :], ALU.mult))
                h0 = cols[:, C_H0:C_H0 + 64].rearrange("p (b f) -> p b f", f=8)[:, :, ds(p, 1)].rearrange(
                    "p b o -> p (b o)")
                st(tt(r_[:, 0:NB], first(a_), h0, ALU.mult))
                st.wait()
                st(tt(first(i_), first(i_), r_[:, 0:NB], ALU.add))
                st(ts(first(a_), first(a_), 0.0, None, ALU.mult))
                st.wait()
                dve.tensor_tensor_scan(out=x, data0=a_, data1=i_, initial=0.0, op0=ALU.mult, op1=ALU.add
                                       ).then_inc(lru_h, 1)
                dve.wait_ge(lru_h, p + 1)
                st(cpy(hlast[:, :, ds(p, 1)].rearrange("p b o -> p (b o)"), flat(uc[:, ds(p, 1), TP - 1:T])[:, 0:65:LS]))

            def lru_lo(p):
                dve.wait_ge(lru_hi, p + 1)
                tt(flat(hl[:, ds(p, 1), :]), flat(uc[:, ds(p, 1), :]), flat(hh[:, ds(p, 1), :]).bitcast(F32),
                   ALU.subtract).then_inc(lru_lo_, 1)

            def u_pair(i, first_=False):
                if not first_:
                    lru_scan(i - 1)
                conv(i, 0)
                if first_:
                    conv(i, 1)
                    lru_square(i)
                else:
                    lru_lo(i - 1)
                    lru_square(i)
                    conv(i, 1)

            def ga_pair(i):
                lru_scan(i + 3)
                lru_lo(i + 3)
                lru_square(i + 4)
            st.wait()
            u_pair(0, True)
            st.loop(1, 4, 2 * 9 + 2 + 5, u_pair)
            ul = ulast[:, :, 3:27].rearrange("p (i j) (b l) -> p i j b l", j=2, l=LW - 1)
            for j in range(2):
                for i in range(4):
                    st(cpy(ul[:, i, j], usamp[j][:, i, :, LS:]))
            st.loop(0, 4, 2 + 5, ga_pair)
            lru_scan(7)
            lru_lo(7)

            def wa_pair(i, t0):
                for j in range(2):
                    dve.wait_ge(tile_done, t0 + j + 1)
                    m_ = merged[:, ds(2 * i + j, 1), :]
                    tt(h2o(m_), rt((T_WA + j) % 2), h2o(m_), ALU.mult).then_inc(tile_evicted, 1)
            dve.wait_ge(tile_evicted, T_WA)
            wa_pair(0, T_WA)
            dve.wait_ge(tile_evicted, T_LC + 2)
            with dve.Fori(1, 4) as i:
                wa_pair(i, T_WA + 2 + 2 * i)

            ig, f_, yy, s3, s4, s5 = (gs[:, m, :] for m in range(6))
            st.link(ts(f_, f_, gbias[:, 1:2], None, ALU.add))
            mul_add(yy, f_, -1.0, f_, ALU.mult, ALU.max).then_inc(gate_abs, 1)
            dve.wait_ge(gate_exp, 1)
            log1p_exp(yy, s3, s4, s5)
            st.link(ts(yy, f_, 0.0, None, ALU.min))
            st.link(tt(f_, yy, s3, ALU.subtract))
            st.link(cpy(yy, f_))
            st.link(cpy(s3, ig))
            st.link(tt(first(s4), first(f_), mst, ALU.add))
            st.link(tt(first(s3), first(s4), first(ig), ALU.max))
            st.link(dve.memset(first(yy), NEG))
            M = s4
            st.link(dve.tensor_tensor_scan(out=M, data0=yy, data1=s3, initial=0.0, op0=ALU.add, op1=ALU.max))
            st.link(dve.memset(yy, 1.0))
            st.link(dve.memset(yy[:, 0:P * (TT - 1) + 1:P], 0.0))
            st.link(dve.memset(first(yy), 0.0))
            Bc = s3
            st.link(dve.tensor_tensor_scan(out=Bc, data0=yy, data1=f_, initial=0.0, op0=ALU.mult, op1=ALU.add))
            A = yy
            st.link(tt(A, Bc, M, ALU.subtract))
            st(cpy(gq[0:HEADS, :], A))
            st(tt(gq[32:32 + HEADS, :], ig, Bc, ALU.subtract))
            st(cpy(gq[96:96 + HEADS, :], M))
            st(cpy(gq[64:64 + HEADS, 0:P], A[:, 0:P]))
            for c in range(1, TT):
                e = P * c + (P if c < 4 else TAIL)
                st(ts(gq[64:64 + HEADS, P * c:e], A[:, P * c:e], M[:, P * c - 1:P * c], None, ALU.add))
            st(tt(gq[64:64 + HEADS, sam].rearrange("p (b l) -> p b l", l=LS),
                  A[:, sam].rearrange("p (b l) -> p b l", l=LS),
                  mst.rearrange("p (b o) -> p b o", o=1).to_broadcast([HEADS, NB, LS]), ALU.add))
            st(cpy(mout, M[:, TP - 1:T:LS]))
            st.wait()
            dve.memset(misc[:, 202:203], 0.0).then_inc(gates_ready, 1)

            def head_variance(h):
                t = norm_tile(h)
                dve.wait_ge(tile_done, t + 1)
                dve.wait_ge(tile_evicted, t)
                st.wait()
                mul_add(h2(hsq[:, 0]), rt(t % 2), 1.0 / DH, h2(den[:, :])).then_inc(tile_evicted, 1)
                dve.wait_ge(tile_evicted, t + 1)
                dve.memset(misc[:, 203:204], 0.0).then_inc(var_done, 1)

            def head_gain(h):
                dve.wait_ge(hsq_done, h + 1)
                for j in range(2):
                    gcol = cols[:, C_HG + 2 * h + j:C_HG + 2 * h + j + 1]
                    st(mul_add(hb[:, 2 * h + j], hb[:, 2 * h + j], gcol, so[h % 2][:, j], ALU.mult, ALU.mult))

            def head_norm(h):
                dve.wait_ge(root_done, h + 1)
                st.link(dve.reciprocal(hsq[:, 0], hsq[:, 0]))
                hv = hb[:, 2 * h:2 * h + 2, :]
                tt(hv, hv, hsq[:, 0:1, :].to_broadcast([P, 2, T]), ALU.mult).then_inc(head_done, 1)

            for h in range(HEADS):
                s = h % 2
                pre = prelude_tile(h)
                ebc, gbc = ebcs[s], gbcs[s]
                dve.wait_ge(tile_evicted, pre + 1)
                for j in range(2):
                    tt(qe[:, j], q[s][:, j], ebc[:, :], ALU.mult).then_inc(qe_done, 1)
                dve.wait_ge(qe_done, 3 * h + 2)
                tt(qn[:, :, :].rearrange("p i (b l) -> p i b l", l=LS),
                   qe[:, :, TP:T].rearrange("p i (b l) -> p i b l", l=LS),
                   nst[:, 1:NS, 2 * h:2 * h + 2].rearrange("p b (i o) -> p i b o", o=1).to_broadcast([P, 2, NB, LS]),
                   ALU.mult).then_inc(qe_done, 1)
                if h:
                    head_variance(h - 1)
                cpr = cp[s]
                if h >= 2:
                    dve.wait_ge(cp_out, 16 * (h - 1))
                for c in range(TT):
                    n, L, c0 = 5 * h + c, P if c < 4 else LAST, P * c
                    X = bx[n % 2]
                    w = wt[0:L, n % 2, 0:L]
                    dve.wait_ge(scores, n + 1)
                    if n:
                        dve.wait_ge(w_done, n)
                    tt(argm[0:L, 0:L], X[0:L, P:P + L], mask[0:L, c // 4, 0:L], ALU.add).then_inc(arg_done, 1)
                    dve.wait_ge(w_done, n + 1)
                    if n:
                        dve.wait_ge(y_done, n)
                    tt(pt[0:L, 0:L], w, X[0:L, 0:L], ALU.mult).then_inc(p_done, 1)
                    kap = 13 * h + c
                    nu = 1 if c < 4 else NS

                    def keys(m):
                        if kap + m >= 2:
                            dve.wait_ge(z_done, kap + m - 1)
                        col = L - 1 if c < 4 else TAIL - 1 + LS * m
                        ts(kw[(kap + m) % 2][0:L, :], kt[s][0:L, c], w[:, col:col + 1], None, ALU.mult
                           ).then_inc(kw_done, 1)

                    def update(m):
                        dve.wait_ge(z_done, kap + m + 1)
                        Z = bz if (m % 2 == 0) else bx[(n + 1) % 2]
                        if m == 0:
                            C = cpr[:, :, :].rearrange("p i v -> p (i v)")
                        else:
                            nb = NB * h + m - 1
                            C = cs[:, nb % 4].rearrange("p i v -> p (i v)")
                        if c == 0:
                            cpy(C, Z).then_inc(z_evicted, 1)
                            return
                        col = c0 + (L - 1 if c < 4 else TAIL - 1 + LS * m)
                        if kap + m:
                            dve.wait_ge(z_evicted, kap + m)
                        mul_add(C, C, ebc[:, col:col + 1], Z).then_inc(z_evicted, 1)

                    keys(0)
                    if h and c == 0:
                        head_gain(h - 1)
                        head_norm(h - 1)
                    if nu > 1:
                        keys(1)
                        for m in range(nu):
                            update(m)
                            if m + 2 < nu:
                                keys(m + 2)
                    dve.wait_ge(y_done, n + 1)
                    st(cpy(hb[:, 2 * h:2 * h + 2, c0:c0 + L],
                           by[:, 0:256].rearrange("p (j t) -> p j t", j=2)[:, :, 0:L]))
                    st(cpy(den[:, c0:c0 + L], by[:, 256:256 + L]))
                    npr = nst[:, 0, 2 * h:2 * h + 2]
                    if c == 0:
                        cpy(npr, by[:, 384:386]).then_inc(y_evicted, 1)
                    elif c < 4:
                        dve.wait_ge(y_evicted, n)
                        mul_add(npr, npr, ebc[:, c0 + L - 1:c0 + L], by[:, 384:386]).then_inc(y_evicted, 1)
                    else:
                        dec = ebc[:, TP - 1:T:LS].rearrange("p (b o) -> p b o", o=1)
                        nall = nst[:, :, 2 * h:2 * h + 2]
                        dve.wait_ge(y_evicted, n)
                        st.link(tt(ntmp[:, :, :], nall, dec.to_broadcast([P, NS, 2]), ALU.mult))
                        tt(nall, ntmp[:, :, :], by[:, 384:384 + 2 * NS].rearrange("p (i b) -> p b i", b=NS),
                           ALU.add).then_inc(y_evicted, 1)
                    if nu == 1:
                        update(0)
                dve.wait_ge(tile_evicted, pre + 2)
                st.wait()
                st.link(mul_add(qe[:, 0], den[:, :], -1.0, den[:, :], ALU.mult, ALU.max))
                st.link(mul_add(qe[:, 0], gbc[:, :], D_MAX, qe[:, 0], ALU.min, ALU.max))
                dve.wait_ge(hsq_done, h + 1)
                tt(hsq[:, 0], hsq[:, 0], hsq[:, 1], ALU.add).then_inc(hsum_done, 1)
                mul_add(den[:, :], qe[:, 0], EPS, qe[:, 0], ALU.mult, ALU.mult).then_inc(guard_used, 1)
                dve.wait_ge(guard_used, h + 1)

            dve.wait_ge(tile_evicted, fill_tile(HEADS - 2, 7) + 1)
            head_gain(HEADS - 1)
            head_variance(HEADS - 1)
            for f in range(8):
                if f == 2:
                    head_norm(HEADS - 1)
                    dve.wait_ge(head_done, HEADS)
                dve.wait_ge(hb_hi, f + 1)
                tt(xl[:, f], hb[:, f], xh[:, f].bitcast(F32), ALU.subtract).then_inc(hb_lo, 1)

            def wb_pair(i):
                for j in range(2):
                    f, t = 2 * i + j, T_WB + 2 * i + j
                    g_, m_ = gbs[:, ds(f, 1), :], merged[:, ds(f, 1), :]
                    dve.wait_ge(tile_done, t + 1)
                    dve.wait_ge(tile_evicted, t)
                    tt(h2o(g_), rt((T_WB + j) % 2), h2o(g_), ALU.mult).then_inc(tile_evicted, 1)
                    dve.wait_ge(tile_evicted, t + 1)
                    tt(flat(m_), flat(m_), flat(g_), ALU.add).then_inc(m_done, 1)
                    dve.wait_ge(m_hi, f + 1)
                    tt(flat(ml[:, ds(f, 1), :]), flat(m_), flat(mh[:, ds(f, 1), :]).bitcast(F32), ALU.subtract
                       ).then_inc(m_lo, 1)
            for n in range(4):
                dve.wait_ge(c_out[n], 16 * 8)
            with dve.Fori(0, 4) as i:
                wb_pair(i)

            dve.wait_ge(tile_evicted, T_OUT)
            dve.wait_ge(res_evicted, 8)

            def out_pair(i):
                for j in range(2):
                    f, t = 2 * i + j, T_OUT + 2 * i + j
                    r_ = resid[:, ds(f, 1), :]
                    dve.wait_ge(tile_done, t + 1)
                    tt(h2o(r_), rt((T_OUT + j) % 2), h2o(r_), ALU.add).then_inc(tile_evicted, 1)
                    dve.wait_ge(x2_hi, f + 1)
                    mul_add(flat(xl[:, ds(f, 1), :]), flat(r_), cols[:, ds(f + C_N2, 1)],
                            flat(xh[:, ds(f, 1), :]).bitcast(F32), ALU.mult, ALU.subtract).then_inc(x2_lo, 1)
                    dve.wait_ge(xsq_done, f + 1)
                    st.wait()
                    st(tt(rbc[:, :], rbc[:, :], xsq[:, j], ALU.add))
            st(dve.memset(rbc[:, :], 0.0))
            st.loop(0, 4, 2, out_pair)
            st.wait()
            dve.memset(misc[:, 204:205], 0.0).then_inc(sq_sum, 1)
            dve.wait_ge(frms, 1)
            dve.reciprocal(rbc[:, :], rbc[:, :]).then_inc(rbc_done, 1)
            st(dve.memset(up[:, :, 0:FW - 1], 0.0))
            dve.wait_ge(rbc_done, 1)
            st.wait()

            for h in range(2):
                t0 = T_FFN + B_HALF * h

                def gated(i):
                    g = HK * h + i
                    st.wait()
                    dve.wait_ge(gelu_done, g + 1)
                    tt(cv[:, 0], cv[:, 0], cv[:, 1], ALU.mult).then_inc(prod_done, 1)
                    dve.wait_ge(g_hi, g + 1)
                    tt(flat(gl[:, ds(i, 1), :]), cv[:, 0], flat(gh[:, ds(i, 1), :]).bitcast(F32), ALU.subtract
                       ).then_inc(g_lo, 1)

                def up_pair(i, first=False):
                    if not first:
                        gated(i - 1)
                    for j in range(2):
                        t = t0 + 2 * i + j
                        ft = i + (HK * h + UPT // 2 * j)
                        U = up[:, j]
                        dve.wait_ge(tile_done, t + 1)
                        tt(h2(U[:, FW - 1:FP]), rt((t0 + j) % 2), h2(rbc[:, :]), ALU.mult).then_inc(tile_evicted, 1)
                        hist = cols[:, C_FC:C_FC + P * NB].rearrange("p (b c) -> p b c", c=P)
                        fs = fsamp[:, j]
                        for m in range(2):
                            st(cpy(fs[:, :, m:m + 1], hist[:, :, ds(ft + UPT * m, 1)]))
                        dve.wait_ge(tile_evicted, t + 1)
                        usm = U[:, FW - 1 + TP:FP].rearrange("p (b l) -> p b l", l=LS)
                        st(cpy(fs[:, :, FW - 1:], usm))
                        fl = flat(flast[:, ds(ft, 1), :])
                        st(cpy(fl[:, 0:2], U[:, TP:TP + 2]))
                        st(cpy(fl[:, 2:18].rearrange("p (b l) -> p b l", l=2), usm[:, :, LS - 2:]))
                        w = [cols[:, ds(ft + C_FCW[m], 1)] for m in range(FW)]
                        bias = cols[:, ds(ft + C_FCB, 1)]
                        cP = cv[:, j, 0:TP]
                        cS = cv[:, j, TP:T].rearrange("p (b l) -> p b l", l=LS)
                        st(ts(cP, U[:, 0:TP], w[0], bias, ALU.mult, ALU.add))
                        st.wait()
                        st(ts(cS, fs[:, :, 0:LS], w[0], bias, ALU.mult, ALU.add))
                        for m in range(1, FW):
                            st(mul_add(cP, U[:, m:m + TP], w[m], cP))
                            st.wait()
                            ins = mul_add(cS, fs[:, :, m:m + LS], w[m], cS)
                            if m == FW - 1 and j:
                                ins.then_inc(gate_conv, 1)
                            else:
                                st(ins)

                if h:
                    dve.wait_ge(tile_done, t0)
                up_pair(0, True)
                st.loop(1, HK, 2 * (5 + 2 + 4) - 1, up_pair)
                gated(HK - 1)
                t1 = t0 + 2 * HK
                with dve.Fori(0, 4) as i:
                    for j in range(2):
                        t = t1 + 2 * i + j
                        r_ = resid[:, ds(2 * i + j, 1), :]
                        dve.wait_ge(tile_done, t + 1)
                        tt(h2o(r_), rt((t1 + j) % 2), h2o(r_), ALU.add).then_inc(tile_evicted, 1)
            dve.wait_ge(fg_in, 16)
            for i in range(TT):
                n, t = P if i < TT - 1 else LAST, T_FIN + i
                dve.wait_ge(fin_rms, i + 1)
                st.link(dve.reciprocal(rmsf[0:n, i:i + 1], rmsf[0:n, i:i + 1]))
                mul_add(y[0:n, i], final[i % 4][0:n, :], rmsf[0:n, i:i + 1], fgb[0:n, :], ALU.mult, ALU.mult
                        ).then_inc(tile_evicted, 1)

        @block.tensor
        def _(pe):
            def begin(t):
                if not isinstance(t, int) or t >= 2:
                    pe.wait_ge(tile_evicted, t - 1)

            def split_product(out, slot, kn, xh_, xl_, wait_k=None, ks=None):
                for kk in ks or range(kn):
                    if wait_k:
                        wait_k(kk)
                    for m, (w, x) in enumerate(((whi, xh_), (whi, xl_), (wlo, xh_))):
                        for hf in range(2):
                            last = pe.matmul(out(hf), w[:, slot, kk * P:kk * P + P], x[:, kk, HALF * hf:HALF * hf + HALF],
                                             start=kk == 0 and m == 0, stop=kk == kn - 1 and m == 2)
                return last

            def gemm(b, t, bslot, tslot, kn, xh_, xl_, wait_k=None):
                pe.wait_ge(w_lo, b + 1)
                begin(t)
                split_product(lambda hf: ring[:, tslot, hf, 0:HALF], bslot, kn, xh_, xl_, wait_k).then_inc(tile_done, 1)

            pe.wait_ge(const_done, 2)
            def row_transposes(t, m0, m1):
                begin(t)
                for m in range(m0, m1):
                    last = pe.transpose(wide[t % 2][:, P * (m - m0):P * (m - m0) + ROWS[m]],
                                        rows[0:ROWS[m], m, :], ident[0:ROWS[m], 0:ROWS[m]])
                last.then_inc(tile_done, 1)
            pe.wait_ge(rows_in[0], 16 * 11)
            row_transposes(T_COLS, *COL_GROUPS[0])
            pe.wait_ge(x_scaled, TT)

            def token_transposes(dst, f, src):
                for i in range(TT):
                    n = P if i < TT - 1 else LAST
                    last = pe.transpose(dst[:, P * i:P * i + n], src[0:n, i, P * f:P * f + P], ident[0:n, 0:n])
                return last

            def gate_step(kk):
                pe.wait_ge(tile_evicted, T_XN + kk + 1)
                return split_product(lambda hf: bank[:, hf, 0:HALF], 0, KT, xh, xl, ks=[kk])
            for f in range(8):
                begin(T_XN + f)
                token_transposes(wide[(T_XN + f) % 2], f, x_tok).then_inc(tile_done, 1)
                if f == 2:
                    pe.wait_ge(w_lo, 1)
                if f >= 2:
                    gate_step(f - 2)
            gate_step(6)
            gate_step(7).then_inc(tile_done, 1)
            pe.wait_ge(rows_in[1], 16 * 7)
            for n in range(2):
                row_transposes(T_COLS2 + n, *COL_GROUPS[1 + n])

            def lru_gates(p):
                pe.wait_ge(conv_done, p + 1)
                pe.wait_ge(bd_in, 64 * (p + 1))
                if not isinstance(p, int):
                    pe.wait_ge(lru_act, 2 * p)
                for g in range(2):
                    for hf in range(2):
                        last = pe.matmul(bank[:, 2 * g + hf, 0:HALF], bd[:, g, :],
                                         flat(uc[:, ds(p, 1), HALF * hf:HALF * hf + HALF]), start=True, stop=True)
                last.then_inc(lru_ps, 1)

            def with_lru(b0, t0, i, p, late=False):
                for j in range(2):
                    if j == 1 and not late:
                        lru_gates(p)
                    gemm(b0 + 2 * i + j, t0 + 2 * i + j, (b0 + j) % 2, (t0 + j) % 2, KT, xh, xl)
                if late:
                    lru_gates(p)
            pe.wait_ge(tile_evicted, T_GATE + 1)
            with_lru(B_U, T_U, 0, 0, late=True)
            with pe.Fori(1, 4) as i:
                with_lru(B_U, T_U, i, i)
            with pe.Fori(0, 4) as i:
                with_lru(B_GA, T_GA, i, i + 4)

            def wa_pair(i, t0, arrived=None):
                for j in range(2):
                    gemm(B_WA + 2 * i + j, t0 + j, (B_WA + j) % 2, (T_WA + j) % 2, KT, hh, hl, None if j else arrived)
            wa_pair(0, T_WA, lambda kk: pe.wait_ge(lru_lo_, kk + 1))
            t = T_LC
            begin(t)
            for f in range(8):
                last = pe.transpose(wide[t % 2][0:27, P * f:P * f + P], ulast[:, f, :], ident[:, :])
            last.then_inc(tile_done, 1)
            begin(t + 1)
            pe.transpose(wide[(t + 1) % 2][0:72, 0:P], stage[:, 0, D + 224:D + 224 + 72], ident[:, :]).then_inc(tile_done, 1)
            with pe.Fori(1, 4) as i:
                wa_pair(i, T_WA + 2 + 2 * i)
            for n in range(8):
                gemm(B_HEAD + n, T_HEAD0 + n, (B_HEAD + n) % 2, (T_HEAD0 + n) % 2, KT, xh, xl)

            def fill(h, n, ks=range(KT)):
                b, t = B_HEAD + 8 * (h + 1) + n, fill_tile(h, n)
                if ks[0] == 0:
                    pe.wait_ge(w_lo, b + 1)
                    begin(t)
                last = split_product(lambda hf: ring[:, t % 2, hf, 0:HALF], b % 2, KT, xh, xl, ks=ks)
                if ks[-1] == KT - 1:
                    last.then_inc(tile_done, 1)

            def prelude(h, t0):
                s = h % 2
                for m, r0 in enumerate((64, 96)):
                    begin(t0 + m)
                    for hf in range(2):
                        last = pe.matmul(ring[:, (t0 + m) % 2, hf, 0:HALF], sel[r0:r0 + HEADS, h, :],
                                         gq[r0:r0 + HEADS, HALF * hf:HALF * hf + HALF], start=True, stop=True)
                    last.then_inc(tile_done, 1)
                for m in range(3):
                    t = t0 + 2 + m
                    begin(t)
                    for cc in range(2 if m < 2 else 1):
                        c = 2 * m + cc
                        L = P if c < 4 else LAST
                        for w_, src in enumerate((k[s], vf)):
                            for jj in range(2):
                                last = pe.transpose(wide[t % 2][0:L, 512 * cc + 256 * w_ + 128 * jj:][:, 0:P],
                                                    src[:, jj, P * c:P * c + L], ident[:, :])
                    last.then_inc(tile_done, 1)

            pe.wait_ge(gates_ready, 1)
            prelude(0, T_PRE0)
            for h in range(HEADS):
                s, t0 = h % 2, T_HEAD + HT * h

                def mix(m):
                    fill(h, 5 + m // 4, range(2 * m % KT, 2 * m % KT + 2))

                def score(c):
                    n, L, c0 = 5 * h + c, P if c < 4 else LAST, P * c
                    X = bx[n % 2]
                    if n >= 2:
                        pe.wait_ge(p_done, n - 1)
                    if h:
                        pe.wait_ge(z_evicted, 13 * h)
                    for jj in range(2):
                        pe.matmul(X[0:L, 0:L], k[s][:, jj, c0:c0 + L], q[s][:, jj, c0:c0 + L], start=jj == 0, stop=jj == 1)
                    pe.matmul(X[0:L, P:P + L], sel[0:HEADS, h, 0:L], gq[0:HEADS, c0:c0 + L], start=True, stop=False
                              ).then_inc(arg_part, 1)
                    pe.wait_ge(arg_part, n + 1)
                    pe.matmul(X[0:L, P:P + L], gq[32:32 + HEADS, c0:c0 + L], sel[32:32 + HEADS, h, 0:L],
                              start=False, stop=True).then_inc(scores, 1)

                def values(c):
                    n, L, c0 = 5 * h + c, P if c < 4 else LAST, P * c
                    kap = 13 * h + c
                    cpr = cp[s]
                    w = wt[0:L, n % 2]
                    pe.wait_ge(p_done, n + 1)
                    if n:
                        pe.wait_ge(y_evicted, n)
                    inter = c > 0
                    for jj in range(2):
                        pe.matmul(by[:, P * jj:P * jj + L], vt[s][0:L, c, P * jj:P * jj + P], pt[0:L, 0:L],
                                  start=jj == 0, stop=not inter, skip_group_check=True)
                    pe.matmul(by[:, 256:256 + L], ones[0:L, :], pt[0:L, 0:L], start=False, stop=not inter,
                              skip_group_check=True)
                    nu = 1 if c < 4 else NS
                    first_ = L - 1 if c < 4 else TAIL - 1
                    for jj in range(2):
                        last = pe.matmul(by[:, 384 + nu * jj:384 + nu * jj + nu], kt[s][0:L, c, P * jj:P * jj + P],
                                         w[:, first_:first_ + LS * (nu - 1) + 1:LS], start=False, stop=True,
                                         skip_group_check=True)

                    def across(cols_, C, ncol=None):
                        for jj in range(2):
                            for ii in range(2):
                                last = pe.matmul(by[:, P * jj + cols_.start:P * jj + cols_.stop], C[:, ii, P * jj:P * jj + P],
                                                 qe[:, ii, c0 + cols_.start:c0 + cols_.stop], start=False, stop=ii == 1,
                                                 skip_group_check=True)
                        for ii in range(2 if ncol is not None else 0):
                            last = pe.matmul(by[:, 256 + cols_.start:256 + cols_.stop],
                                             ncol[:, ii:ii + 1].to_broadcast([P, P]),
                                             qe[:, ii, c0 + cols_.start:c0 + cols_.stop], start=False, stop=ii == 1,
                                             skip_group_check=True)
                        return last

                    def outer(m):
                        Z = bz if m % 2 == 0 else bx[(n + 1) % 2]
                        pe.wait_ge(kw_done, kap + m + 1)
                        if kap + m >= (2 if c == 4 else 1):
                            pe.wait_ge(z_evicted, kap + m - (1 if c == 4 and m > 1 else 0))
                        for ii in range(2):
                            lz = pe.matmul(Z[:, 256 * ii:256 * ii + 256], kw[(kap + m) % 2][0:L, P * ii:P * ii + P],
                                           vt[s][0:L, c, :], start=True, stop=True)
                        lz.then_inc(z_done, 1)

                    if inter:
                        pe.wait_ge(qe_done, 3 * h + 3)
                        pe.wait_ge(z_evicted, kap)
                        last = across(slice(0, L if c < 4 else TAIL), cpr, nst[:, 0, 2 * h:2 * h + 2])
                    if c < 4:
                        last.then_inc(y_done, 1)
                        outer(0)
                        return
                    for ii in range(2):
                        pe.matmul(by[:, 256 + TAIL:256 + L], ones[:, :], qn[:, ii, :], start=False, stop=ii == 1,
                                  skip_group_check=True)
                    mix(0)
                    outer(0)
                    for b in range(NB):
                        nb = NB * h + b
                        pe.wait_ge(c_in[nb % 4], 16 * (nb // 4 + 1))
                        last = across(slice(TAIL + LS * b, TAIL + LS * b + LS), cs[:, nb % 4])
                        if b == NB - 1:
                            last.then_inc(y_done, 1)
                        if b < NB - 1:
                            mix(b + 1)
                        outer(1 + b)

                score(0)
                fill(h, 0)
                for c in range(TT):
                    values(c)
                    if c < 4:
                        score(c + 1)
                        fill(h, c + 1)

                def norm_sums():
                    t = norm_tile(h)
                    pe.wait_ge(hsum_done, h + 1)
                    begin(t)
                    for hf in range(2):
                        last = pe.matmul(ring[:, t % 2, hf, 0:HALF], ones[:, :], hsq[:, 0, HALF * hf:HALF * hf + HALF],
                                         start=True, stop=True)
                    last.then_inc(tile_done, 1)
                if h + 1 < HEADS:
                    prelude(h + 1, t0 + 7)
                fill(h, 7)
                norm_sums()
            t = T_NOUT
            pe.wait_ge(y_evicted, 5 * HEADS)
            begin(t)
            pe.transpose(wide[t % 2][0:72, 0:P], nst[:, :, :].rearrange("p b n -> p (b n)"), ident[:, :]
                         ).then_inc(tile_done, 1)
            for f in range(8):
                t = T_WB + f
                gemm(B_WB + f, t, (B_WB + f) % 2, t % 2, KT, xh, xl,
                     (lambda kk: pe.wait_ge(hb_lo, kk + 1)) if f == 0 else None)
                if f == 4:
                    pe.wait_ge(x2_in, 16 * 7)
                for e in range(2 if f >= 4 else 0):
                    n = 2 * f - 8 + e
                    if n >= 2:
                        pe.wait_ge(res_evicted, n - 1)
                    token_transposes(bank2(e), n, x_tok2).then_inc(res_done, 1)

            for f in range(8):
                gemm(B_OUT + f, T_OUT + f, (B_OUT + f) % 2, (T_OUT + f) % 2, KT, mh, ml,
                     None if f else lambda kk: pe.wait_ge(m_lo, kk + 1))

            def x2_arrived(kk):
                pe.wait_ge(x2_lo, kk + 1)
                if kk == 6:
                    pe.wait_ge(res_evicted, 8)
                    pe.wait_ge(sq_sum, 1)
                    for hf in range(2):
                        last = pe.matmul(bank[:, hf, 0:HALF], ones[:, :], rbc[:, HALF * hf:HALF * hf + HALF],
                                         start=True, stop=True)
                    last.then_inc(ssum_done, 1)
            for h in range(2):
                b0, t0 = B_FFN + B_HALF * h, T_FFN + B_HALF * h
                if h == 0:
                    for j in range(2):
                        gemm(b0 + j, t0 + j, (b0 + j) % 2, (t0 + j) % 2, KT, xh, xl, None if j else x2_arrived)
                with pe.Fori(1 - h, HK) as i:
                    for j in range(2):
                        gemm(b0 + 2 * i + j, t0 + 2 * i + j, (b0 + j) % 2, (t0 + j) % 2, KT, xh, xl)
                b1, t1 = b0 + 2 * HK, t0 + 2 * HK

                def arrived(kk):
                    pe.wait_ge(g_lo, HK * h + kk + 1)
                for m in range(8):
                    gemm(b1 + m, t1 + m, (b1 + m) % 2, (t1 + m) % 2, HK, gh, gl, arrived if m == 0 else None)
                    if h and 1 <= m <= FC:
                        n = m - 1
                        if n >= 2:
                            pe.wait_ge(fc_evicted, n - 1)
                        for ft in range(8 * n, min(8 * n + 8, UPT)):
                            last = pe.transpose(bank2(n % 2)[0:18, P * (ft - 8 * n):P * (ft - 8 * n) + P],
                                                flast[:, ft, :], ident[:, :])
                        last.then_inc(fc_done, 1)
            pe.wait_ge(tile_evicted, T_FIN)
            for i in range(TT):
                n, t = P if i < TT - 1 else LAST, T_FIN + i
                if i >= 4:
                    pe.wait_ge(tile_evicted, t - 3)
                elif i == 2:
                    pe.wait_ge(fc_evicted, FC)
                for f in range(8):
                    last = pe.transpose(final[i % 4][0:n, P * f:P * f + P], resid[:, f, P * i:P * i + n], ident[:, :])
                last.then_inc(tile_done, 1)


_INS = ["x_prompt", "x_sample", "state_lru_conv", "state_lru_h", "state_mlstm_C", "state_mlstm_n",
        "state_mlstm_m", "state_ffn_conv", "meta_tokens", "norm1_g", "w_in", "b_in", "lru_conv_w", "lru_conv_b",
        "lru_w_r", "lru_b_r", "lru_w_i", "lru_b_i", "lru_lambda", "mlstm_head_g", "w_branch_a", "w_branch_b",
        "w_out", "norm2_g", "w_up", "ffn_conv_w", "ffn_conv_b", "w_down", "final_g"]
_OUTS = [("y_prompt", (1, SEQ, D)), ("y_sample", (NB, LS, D)),
         ("p_lru_conv", (1, 1, 3, D)), ("p_lru_h", (1, 1, D)), ("p_mlstm_C", (1, 1, HEADS, DH, DH)),
         ("p_mlstm_n", (1, 1, HEADS, DH)), ("p_mlstm_m", (1, 1, HEADS)), ("p_ffn_conv", (1, 1, 2, 2 * FF)),
         ("s_lru_conv", (1, NB, 3, D)), ("s_lru_h", (1, NB, D)), ("s_mlstm_C", (1, NB, HEADS, DH, DH)),
         ("s_mlstm_n", (1, NB, HEADS, DH)), ("s_mlstm_m", (1, NB, HEADS)), ("s_ffn_conv", (1, NB, 2, 2 * FF))]


def kernel(**inputs):
    import concourse.bacc as bacc
    from concourse.bass_utils import run_bass_kernel_spmd

    nc = bacc.Bacc("TRN2", target_bir_lowering=False, num_devices=1)
    arrays, a, o = {}, {}, {}
    for name in _INS:
        x = np.ascontiguousarray(inputs[name])
        arrays[f"in_{name}"] = x
        a[name] = nc.dram_tensor(f"in_{name}", x.shape, mybir.dt.from_np(x.dtype), kind="ExternalInput").ap()
    for name, shape in _OUTS:
        o[name] = nc.dram_tensor(f"out_{name}", shape, F32, kind="ExternalOutput").ap()
    hybrid_layer(nc, a, o)
    r = run_bass_kernel_spmd(nc, [arrays], core_ids=[0])
    return tuple(r.results[0][f"out_{name}"] for name, _ in _OUTS)
```
